# Optimizing a Trainium2 kernel written in Bass

```python
import jax, jax.numpy as jnp
from jax import lax
import numpy as np
import math

D_MODEL = 1024
BATCH = 1
SEQ = 512
DEPTH = 1

HEAD_DIM = 64
HEADS_PER_GROUP = 4
DILATED_GROUPS = ((128, 1), (512, 4), (2048, 16))
N_GROUPS = len(DILATED_GROUPS)
N_ATTN_HEADS = N_GROUPS * HEADS_PER_GROUP
ATTN_WIDTH = N_ATTN_HEADS * HEAD_DIM
ATTN_OUT_WIDTH = HEADS_PER_GROUP * HEAD_DIM
ROT_DIM = HEAD_DIM // 4
ROPE_THETA = 500000.0
BLOCK = 128
POOL_WINDOWS = (2, 4, 8, 16)
POOL_GROUP_WIDTH = 128
POOL_WIDTH = len(POOL_WINDOWS) * POOL_GROUP_WIDTH
N_BRANCHES = 2
IN_WIDTH = 3 * ATTN_WIDTH + POOL_WIDTH + N_BRANCHES * D_MODEL
D_FF = 2816
RMS_EPS = 1e-6


def rms_norm(x, g):
    xf = x.astype(jnp.float32)
    y = xf * lax.rsqrt(jnp.mean(xf * xf, axis=-1, keepdims=True) + RMS_EPS)
    return (y * g.astype(jnp.float32)).astype(x.dtype)

def swiglu(x, w1, w3, w2):
    return (jax.nn.silu(x @ w1) * (x @ w3)) @ w2

def rope_tables(seq):
    pos = jnp.arange(seq, dtype=jnp.float32)
    inv = ROPE_THETA ** (-jnp.arange(0, ROT_DIM, 2, dtype=jnp.float32) / ROT_DIM)
    ang = pos[:, None] * inv[None, :]
    return jnp.cos(ang), jnp.sin(ang)

def apply_partial_rope(x, cos, sin):
    xf = x.astype(jnp.float32)
    half = ROT_DIM // 2
    x1, x2 = xf[..., :half], xf[..., half:ROT_DIM]
    c, s = cos[None, :, None, :], sin[None, :, None, :]
    out = jnp.concatenate([x1 * c - x2 * s, x2 * c + x1 * s, xf[..., ROT_DIM:]], axis=-1)
    return out.astype(x.dtype)

def dilated_window_attention(q, k, v, window, dilation):
    B, S, H, Dh = q.shape
    r = dilation
    L = S // r
    n_back = window // r
    nb = -(-L // BLOCK)
    Lp = nb * BLOCK

    def to_blocks(t):
        t = t.reshape(B, L, r, H, Dh).transpose(0, 2, 1, 3, 4)
        t = jnp.pad(t, ((0, 0), (0, 0), (0, Lp - L), (0, 0), (0, 0)))
        return t.reshape(B, r, nb, BLOCK, H, Dh)

    def band(t):
        prev = jnp.pad(t[:, :, :-1], ((0, 0), (0, 0), (1, 0), (0, 0), (0, 0), (0, 0)))
        return jnp.concatenate([prev, t], axis=3)

    qb = to_blocks(q)
    kk = band(to_blocks(k))
    vv = band(to_blocks(v))
    s = jnp.einsum('brnqhd,brnkhd->brnhqk', qb, kk).astype(jnp.float32) * (Dh ** -0.5)
    qi = jnp.arange(BLOCK)[:, None]
    kj = jnp.arange(2 * BLOCK)[None, :]
    dist = qi + BLOCK - kj
    key_pos = (jnp.arange(nb)[:, None, None] - 1) * BLOCK + kj[None]
    allowed = (dist >= 0)[None] & (dist <= n_back)[None] & (key_pos >= 0)
    s = jnp.where(allowed[None, None, :, None], s, -jnp.inf)
    m = jnp.max(s, axis=-1, keepdims=True)
    p = jnp.exp(s - m)
    l = jnp.sum(p, axis=-1, keepdims=True)
    o = jnp.einsum('brnhqk,brnkhd->brnqhd', p, vv.astype(jnp.float32)) / jnp.swapaxes(l, 3, 4)
    lse = (m + jnp.log(l))[..., 0]
    o = o.reshape(B, r, Lp, H, Dh)[:, :, :L].transpose(0, 2, 1, 3, 4).reshape(B, S, H, Dh)
    lse = lse.transpose(0, 1, 2, 4, 3).reshape(B, r, Lp, H)[:, :, :L].transpose(0, 2, 1, 3).reshape(B, S, H)
    return o, lse

def dilated_mixture_attention(q, k, v):
    B, S = q.shape[:2]
    cos, sin = rope_tables(S)
    q = apply_partial_rope(q, cos, sin)
    k = apply_partial_rope(k, cos, sin)
    outs, lses = [], []
    for g, (window, dilation) in enumerate(DILATED_GROUPS):
        hs = slice(g * HEADS_PER_GROUP, (g + 1) * HEADS_PER_GROUP)
        o, lse = dilated_window_attention(q[:, :, hs], k[:, :, hs], v[:, :, hs], window, dilation)
        outs.append(o)
        lses.append(lse)
    alpha = jax.nn.softmax(jnp.stack(lses, axis=0), axis=0)
    o = jnp.sum(alpha[..., None] * jnp.stack(outs, axis=0), axis=0)
    return o.reshape(B, S, ATTN_OUT_WIDTH).astype(v.dtype)

def multiscale_pool(p, w_pool, pool_scale):
    B, S, C = p.shape
    pf = p.astype(jnp.float32)
    cs0 = jnp.concatenate([jnp.zeros((B, 1, C), jnp.float32), jnp.cumsum(pf, axis=1)], axis=1)
    outs = []
    for gi, win in enumerate(POOL_WINDOWS):
        cs = slice(gi * POOL_GROUP_WIDTH, (gi + 1) * POOL_GROUP_WIDTH)
        c = cs0[..., cs]
        lagged = jnp.pad(c[:, :S - win + 1], ((0, 0), (win - 1, 0), (0, 0)))
        cnt = jnp.minimum(jnp.arange(1, S + 1), win).astype(jnp.float32)[None, :, None]
        outs.append((c[:, 1:] - lagged) / cnt - pf[..., cs])
    d = jnp.stack(outs, axis=2).astype(p.dtype)
    y = jnp.einsum('bsgc,gcd->bsgd', d, w_pool).reshape(B, S, C)
    return y * pool_scale

def first_inputs(seed: int = 0) -> dict:
    key = jax.random.key(seed)
    ks = jax.random.split(key, 20)
    f32 = jnp.float32

    def nrm(k, shape, fan_in):
        return jax.random.normal(k, shape, f32) * (fan_in ** -0.5)

    def gain(k, shape):
        return 1.0 + 0.02 * jax.random.normal(k, shape, f32)

    L = DEPTH
    return {
        "x": jax.random.normal(ks[0], (BATCH, SEQ, D_MODEL), f32),
        "ffn1_norm": gain(ks[1], (L, D_MODEL)),
        "ffn1_w1": nrm(ks[2], (L, D_MODEL, D_FF), D_MODEL),
        "ffn1_w3": nrm(ks[3], (L, D_MODEL, D_FF), D_MODEL),
        "ffn1_w2": nrm(ks[4], (L, D_FF, D_MODEL), D_FF),
        "mix_norm": gain(ks[5], (L, D_MODEL)),
        "w_in": nrm(ks[6], (L, D_MODEL, IN_WIDTH), D_MODEL),
        "w_branch_attn": nrm(ks[7], (L, ATTN_OUT_WIDTH, D_MODEL), ATTN_OUT_WIDTH),
        "w_branch_pool": nrm(ks[8], (L, POOL_WIDTH, D_MODEL), POOL_WIDTH),
        "pool_w": nrm(ks[9], (L, len(POOL_WINDOWS), POOL_GROUP_WIDTH, POOL_GROUP_WIDTH), POOL_GROUP_WIDTH),
        "pool_scale": gain(ks[10], (L, POOL_WIDTH)),
        "w_out": nrm(ks[11], (L, D_MODEL, D_MODEL), D_MODEL),
        "ffn2_norm": gain(ks[12], (L, D_MODEL)),
        "ffn2_w1": nrm(ks[13], (L, D_MODEL, D_FF), D_MODEL),
        "ffn2_w3": nrm(ks[14], (L, D_MODEL, D_FF), D_MODEL),
        "ffn2_w2": nrm(ks[15], (L, D_FF, D_MODEL), D_FF),
        "final_norm": gain(ks[16], (D_MODEL,)),
    }

def first_block(x, ffn1_norm, ffn1_w1, ffn1_w3, ffn1_w2, mix_norm, w_in, w_branch_attn, w_branch_pool,
              pool_w, pool_scale, w_out, ffn2_norm, ffn2_w1, ffn2_w3, ffn2_w2, final_norm):
    B, S, D = x.shape
    h = x
    for l in range(DEPTH):
        h = h + 0.5 * swiglu(rms_norm(h, ffn1_norm[l]), ffn1_w1[l], ffn1_w3[l], ffn1_w2[l])
        u = rms_norm(h, mix_norm[l])
        proj = u @ w_in[l]
        o = 0
        q = proj[..., o:o + ATTN_WIDTH].reshape(B, S, N_ATTN_HEADS, HEAD_DIM); o += ATTN_WIDTH
        k = proj[..., o:o + ATTN_WIDTH].reshape(B, S, N_ATTN_HEADS, HEAD_DIM); o += ATTN_WIDTH
        v = proj[..., o:o + ATTN_WIDTH].reshape(B, S, N_ATTN_HEADS, HEAD_DIM); o += ATTN_WIDTH
        pz = proj[..., o:o + POOL_WIDTH]; o += POOL_WIDTH
        gates = jax.nn.sigmoid(proj[..., o:o + N_BRANCHES * D_MODEL].reshape(B, S, N_BRANCHES, D_MODEL))
        y_attn = dilated_mixture_attention(q, k, v) @ w_branch_attn[l]
        y_pool = multiscale_pool(pz, pool_w[l], pool_scale[l]) @ w_branch_pool[l]
        merged = gates[:, :, 0] * y_attn + gates[:, :, 1] * y_pool
        h = h + merged @ w_out[l]
        h = h + 0.5 * swiglu(rms_norm(h, ffn2_norm[l]), ffn2_w1[l], ffn2_w3[l], ffn2_w2[l])
    return rms_norm(h, final_norm)


DEPTH_2 = 2

CHUNK = 64
N_MIXERS = 2
N_HEADS = 16
HEAD_DIM_2 = D_MODEL // N_HEADS
IDX_HEADS = 8
IDX_DIM = 64
TOPK_MAX = 256
Q_BLOCK = 128
ROPE_THETA_2 = 10000.0
SSM_GROUP = 16
N_GROUPS_2 = D_MODEL // SSM_GROUP
SSM_STATE = 64
CONV_W = 3
EPS = 1e-6
NEG = -1e30
N_ATTN = (DEPTH_2 + 1) // 2
N_SSM = DEPTH_2 // 2
IN_COLS = 3 * D_MODEL + IDX_HEADS * IDX_DIM + IDX_DIM + IDX_HEADS


def rms_norm_2(x, g):
    xf = x.astype(jnp.float32)
    y = xf * lax.rsqrt(jnp.mean(xf * xf, axis=-1, keepdims=True) + EPS)
    return (y * g.astype(jnp.float32)).astype(x.dtype)

def rope(x, positions):
    half = x.shape[-1] // 2
    inv = ROPE_THETA_2 ** (-jnp.arange(half, dtype=jnp.float32) / half)
    ang = positions.astype(jnp.float32)[..., None] * inv
    cos = jnp.cos(ang)[:, :, None, :]
    sin = jnp.sin(ang)[:, :, None, :]
    xf = x.astype(jnp.float32)
    x1, x2 = xf[..., :half], xf[..., half:]
    return jnp.concatenate([x1 * cos - x2 * sin, x2 * cos + x1 * sin], axis=-1).astype(x.dtype)

def dsa_attention(h, positions, w_in, q_gain, k_gain, w_out):
    B, L, D = h.shape
    proj = h @ w_in
    s1 = D
    s2 = 2 * D
    s3 = 3 * D
    s4 = s3 + IDX_HEADS * IDX_DIM
    s5 = s4 + IDX_DIM
    q = proj[..., :s1].reshape(B, L, N_HEADS, HEAD_DIM_2)
    k = proj[..., s1:s2].reshape(B, L, N_HEADS, HEAD_DIM_2)
    v = proj[..., s2:s3].reshape(B, L, N_HEADS, HEAD_DIM_2)
    qi = proj[..., s3:s4].reshape(B, L, IDX_HEADS, IDX_DIM)
    ki = proj[..., s4:s5].reshape(B, L, 1, IDX_DIM)
    wi = proj[..., s5:].astype(jnp.float32) * IDX_HEADS ** -0.5
    q = rope(rms_norm_2(q, q_gain), positions)
    k = rope(rms_norm_2(k, k_gain), positions)
    qi = rope(qi, positions).astype(jnp.float32)
    ki = rope(ki, positions)[:, :, 0, :].astype(jnp.float32)
    topk = min(TOPK_MAX, L // 4)
    key_chunk = jnp.arange(L) // CHUNK
    n_blk = L // Q_BLOCK

    def block(i):
        start = i * Q_BLOCK
        qb = lax.dynamic_slice_in_dim(q, start, Q_BLOCK, axis=1)
        qib = lax.dynamic_slice_in_dim(qi, start, Q_BLOCK, axis=1)
        wib = lax.dynamic_slice_in_dim(wi, start, Q_BLOCK, axis=1)
        q_chunk = (start + jnp.arange(Q_BLOCK)) // CHUNK
        logits = jnp.einsum('bqhd,bsd->bqhs', qib, ki) * IDX_DIM ** -0.5
        score = jnp.einsum('bqh,bqhs->bqs', wib, jax.nn.relu(logits))
        admissible = key_chunk[None, :] <= q_chunk[:, None]
        score = jnp.where(admissible[None], score, NEG)
        _, idx = lax.top_k(score, topk)
        valid = (idx // CHUNK) <= q_chunk[None, :, None]
        kg = jax.vmap(lambda kb, ib: kb[ib])(k, idx)
        vg = jax.vmap(lambda vb, ib: vb[ib])(v, idx)
        s = jnp.einsum('bqhd,bqkhd->bqhk', qb.astype(jnp.float32), kg.astype(jnp.float32)) * HEAD_DIM_2 ** -0.5
        s = jnp.where(valid[:, :, None, :], s, NEG)
        p = jax.nn.softmax(s, axis=-1)
        o = jnp.einsum('bqhk,bqkhd->bqhd', p.astype(v.dtype), vg)
        return o.reshape(B, Q_BLOCK, D)

    out = lax.map(block, jnp.arange(n_blk))
    out = out.transpose(1, 0, 2, 3).reshape(B, L, D)
    return out @ w_out

def _complex_scan_op(e1, e2):
    a1r, a1i, b1r, b1i = e1
    a2r, a2i, b2r, b2i = e2
    ar = a2r * a1r - a2i * a1i
    ai = a2r * a1i + a2i * a1r
    br = a2r * b1r - a2i * b1i + b2r
    bi = a2r * b1i + a2i * b1r + b2i
    return (ar, ai, br, bi)

def s5_mixer(h, a_re, a_im, log_dt, b_re, b_im, c_re, c_im, d_skip, w_glu):
    B, L, D = h.shape
    u = h.astype(jnp.float32).reshape(B, L, N_GROUPS_2, SSM_GROUP)
    a_re = a_re.astype(jnp.float32)
    a_im = a_im.astype(jnp.float32)
    dt = jnp.exp(log_dt.astype(jnp.float32))[:, None]
    decay = jnp.exp(a_re * dt)
    ab_re = decay * jnp.cos(a_im * dt)
    ab_im = decay * jnp.sin(a_im * dt)
    den = a_re * a_re + a_im * a_im
    nr = ab_re - 1.0
    ni = ab_im
    coef_re = ((nr * a_re + ni * a_im) / den)[..., None]
    coef_im = ((ni * a_re - nr * a_im) / den)[..., None]
    br = b_re.astype(jnp.float32)
    bim = b_im.astype(jnp.float32)
    bb_re = coef_re * br - coef_im * bim
    bb_im = coef_re * bim + coef_im * br
    bu_re = jnp.einsum('blgc,gpc->blgp', u, bb_re)
    bu_im = jnp.einsum('blgc,gpc->blgp', u, bb_im)
    ar = jnp.broadcast_to(ab_re, bu_re.shape)
    ai = jnp.broadcast_to(ab_im, bu_re.shape)
    _, _, x_re, x_im = lax.associative_scan(_complex_scan_op, (ar, ai, bu_re, bu_im), axis=1)
    y = (jnp.einsum('blgp,gcp->blgc', x_re, c_re.astype(jnp.float32))
         - jnp.einsum('blgp,gcp->blgc', x_im, c_im.astype(jnp.float32)))
    y = y.reshape(B, L, D) + d_skip.astype(jnp.float32) * u.reshape(B, L, D)
    g = jax.nn.gelu(y).astype(h.dtype)
    ga, gb = jnp.split(g @ w_glu, 2, axis=-1)
    return ga * jax.nn.sigmoid(gb)

def conv_ffn(h, w_up, conv_w, conv_b, w_down):
    up = h @ w_up
    up = lax.conv_general_dilated(
        up, conv_w[:, None, :], window_strides=(1,), padding=[(CONV_W - 1, 0)],
        dimension_numbers=('NWC', 'WIO', 'NWC'), feature_group_count=2 * D_FF) + conv_b
    val, gate = jnp.split(up, 2, axis=-1)
    return (jax.nn.silu(gate) * val) @ w_down

def second_inputs(seed: int = 0) -> dict:
    key = jax.random.key(seed)
    ks = jax.random.split(key, 32)
    D = D_MODEL
    f32 = jnp.float32
    nrm = lambda k, shape, s: jax.random.normal(k, shape, f32) * s
    x = nrm(ks[0], (BATCH, SEQ, D), 1.0)
    c = nrm(ks[1], (BATCH, D), 1.0)
    offsets = jax.random.randint(ks[2], (BATCH, 1), 0, 4096, dtype=jnp.int32)
    positions = (offsets + jnp.arange(SEQ, dtype=jnp.int32)[None, :]).astype(jnp.int32)
    n_idx = jnp.arange(SSM_STATE, dtype=f32)
    return {
        "x": x,
        "c": c,
        "positions": positions,
        "ada_w": nrm(ks[3], (DEPTH_2, D, 6 * D), 0.5 * D ** -0.5),
        "ada_b": nrm(ks[4], (DEPTH_2, 6 * D), 0.02),
        "norm_mix": 1.0 + nrm(ks[5], (DEPTH_2, D), 0.02),
        "norm_ffn": 1.0 + nrm(ks[6], (DEPTH_2, D), 0.02),
        "attn_w_in": nrm(ks[7], (N_ATTN, D, IN_COLS), D ** -0.5),
        "attn_q_gain": 1.0 + nrm(ks[8], (N_ATTN, HEAD_DIM_2), 0.02),
        "attn_k_gain": 1.0 + nrm(ks[9], (N_ATTN, HEAD_DIM_2), 0.02),
        "attn_w_out": nrm(ks[10], (N_ATTN, D, D), D ** -0.5),
        "ssm_a_re": -0.5 * jnp.exp(nrm(ks[11], (N_SSM, N_GROUPS_2, SSM_STATE), 0.05)),
        "ssm_a_im": math.pi * n_idx + nrm(ks[12], (N_SSM, N_GROUPS_2, SSM_STATE), 0.05),
        "ssm_log_dt": jax.random.uniform(ks[13], (N_SSM, N_GROUPS_2), f32, math.log(1e-3), math.log(1e-1)),
        "ssm_b_re": nrm(ks[14], (N_SSM, N_GROUPS_2, SSM_STATE, SSM_GROUP), (2 * SSM_GROUP) ** -0.5),
        "ssm_b_im": nrm(ks[15], (N_SSM, N_GROUPS_2, SSM_STATE, SSM_GROUP), (2 * SSM_GROUP) ** -0.5),
        "ssm_c_re": nrm(ks[16], (N_SSM, N_GROUPS_2, SSM_GROUP, SSM_STATE), SSM_STATE ** -0.5),
        "ssm_c_im": nrm(ks[17], (N_SSM, N_GROUPS_2, SSM_GROUP, SSM_STATE), SSM_STATE ** -0.5),
        "ssm_d": nrm(ks[18], (N_SSM, D), 1.0),
        "ssm_w_glu": nrm(ks[19], (N_SSM, D, 2 * D), D ** -0.5),
        "ffn_w_up": nrm(ks[20], (DEPTH_2, D, 2 * D_FF), D ** -0.5),
        "ffn_conv_w": nrm(ks[21], (DEPTH_2, CONV_W, 2 * D_FF), CONV_W ** -0.5),
        "ffn_conv_b": nrm(ks[22], (DEPTH_2, 2 * D_FF), 0.02),
        "ffn_w_down": nrm(ks[23], (DEPTH_2, D_FF, D), D_FF ** -0.5),
    }

def second_block(x, c, positions, ada_w, ada_b, norm_mix, norm_ffn, attn_w_in, attn_q_gain,
              attn_k_gain, attn_w_out, ssm_a_re, ssm_a_im, ssm_log_dt, ssm_b_re, ssm_b_im,
              ssm_c_re, ssm_c_im, ssm_d, ssm_w_glu, ffn_w_up, ffn_conv_w, ffn_conv_b, ffn_w_down):
    cond = jax.nn.silu(c)
    for i in range(DEPTH_2):
        mod = cond @ ada_w[i] + ada_b[i]
        sh_m, sc_m, g_m, sh_f, sc_f, g_f = [m[:, None, :] for m in jnp.split(mod, 6, axis=-1)]
        h = rms_norm_2(x, norm_mix[i]) * (1.0 + sc_m) + sh_m
        j = i // N_MIXERS
        if i % N_MIXERS == 0:
            y = dsa_attention(h, positions, attn_w_in[j], attn_q_gain[j], attn_k_gain[j], attn_w_out[j])
        else:
            y = s5_mixer(h, ssm_a_re[j], ssm_a_im[j], ssm_log_dt[j], ssm_b_re[j], ssm_b_im[j],
                         ssm_c_re[j], ssm_c_im[j], ssm_d[j], ssm_w_glu[j])
        x = x + g_m * y
        h = rms_norm_2(x, norm_ffn[i]) * (1.0 + sc_f) + sh_f
        x = x + g_f * conv_ffn(h, ffn_w_up[i], ffn_conv_w[i], ffn_conv_b[i], ffn_w_down[i])
    return x


def setup_inputs(seed=0):
    out = dict(first_inputs(seed))
    for name, value in second_inputs(seed + 1).items():
        if name != "x":
            out[name + "_2"] = value
    return out


def reference(
    x, ffn1_norm, ffn1_w1, ffn1_w3, ffn1_w2, mix_norm, w_in, w_branch_attn, w_branch_pool,
    pool_w, pool_scale, w_out, ffn2_norm, ffn2_w1, ffn2_w3, ffn2_w2, final_norm, c_2,
    positions_2, ada_w_2, ada_b_2, norm_mix_2, norm_ffn_2, attn_w_in_2, attn_q_gain_2,
    attn_k_gain_2, attn_w_out_2, ssm_a_re_2, ssm_a_im_2, ssm_log_dt_2, ssm_b_re_2, ssm_b_im_2,
    ssm_c_re_2, ssm_c_im_2, ssm_d_2, ssm_w_glu_2, ffn_w_up_2, ffn_conv_w_2, ffn_conv_b_2,
    ffn_w_down_2,
):
    x = first_block(
        x, ffn1_norm, ffn1_w1, ffn1_w3, ffn1_w2, mix_norm, w_in, w_branch_attn, w_branch_pool,
        pool_w, pool_scale, w_out, ffn2_norm, ffn2_w1, ffn2_w3, ffn2_w2, final_norm,
    )
    return second_block(
        x, c_2, positions_2, ada_w_2, ada_b_2, norm_mix_2, norm_ffn_2, attn_w_in_2,
        attn_q_gain_2, attn_k_gain_2, attn_w_out_2, ssm_a_re_2, ssm_a_im_2, ssm_log_dt_2,
        ssm_b_re_2, ssm_b_im_2, ssm_c_re_2, ssm_c_im_2, ssm_d_2, ssm_w_glu_2, ffn_w_up_2,
        ffn_conv_w_2, ffn_conv_b_2, ffn_w_down_2,
    )


_drawn_inputs = setup_inputs


def setup_inputs(seed=0):
    import zlib

    import numpy as np

    out = dict(_drawn_inputs(seed))
    spreads = {}
    factors = {'ffn1_norm': 5.332,
     'mix_norm': 5.013,
     'pool_scale': 5.573,
     'ffn2_norm': 6.749,
     'norm_mix_2': 8.0,
     'norm_ffn_2': 6.393,
     'attn_q_gain_2': 8.0,
     'attn_k_gain_2': 8.0,
     'ssm_a_re_2': 64.0,
     'ssm_a_im_2': 35.64,
     'ssm_log_dt_2': 43.32,
     'ssm_b_re_2': 46.888,
     'ssm_b_im_2': 48.896,
     'ssm_c_re_2': 46.64,
     'ssm_c_im_2': 51.92,
     'ffn_conv_b_2': 6.872}
    for name, (base, spread) in spreads.items():
        noise = np.random.default_rng([zlib.crc32(name.encode()), seed]).standard_normal(out[name].shape)
        drawn = base * np.exp(spread * noise) if base else spread * noise
        out[name] = __import__('jax').numpy.asarray(drawn.astype(out[name].dtype))
    for name, factor in factors.items():
        out[name] = (out[name] * factor).astype(out[name].dtype)
    return out
```

```python
from contextlib import ExitStack

import numpy as np

import concourse.bass as bass
from concourse import mybir

F32 = mybir.dt.float32
I32 = mybir.dt.int32
ALU = mybir.AluOpType
ACT = mybir.ActivationFunctionType
AX = mybir.AxisListType

P = 128
T = 512
D = 1024
KC = D // P
F = 2816
FC = F // P
NB = T // P
EPS = 1e-6
RING = 4
WCOL = 256
SLOT = (FC // 2) * WCOL

HD = 64
G1, HPG = 3, 4
DILATIONS = (1, 4, 16)
AW = G1 * HPG * HD
QT = AW // P
POOLS = (2, 4, 8, 16)
PAD = 16
H2 = D // HD
IDX = 8
TOPK = min(256, T // 4)
ROUNDS = TOPK // 8
CHUNK = 64
BIG = -1e30
GONE = -3e38
SCOLS = [0, 128, 384, 768]
SALL = 1280
PAIRS = 32

CONST = {}


def shape_constants():
    parts = []

    def add(name, a):
        a = np.asarray(a, np.float32)
        if a.ndim == 1:
            a = a[:, None]
        full = np.zeros((P, a.shape[1]), np.float32)
        full[:a.shape[0]] = a
        start = sum(x.shape[1] for x in parts)
        CONST[name] = (start, start + full.shape[1])
        parts.append(full)

    i = np.arange(P)
    add("ident", np.eye(P))
    add("ones", np.ones((P, P)))
    add("head_ones", (i[:, None] // HD == i[None, :] // HD))
    for name, half in (("rot8", 8), ("rot32", 32)):
        r = np.zeros((P, P))
        for p in range(P):
            d = p % HD
            if d < half:
                r[p + half, p] = -1
            elif d < 2 * half:
                r[p - half, p] = 1
        add(name, r)
    pos = np.arange(T, dtype=np.float32)
    inv = (np.float32(500000.0) ** (-np.arange(0, 16, 2, dtype=np.float32) / np.float32(16))).astype(np.float32)
    ang = (pos[:, None] * inv[None, :]).astype(np.float32)
    cos, sin = np.ones((P, T)), np.zeros((P, T))
    for p in range(P):
        if p % HD < 16:
            cos[p] = np.cos(ang[:, p % HD % 8])
            sin[p] = np.sin(ang[:, p % HD % 8])
    add("cos", cos)
    add("sin", sin)
    qi, kj = np.arange(P)[:, None], np.arange(2 * P)[None, :]
    dist = qi + P - kj
    band = (dist >= 0) & (dist <= P)
    first = band & (kj >= P)
    add("mask_band0", np.where(np.concatenate([first, band], 1), 0, BIG))
    add("mask_band1", np.where(np.concatenate([band, band], 1), 0, BIG))
    d = i[:, None] - i[None, :]
    add("mask_step4", np.where(d >= 0, 0, BIG))
    add("mask_step16", np.where((d >= 0) & (d % 4 == 0), 0, BIG))
    sel = np.zeros((HPG, 2, P))
    for h in range(HPG):
        sel[h, h // 2, (h % 2) * HD:(h % 2 + 1) * HD] = 1
    add("pair_select", sel.reshape(HPG, 2 * P))
    cnt = np.zeros((P, len(POOLS), PAD))
    for g, w in enumerate(POOLS):
        cnt[:, g] = (np.float32(1) / np.minimum(np.arange(1, PAD + 1), w).astype(np.float32))[None]
    add("pool_count", cnt.reshape(P, -1))
    add("admissible", np.where((i[:, None] // CHUNK) >= (i[None, :] // CHUNK), 0, BIG))
    add("inv_freq", np.float32(10000.0) ** (-(i % 32).astype(np.float32) / np.float32(32)))
    add("group_even", i // 16 % 2 == 0)
    add("group_odd", i // 16 % 2 == 1)
    add("eps", np.full(P, EPS))
    add("half_pi", np.full(P, np.pi / 2))
    add("magic", np.broadcast_to([12582912.0, -12582912.0], (P, 2)))
    return np.concatenate(parts, 1)


SHAPE_CONSTANTS = shape_constants()
NCONST = SHAPE_CONSTANTS.shape[1]
STEPS = np.broadcast_to(np.arange(1, T + 1), (P, T)).astype(np.float32)

VROWS = {}
VTILES = 6


def vector_rows():
    at = 0
    for name, n in (("ffn1_norm", 8), ("mix_norm", 8), ("ffn2_norm", 8), ("final_norm", 8), ("norm_mix_2", 16),
                    ("norm_ffn_2", 16), ("pool_scale", 4), ("ssm_d_2", 8), ("c_2", 8), ("attn_q_gain_2", 1),
                    ("attn_k_gain_2", 1)):
        VROWS[name] = at
        at += n
    VROWS["ada_b_2"] = P
    VROWS["ffn_conv_w_2"] = 2 * P
    VROWS["ffn_conv_b_2"] = 5 * P
    return at


VFIRST = vector_rows()
CONV_ROWS = 88

FFN_SLOTS, FFN_TILES = 2 * (FC // 2) + 8, 2 * FC + KC
M1_SLOTS, M1_TILES = 6 + 3 + 8 + 2 + 3 + 4, 12 + 12 + 16 + 4 + 16 + 8
M2_SLOTS, M2_TILES = 2 + 1 + 8 + 4 + 4, 4 + 1 + 1 + 16 + 16 + 8
SSM_SLOTS, SSM_TILES = 8, 16
_order = [("ffn0", FFN_SLOTS, FFN_TILES), ("mix1", M1_SLOTS, M1_TILES), ("ffn1", FFN_SLOTS, FFN_TILES),
          ("mix2", M2_SLOTS, M2_TILES), ("ffn2", FFN_SLOTS, FFN_TILES), ("ssm", SSM_SLOTS, SSM_TILES),
          ("ffn3", FFN_SLOTS, FFN_TILES)]
SLOT0, TILE0 = {}, {}
_n = _e = 0
for _name, _s, _t in _order:
    SLOT0[_name], TILE0[_name] = _n, _e
    _n += _s
    _e += _t
NSLOTS = _n
NORM_OF_FFN = (0, 2, 5, 7)
STAGES = ("ffn0", "mix1", "ffn1", "mix2", "ffn2", "ssm", "ffn3")


def slot_frees():
    frees = {}

    def put(n, e):
        frees[n] = e

    for k in range(4):
        n, e = SLOT0[f"ffn{k}"], TILE0[f"ffn{k}"]
        for b in range(FC // 2):
            put(n + 2 * b, e + 4 * b + 3)
            put(n + 2 * b + 1, e + 4 * b + 4)
        n, e = n + FC, e + 2 * FC
        for q in range(4):
            put(n + 2 * q, e + 2 * q + 1)
            put(n + 2 * q + 1, e + 2 * q + 2)
    n, e = SLOT0["mix1"], TILE0["mix1"]
    for s in range(6):
        put(n + s, e + 2 * s + 2)
    n, e = n + 6, e + 12
    for s in range(3):
        put(n + s, e + 4 * s + 4)
    n, e = n + 3, e + 12
    for s in range(8 + 2):
        put(n + s, e + 2 * s + 2)
    n, e = n + 10, e + 20
    for s in range(3):
        put(n + s, e + 16)
    n, e = n + 3, e + 16
    for s in range(4):
        put(n + s, e + 2 * s + 2)
    n, e = SLOT0["mix2"], TILE0["mix2"]
    put(n, e + 2)
    put(n + 1, e + 4)
    put(n + 2, e + 6)
    n, e = n + 3, e + 6
    for s in range(8):
        put(n + s, e + 2 * s + 2)
    n, e = n + 8, e + 16
    for s in range(4):
        put(n + s, e + 4 * s + 4)
    n, e = n + 4, e + 16
    for s in range(4):
        put(n + s, e + 2 * s + 2)
    n, e = SLOT0["ssm"], TILE0["ssm"]
    for b in range(4):
        put(n + 2 * b, e + 4 * b + 3)
        put(n + 2 * b + 1, e + 4 * b + 4)
    return frees


FREES = slot_frees()


def attention_units():
    units = []
    for hp in range(2):
        for h in (2 * hp, 2 * hp + 1):
            units += [(0, h, 0), (0, h, 1)]
        for g in (1, 2):
            units += [(g, 2 * hp, 0), (g, 2 * hp + 1, 0)]
    return units


UNITS = attention_units()


def build(nc, a, out, stop=None):
    ctx = ExitStack()
    with ctx:
        def sb(name, shape, dt=F32):
            return ctx.enter_context(nc.sbuf_tensor(name, shape, dt))

        def sem(name):
            return ctx.enter_context(nc.semaphore(name))

        xT = sb("xT", [P, KC, T])
        hT = sb("hT", [P, KC, T])
        ring = sb("ring", [P, RING, SLOT])
        const = sb("const", [P, NCONST])
        vcol = sb("vcol", [P, VTILES, P])
        mod = sb("mod", [P, 96])
        modg = sb("modg", [P, 32])
        poolw = sb("poolw", [P, 4, P])
        acc = sb("acc", [P, T])
        sq = sb("sq", [P, 2, T])
        rs = sb("rs", [P, T])
        act_t = sb("act_t", [P, 4, T])
        phase = sb("phase", [P, 24576])
        ps = ctx.enter_context(nc.psum_tensor("ps", [P, 8, T], F32))

        def C(name, rows=P):
            lo, hi = CONST[name]
            return const[0:rows, lo:hi]

        def vec(name, k):
            row = VROWS[name] + k
            if name == "ffn_conv_w_2":
                row = VROWS[name] + P * (k // CONV_ROWS) + k % CONV_ROWS
            return vcol[:, row // P, row % P:row % P + 1]

        class Region:

            def __init__(self, start=0):
                self.at = start

            def take(self, n):
                self.at += n
                assert self.at <= 24576, self.at
                return phase[:, self.at - n:self.at]

        gT = phase[:, 0:FC * T]
        x_rows = phase[:, 0:NB * D].rearrange("p (i d) -> p i d", i=NB)
        v_rows = phase[:, NB * D:NB * D + VTILES * P].rearrange("p (i d) -> p i d", i=VTILES)
        ada_acc = phase[:, FC * T:FC * T + 12 * D].rearrange("p (j d) -> p j d", j=12)
        ada_slab = [phase[:, 24576 - D:], act_t[:, 2:4, :].rearrange("p j t -> p (j t)")]
        cond = sb("cond", [P, KC])

        r = Region()
        qk1 = r.take(12 * T).rearrange("p (j t) -> p j t", j=12)
        gates = r.take(16 * T).rearrange("p (j t) -> p j t", j=16)
        v1 = r.take(12 * 256).rearrange("p (j t) -> p j t", j=12)
        og1 = r.take(6 * T).rearrange("p (j t) -> p j t", j=6)
        s1 = r.take(2 * T).rearrange("p (j t) -> p j t", j=2)
        pt1 = r.take(2 * T).rearrange("p (j t) -> p j t", j=2)
        mst = r.take(48).rearrange("p (j t) -> p j t", j=12)
        lst = r.take(48).rearrange("p (j t) -> p j t", j=12)
        z = Region()
        merged = z.take(8 * T).rearrange("p (j t) -> p j t", j=8)
        attnT = z.take(2 * T).rearrange("p (j t) -> p j t", j=2)
        rows = merged[0:HPG]
        pool_x = [v1.rearrange("p j t -> p (j t)")[:, g * (PAD + T):(g + 1) * (PAD + T)] for g in range(4)]
        pool_s = [v1.rearrange("p j t -> p (j t)")[:, 4 * (PAD + T):5 * (PAD + T)],
                  s1.rearrange("p j t -> p (j t)")[:, 0:PAD + T]]

        s_const = sem("const_loaded")
        s_vrows = sem("vector_rows_loaded")
        s_vbank = sem("vectors_turned")
        s_vcol = sem("vector_columns")
        s_xrows = sem("x_loaded")
        w_loaded = [sem(f"w_loaded{i}") for i in range(RING)]
        tile_done = sem("tile_done")
        x_turned = sem("x_turned")
        v_cleared = sem("vector_rows_cleared")
        x_ready = sem("x_ready")
        sq_ready = sem("sq_ready")
        sq_added = sem("sq_added")
        sum_done = sem("sum_done")
        root_done = sem("root_done")
        rinv_done = sem("rinv_done")
        h_scaled = sem("h_scaled")
        h_ready = sem("h_ready")
        silu_done = sem("silu_done")
        gated = sem("gated")
        slab_loaded = [sem(f"slab_loaded{i}") for i in range(2)]
        cond_done = sem("cond_done")
        ada_step = sem("ada_step")
        ada_sum = sem("ada_sum")
        mod_done = sem("mod_done")
        evac1 = sem("proj1_evacuated")
        rot_done = sem("rot_done")
        roped = sem("roped")
        s_scores = sem("scores1")
        s_soft = sem("soft1")
        s_sum = sem("sum1")
        s_gate = sem("gates1")
        s_exp = sem("exp1")
        s_pt = sem("turned1")
        s_ptc = sem("turned1_copied")
        s_pv = sem("pv1")
        s_og = sem("outputs1")
        s_strow = sem("stat_rows")
        s_stc = sem("stat_rows_copied")
        s_w = sem("weights1")
        s_wexp = sem("weights1_exp")
        s_wb = sem("weights1_spread")
        s_mix = sem("mixed1")
        s_pool = sem("pool_steps")
        s_py = sem("pool_done")
        s_pyc = sem("pool_scaled")
        s_merge = sem("merged")
        s_out_t = sem("out_turned")
        s_out_c = sem("out_copied")
        s_out = [sem(f"out_stored{j}") for j in range(2)]

        def feat(w):
            return w.rearrange("(c p) n -> p c n", p=P)

        def slot_wait(pe, n):
            pe.wait_ge(w_loaded[n % RING], 16 * (n // RING + 1))

        def load_slot(sp, n, src, dst_cols=None):
            if n >= RING:
                sp.wait_ge(tile_done, FREES[n - RING])
            _, c, w = src.shape
            dst = ring[:, n % RING, 0:c * w].rearrange("p (c w) -> p c w", c=c)
            sp.dma_start(dst, src).then_inc(w_loaded[n % RING], 16)

        def ffn_loads(sp, k, wa, wb, wd, b_off, before_down=None):
            n0, e0 = SLOT0[f"ffn{k}"], TILE0[f"ffn{k}"]
            wa, wb, wd = feat(wa), feat(wb), feat(wd)

            def up(b):
                load_slot(sp, n0 + 2 * b, wa[:, :, b * WCOL:(b + 1) * WCOL])
                load_slot(sp, n0 + 2 * b + 1, wb[:, :, b_off + b * WCOL:b_off + (b + 1) * WCOL])

            for b in range(3):
                up(b)
            with sp.Fori(0, 4) as i:
                for j in range(4):
                    n = n0 + 6 + j
                    w, off = (wa, 0) if j % 2 == 0 else (wb, b_off)
                    sp.wait_ge(tile_done, i * 8 + FREES[n - RING])
                    src = w[:, :, bass.ds(i * (2 * WCOL) + (off + (3 + j // 2) * WCOL), WCOL)]
                    dst = ring[:, n % RING, 0:KC * WCOL].rearrange("p (c w) -> p c w", c=KC)
                    sp.dma_start(dst, src).then_inc(w_loaded[n % RING], 16)
            if before_down is not None:
                before_down()
            for q in range(4):
                for s in range(2):
                    load_slot(sp, n0 + FC + 2 * q + s,
                              wd[:, s * (FC // 2):(s + 1) * (FC // 2), q * WCOL:(q + 1) * WCOL])

        def wtile(n, c, chunks, lo, hi):
            width = {KC: WCOL, FC // 2: WCOL}[chunks]
            return ring[:, n % RING, c * width + lo:c * width + hi]

        def h_before(norm):
            return KC * (norm - (norm > 3))

        def ffn_pe(pe, k, after_quarter=None):
            n0, e0 = SLOT0[f"ffn{k}"], TILE0[f"ffn{k}"]
            norm = NORM_OF_FFN[k]
            p0 = FC * k

            def pair(nb, j, bank, first):
                for w in range(2):
                    for c in range(KC):
                        if first and w == 0:
                            pe.wait_ge(h_ready, h_before(norm) + c + 1)
                        mm = pe.matmul(ps[:, bank + w, :], wtile(nb + w, c, KC, j * P, (j + 1) * P),
                                       hT[:, c, :], start=(c == 0), stop=(c == KC - 1))
                    mm.then_inc(tile_done, 1)

            slot_wait(pe, n0)
            slot_wait(pe, n0 + 1)
            pair(n0, 0, 0, True)
            pair(n0, 1, 2, False)
            with pe.Fori(0, 5) as i:
                for b in range(2):
                    nb = n0 + 2 + 2 * b
                    for w in range(2):
                        pe.wait_ge(w_loaded[(nb + w) % RING], i * 16 + 16 * ((nb + w) // RING + 1))
                    for j in range(2):
                        pr = p0 + 2 + 2 * b + j
                        if k < 2:
                            pe.wait_ge(silu_done, i * 4 + (pr - 1))
                            pe.wait_ge(gated, i * 4 + (pr - 1))
                        else:
                            pe.wait_ge(taps, i * 16 + 4 * (pr - 2 * FC - 1))
                        pair(nb, j, 2 * j, False)
            nd = n0 + FC
            for q in range(4):
                for s in range(2):
                    slot_wait(pe, nd + 2 * q + s)
                    for t in range(2):
                        m = 2 * q + t
                        if s == 0:
                            if q == 0 and t == 0:
                                pe.wait_ge(gated, p0 + FC - 1)
                            if q >= 2:
                                pe.wait_ge(x_ready, KC * (norm + 1) + m - 3)
                        for c in range(FC // 2):
                            f = s * (FC // 2) + c
                            if q == 0 and t == 0 and f == FC - 1:
                                pe.wait_ge(gated, p0 + FC)
                            mm = pe.matmul(ps[:, (q % 2) * 2 + t, :],
                                           wtile(nd + 2 * q + s, c, FC // 2, t * P, (t + 1) * P),
                                           gT[:, f * T:(f + 1) * T], start=(f == 0), stop=(f == FC - 1))
                        if s == 1:
                            mm.then_inc(tile_done, 1)
                if after_quarter is not None:
                    after_quarter(q)

        def ffn_act(act, k):
            e0, p0 = TILE0[f"ffn{k}"], FC * k

            def one(i, p):
                act.wait_ge(tile_done, i * 8 + (e0 + 2 * p + 1))
                if p0 + p >= 2:
                    act.wait_ge(gated, i * 4 + (p0 + p - 1))
                act.activation(act_t[:, p % 2, :], ps[:, 2 * (p % 2), :], ACT.Silu).then_inc(silu_done, 1)

            one(0, 0)
            one(0, 1)
            with act.Fori(0, 5) as i:
                for p in range(2, 6):
                    one(i, p)

        def ffn_dve(dve, k):
            e0, p0 = TILE0[f"ffn{k}"], FC * k

            def one(i, p, loop):
                dve.wait_ge(silu_done, i * 4 + (p0 + p + 1))
                dve.wait_ge(tile_done, i * 8 + (e0 + 2 * p + 2))
                dst = gT[:, bass.ds(i * (4 * T) + p * T, T)] if loop else gT[:, p * T:(p + 1) * T]
                dve.tensor_tensor(dst, act_t[:, p % 2, :], ps[:, 2 * (p % 2) + 1, :], ALU.mult).then_inc(gated, 1)

            one(0, 0, False)
            one(0, 1, False)
            with dve.Fori(0, 5) as i:
                for p in range(2, 6):
                    one(i, p, True)

        def square(act, n, m):
            act.wait_ge(x_ready, KC * n + m + 1)
            if KC * n + m >= 2:
                act.wait_ge(sq_added, KC * n + m - 1)
            act.activation(sq[:, m % 2, :], xT[:, m, :], ACT.Square).then_inc(sq_ready, 1)

        def add_square(dve, n, m):
            dve.wait_ge(sq_ready, KC * n + m + 1)
            if m == 0:
                if n:
                    dve.wait_ge(sum_done, n)
                    dve.wait_ge(sq_added, KC * n)
                dve.tensor_copy(acc[:, :], sq[:, 0, :]).then_inc(sq_added, 1)
            else:
                dve.wait_ge(sq_added, KC * n + m)
                dve.tensor_tensor(acc[:, :], acc[:, :], sq[:, m % 2, :], ALU.add).then_inc(sq_added, 1)

        def residual_dve(dve, n, tile, bank_of, factor, after=None, squares=True):
            for m in range(KC):
                dve.wait_ge(tile_done, tile + m + 1)
                dve.scalar_tensor_tensor(xT[:, m, :], ps[:, bank_of(m), :], factor(m), xT[:, m, :],
                                         ALU.mult, ALU.add).then_inc(x_ready, 1)
                if m >= 1 and squares:
                    add_square(dve, n, m - 1)
                if after is not None and m in after:
                    after[m]()
            if squares:
                add_square(dve, n, KC - 1)

        def norm_pe(pe, n):
            pe.wait_ge(sq_added, KC * (n + 1))
            pe.matmul(ps[:, 4, :], C("ones"), acc[:, :], start=True, stop=True).then_inc(sum_done, 1)

        def norm_act(act, n):
            act.wait_ge(sum_done, n + 1)
            act.activation(rs[:, :], ps[:, 4, :], ACT.Sqrt, bias=C("eps"), scale=1.0 / D).then_inc(root_done, 1)

        def norm_dve(dve, n, gain, shifted=False, dst=None, signal=None):
            dst = hT if dst is None else dst
            signal = signal or (h_scaled if shifted else h_ready)
            dve.wait_ge(root_done, n + 1)
            dve.reciprocal(rs[:, :], rs[:, :]).then_inc(rinv_done, 1)
            dve.wait_ge(rinv_done, n + 1)
            for c in range(KC):
                dve.scalar_tensor_tensor(dst[:, c, :], xT[:, c, :], gain(c), rs[:, :],
                                         ALU.mult, ALU.mult).then_inc(signal, 1)

        def shift_act(act, n, first, shift):
            for c in range(KC):
                act.wait_ge(h_scaled, first + c + 1)
                act.activation(hT[:, c, :], hT[:, c, :], ACT.Identity, bias=shift(c)).then_inc(h_ready, 1)

        taps = sem("conv_taps")
        base_tap = sem("conv_base")

        ADA_STEPS = 15

        def ada_pool(pool):
            w = a["ada_w_2"]

            def load(s):
                j, c = s // KC, s % KC
                pool.dma_start(ada_slab[s % 2], w[j // 6, c * P:(c + 1) * P, (j % 6) * D:(j % 6 + 1) * D])\
                    .then_inc(slab_loaded[s % 2], 16)

            load(0)
            load(1)
            pool.wait_ge(cond_done, 1)
            pool.wait_ge(x_ready, KC)
            pool.wait_ge(s_vcol, 2)
            for s in range(12 * KC):
                j, c = s // KC, s % KC
                base = ADA_STEPS * j
                scaled = base + (1 if c == 0 else 2 * c)
                slab = ada_slab[s % 2]
                pool.wait_ge(slab_loaded[s % 2], 16 * (s // 2 + 1))
                pool.tensor_scalar(slab, slab, cond[:, c:c + 1], 0.0, ALU.mult, ALU.add).then_inc(ada_step, 1)
                if c == 0:
                    continue
                pool.wait_ge(ada_step, scaled)
                before = ada_slab[0] if c == 1 else ada_acc[:, j, :]
                pool.tensor_tensor(ada_acc[:, j, :], before, slab, ALU.add).then_inc(ada_step, 1)
                pool.wait_ge(ada_step, scaled + 1)
                for nxt in ((s + 1, s + 2) if c == 1 else (s + 2,)):
                    if nxt < 12 * KC:
                        load(nxt)

        def ada_pe(pe):
            for j in range(12):
                pe.wait_ge(ada_step, ADA_STEPS * (j + 1))
                for m in range(KC):
                    mm = pe.matmul(ps[:, 7, j * KC + m:j * KC + m + 1], ada_acc[:, j, m * P:(m + 1) * P],
                                   C("ones")[:, 0:1], start=True, stop=True)
            mm.then_inc(ada_sum, 1)

        def ada_dve(dve):
            dve.wait_ge(ada_sum, 1)
            dve.tensor_tensor(mod[:, :], ps[:, 7, 0:96], vcol[:, 1, 0:96], ALU.add).then_inc(mod_done, 1)
            dve.wait_ge(mod_done, 1)
            for l in range(2):
                for part, name in ((1, "norm_mix_2"), (4, "norm_ffn_2")):
                    row = VROWS[name] + KC * l
                    dve.scalar_tensor_tensor(modg[:, KC * (2 * l + part // 4):KC * (2 * l + part // 4 + 1)],
                                             mod[:, (6 * l + part) * KC:(6 * l + part + 1) * KC], 1.0,
                                             vcol[:, 0, row:row + KC], ALU.add, ALU.mult).then_inc(mod_done, 1)

        def shift_of(l, part, c):
            at = (6 * l + part) * KC + c
            return mod[:, at:at + 1]

        e1, n1 = TILE0["mix1"], SLOT0["mix1"]
        E_V, E_GATE, E_PZ, E_BR, E_OUT1 = 12, 24, 40, 44, 60
        NU = len(UNITS)

        def mix1_loads(sp):
            w = feat(a["w_in"][0])
            for s in range(6 + 3):
                load_slot(sp, n1 + s, w[:, :, s * WCOL:(s + 1) * WCOL])
            gate0, pool0 = 3 * AW + 4 * P, 3 * AW
            for s in range(8):
                load_slot(sp, n1 + 9 + s, w[:, :, gate0 + s * WCOL:gate0 + (s + 1) * WCOL])
            for s in range(2):
                load_slot(sp, n1 + 17 + s, w[:, :, pool0 + s * WCOL:pool0 + (s + 1) * WCOL])
            load_slot(sp, n1 + 19, feat(a["w_branch_attn"][0]))
            wp = feat(a["w_branch_pool"][0])
            for s in range(2):
                load_slot(sp, n1 + 20 + s, wp[:, 2 * s:2 * s + 2, :])
            wo = feat(a["w_out"][0])
            for s in range(4):
                load_slot(sp, n1 + 22 + s, wo[:, :, s * WCOL:(s + 1) * WCOL])

        def head1(base, g, h):
            hh = g * HPG + h
            return qk1[(hh % 2) * HD:(hh % 2 + 1) * HD, base + hh // 2, :]

        def mix1_pe(pe):
            def gemm(out, n, t, src, chunks=KC, first=None):
                for c in range(chunks):
                    if first is not None:
                        first(c)
                    mm = pe.matmul(out, wtile(n, c, KC, t * P, (t + 1) * P), src(c),
                                   start=(c == 0), stop=(c == chunks - 1))
                mm.then_inc(tile_done, 1)

            def rotate(t):
                pe.wait_ge(evac1, t + 1)
                if t >= 2:
                    pe.wait_ge(roped, 3 * (t - 2) + 2)
                pe.matmul(ps[:, 5 + t % 2, :], C("rot8"), act_t[:, t % 2, :], start=True, stop=True)\
                    .then_inc(rot_done, 1)

            for t in range(12):
                if t % 2 == 0:
                    slot_wait(pe, n1 + t // 2)
                if t >= 4:
                    pe.wait_ge(evac1, t - 3)
                gemm(ps[:, t % 4, :], n1 + t // 2, t % 2, lambda c: hT[:, c, :],
                     first=(lambda c: pe.wait_ge(h_ready, KC + c + 1)) if t == 0 else None)
                if t >= 1:
                    rotate(t - 1)
            for k in range(12):
                g, i = k // 4, k % 4
                if i == 0:
                    slot_wait(pe, n1 + 6 + g)
                pe.wait_ge(evac1, E_V + k - 3)
                tok = slice(i * P, (i + 1) * P) if g == 0 else slice(i, T, 4)
                for c in range(KC):
                    mm = pe.matmul(ps[:, k % 4, 0:256], hT[:, c, tok], wtile(n1 + 6 + g, c, KC, 0, 256),
                                   start=(c == 0), stop=(c == KC - 1))
                mm.then_inc(tile_done, 1)
                if k == 0:
                    rotate(11)

            def scores(u):
                g, h, w = UNITS[u]
                bank = 5 + u % 2
                if u == 0:
                    pe.wait_ge(roped, 36)
                if u >= 2:
                    pe.wait_ge(s_soft, 3 * (u - 2) + 1)
                q, k = head1(0, g, h), head1(6, g, h)
                if g == 0:
                    for b in (2 * w, 2 * w + 1):
                        at = (b % 2) * 2 * P
                        qb = q[:, b * P:(b + 1) * P]
                        if b == 0:
                            for half in range(2):
                                mm = pe.matmul(ps[:, bank, at + half * P:at + (half + 1) * P], qb, k[:, 0:P],
                                               start=True, stop=True)
                        else:
                            mm = pe.matmul(ps[:, bank, at:at + 2 * P], qb, k[:, (b - 1) * P:(b + 1) * P],
                                           start=True, stop=True)
                else:
                    for r in range(4):
                        mm = pe.matmul(ps[:, bank, r * P:(r + 1) * P], q[:, r:T:4], k[:, r:T:4],
                                       start=True, stop=True)
                mm.then_inc(s_scores, 1)

            def turn(u):
                pe.wait_ge(s_exp, u + 1)
                if u >= 2:
                    pe.wait_ge(s_ptc, u - 1)
                for part in range(4):
                    mm = pe.transpose(ps[:, 7 if u % 2 == 0 else 4, part * P:(part + 1) * P],
                                      s1[:, u % 2, part * P:(part + 1) * P], C("ident"))
                mm.then_inc(s_pt, 1)

            def values(u):
                g, h, w = UNITS[u]
                o = 3 * (h // 2) + g
                pe.wait_ge(s_ptc, u + 1)
                if o >= 2:
                    pe.wait_ge(s_og, o - 1)
                rows_of = ps[(h % 2) * HD:(h % 2 + 1) * HD, 2 + o % 2, :]
                for part in range(4):
                    p_t = pt1[:, u % 2, part * P:(part + 1) * P]
                    if g == 0:
                        b = 2 * w + part // 2
                        keys = b if part % 2 else max(b - 1, 0)
                        mm = pe.matmul(rows_of[:, b * P:(b + 1) * P], v1[:, keys, h * HD:(h + 1) * HD], p_t,
                                       start=(part % 2 == 0), stop=(part % 2 == 1))
                    else:
                        mm = pe.matmul(rows_of[:, part * P:(part + 1) * P],
                                       v1[:, 4 * g + part, h * HD:(h + 1) * HD], p_t, start=True, stop=True)
                mm.then_inc(s_pv, 1)

            pe.wait_ge(evac1, E_GATE)
            for u in range(NU + 2):
                if u < NU:
                    scores(u)
                if 1 <= u <= NU:
                    turn(u - 1)
                if u >= 2:
                    values(u - 2)
                if u < NU:
                    if u % 2 == 0:
                        slot_wait(pe, n1 + 9 + u // 2)
                    if u >= 2:
                        pe.wait_ge(evac1, E_GATE + u - 1)
                    gemm(ps[:, u % 2, :], n1 + 9 + u // 2, u % 2, lambda c: hT[:, c, :])
            pe.wait_ge(s_sum, NU)
            pe.wait_ge(s_og, 6)
            for k in range(6):
                stat = mst if k % 2 == 0 else lst
                g = k // 2
                for i in range(NB):
                    mm = pe.transpose(ps[0:HPG, 2 + k, i * P:(i + 1) * P], stat[:, g * HPG:(g + 1) * HPG, i],
                                      C("ident"))
            mm.then_inc(s_strow, 1)
            for k in range(4):
                if k % 2 == 0:
                    slot_wait(pe, n1 + 17 + k // 2)
                pe.wait_ge(evac1, E_PZ + k - 1)
                gemm(ps[:, k % 2, :], n1 + 17 + k // 2, k % 2, lambda c: hT[:, c, :])
            pe.wait_ge(s_stc, 6)
            for hp in range(2):
                for g in range(G1):
                    pe.wait_ge(s_w, 12 + g)
                    pe.matmul(ps[:, 2 + 3 * hp + g, :], C("pair_select", HPG)[:, hp * P:(hp + 1) * P],
                              rows[:, 2 * g, :], start=True, stop=True).then_inc(s_wb, 1)
            pe.wait_ge(evac1, E_PZ + 4)
            for g in range(4):
                pe.wait_ge(s_pool, POOL_AT[g])
                if g >= 2:
                    pe.wait_ge(s_pyc, g - 1)
                pe.matmul(ps[:, g % 2, :], poolw[:, g, :], pool_x[g][:, PAD:], start=True, stop=True)\
                    .then_inc(s_py, 1)
            for s in range(3):
                slot_wait(pe, n1 + 19 + s)
            pe.wait_ge(s_pyc, 4)
            for m in range(KC):
                if m >= 2:
                    pe.wait_ge(s_merge, 3 * (m - 2) + 2)
                for c in range(4):
                    mm = pe.matmul(ps[:, m % 2, :], ring[:, (n1 + 20 + c // 2) % RING,
                                                         (c % 2) * D + m * P:(c % 2) * D + (m + 1) * P],
                                   hT[:, c, :], start=(c == 0), stop=(c == 3))
                mm.then_inc(tile_done, 1)
                if m == 0:
                    pe.wait_ge(s_mix, 10)
                for c in range(2):
                    mm = pe.matmul(ps[:, 2 + m % 2, :], ring[:, (n1 + 19) % RING, c * D + m * P:c * D + (m + 1) * P],
                                   attnT[:, c, :], start=(c == 0), stop=(c == 1))
                mm.then_inc(tile_done, 1)
            for m in range(KC):
                if m % 2 == 0:
                    slot_wait(pe, n1 + 22 + m // 2)
                if m >= 4:
                    pe.wait_ge(x_ready, 2 * KC + m - 3)
                gemm(ps[:, 4 + m % 4, :], n1 + 22 + m // 2, m % 2, lambda c: merged[:, c, :],
                     first=(lambda c: pe.wait_ge(s_merge, 3 * (c + 1))) if m == 0 else None)

        def natural(x):
            return x.rearrange("p (r q) -> p r q", r=4)

        def by_residue(x):
            return x.rearrange("p (q r) -> p r q", r=4)

        def mix1_act(act):
            for t in range(12):
                act.wait_ge(tile_done, e1 + t + 1)
                if t >= 2:
                    act.wait_ge(roped, 3 * (t - 2) + 2)
                act.activation(act_t[:, t % 2, :], ps[:, t % 4, :], ACT.Copy).then_inc(evac1, 1)
            for k in range(12):
                act.wait_ge(tile_done, e1 + E_V + k + 1)
                act.activation(v1[:, k, :], ps[:, k % 4, 0:256], ACT.Copy).then_inc(evac1, 1)
            for u in range(NU + 1):
                if u >= 1:
                    act.wait_ge(s_pt, u)
                    if u >= 3:
                        act.wait_ge(s_pv, u - 2)
                    v = u - 1
                    act.activation(pt1[:, v % 2, :], ps[:, 7 if v % 2 == 0 else 4, :], ACT.Copy).then_inc(s_ptc, 1)
                if u < NU:
                    act.wait_ge(s_soft, 3 * u + 3)
                    act.activation(s1[:, u % 2, :], s1[:, u % 2, :], ACT.Exp, scale=HD ** -0.5).then_inc(s_exp, 1)
                    act.wait_ge(tile_done, e1 + E_GATE + u + 1)
                    act.activation(gates[:, u, :], ps[:, u % 2, :], ACT.Exp, scale=-1.0).then_inc(evac1, 1)
            act.wait_ge(s_strow, 1)
            for k in range(6):
                dst, src = rows[:, k, :], ps[0:HPG, 2 + k, :]
                if k >= 2:
                    dst, src = by_residue(dst), natural(src)
                act.activation(dst, src, ACT.Copy).then_inc(s_stc, 1)
            for g in range(G1):
                act.wait_ge(s_w, 3 + g)
                act.activation(rows[:, 2 * g, :], rows[:, 2 * g, :], ACT.Exp, scale=HD ** -0.5).then_inc(s_wexp, 1)
            for k in range(4):
                act.wait_ge(tile_done, e1 + E_PZ + k + 1)
                act.activation(pool_x[k][:, PAD:], ps[:, k % 2, :], ACT.Copy).then_inc(evac1, 1)
            for g in range(4):
                act.wait_ge(s_py, g + 1)
                act.activation(hT[:, g, :], ps[:, g % 2, :], ACT.Identity, scale=vec("pool_scale", g)).then_inc(s_pyc, 1)

        def mix1_dve(dve):
            for t in range(12):
                dve.wait_ge(evac1, t + 1)
                dve.tensor_tensor(qk1[:, t, :], act_t[:, t % 2, :], C("cos"), ALU.mult).then_inc(roped, 1)
                dve.wait_ge(rot_done, t + 1)
                if t >= 2:
                    dve.wait_ge(roped, 3 * (t - 2) + 3)
                dve.tensor_tensor(act_t[:, 2 + t % 2, :], ps[:, 5 + t % 2, :], C("sin"), ALU.mult).then_inc(roped, 1)
                dve.wait_ge(roped, 3 * t + 2)
                dve.tensor_tensor(qk1[:, t, :], qk1[:, t, :], act_t[:, 2 + t % 2, :], ALU.add).then_inc(roped, 1)

            def parts(u):
                g, h, w = UNITS[u]
                hh = g * HPG + h
                if g == 0:
                    return (s1[:, u % 2, :].rearrange("p (b k) -> p b k", b=2), mst[:, hh, 2 * w:2 * w + 2],
                            lst[:, hh, 2 * w:2 * w + 2], C(f"mask_band{w}").rearrange("p (b k) -> p b k", b=2), 2)
                mask = C("mask_step4" if g == 1 else "mask_step16").unsqueeze(1).to_broadcast([P, 4, P])
                return (s1[:, u % 2, :].rearrange("p (b k) -> p b k", b=4), mst[:, hh, :], lst[:, hh, :], mask, 4)

            def soft(u):
                s, m, _, mask, b = parts(u)
                dve.wait_ge(s_scores, u + 1)
                if u >= 2:
                    dve.wait_ge(s_pt, u - 1)
                    dve.wait_ge(s_sum, u - 1)
                dve.tensor_tensor(s, ps[:, 5 + u % 2, :].rearrange("p (b k) -> p b k", b=b), mask, ALU.add)\
                    .then_inc(s_soft, 1)
                dve.wait_ge(s_soft, 3 * u + 1)
                dve.tensor_reduce(m, s, AX.X, ALU.max).then_inc(s_soft, 1)
                dve.wait_ge(s_soft, 3 * u + 2)
                dve.tensor_tensor(s, s, m.unsqueeze(2).to_broadcast([P, b, T // b]), ALU.subtract).then_inc(s_soft, 1)

            def total(u):
                s, _, l, _, _ = parts(u)
                dve.wait_ge(s_exp, u + 1)
                dve.tensor_reduce(l, s, AX.X, ALU.add).then_inc(s_sum, 1)

            def gate(u):
                dve.wait_ge(evac1, E_GATE + u + 1)
                dve.tensor_scalar(gates[:, u, :], gates[:, u, :], 1.0, None, ALU.add).then_inc(s_gate, 1)
                dve.wait_ge(s_gate, 2 * u + 1)
                dve.reciprocal(gates[:, u, :], gates[:, u, :]).then_inc(s_gate, 1)

            for u in range(NU + 2):
                if u < NU:
                    soft(u)
                if 1 <= u <= NU:
                    total(u - 1)
                    gate(u - 1)
                if u >= 2 and (u == NU + 1 or (UNITS[u - 2][0], UNITS[u - 2][1] // 2) !=
                               (UNITS[u - 1][0], UNITS[u - 1][1] // 2)):
                    g, h, _ = UNITS[u - 2]
                    o = 3 * (h // 2) + g
                    dve.wait_ge(s_pv, u - 1)
                    dst, src = og1[:, o, :], ps[:, 2 + o % 2, :]
                    if g:
                        dst, src = by_residue(dst), natural(src)
                    dve.tensor_copy(dst, src).then_inc(s_og, 1)
            dve.wait_ge(s_stc, 6)
            mx, tot = rows[:, 6, :], rows[:, 7, :]
            dve.tensor_tensor(mx, rows[:, 0, :], rows[:, 2, :], ALU.max).then_inc(s_w, 1)
            dve.wait_ge(s_w, 1)
            dve.tensor_tensor(mx, mx, rows[:, 4, :], ALU.max).then_inc(s_w, 1)
            dve.wait_ge(s_w, 2)
            for g in range(G1):
                dve.tensor_tensor(rows[:, 2 * g, :], rows[:, 2 * g, :], mx, ALU.subtract).then_inc(s_w, 1)
            for g in range(G1):
                dve.wait_ge(s_wexp, g + 1)
                dve.tensor_tensor(rows[:, 2 * g + 1, :], rows[:, 2 * g + 1, :], rows[:, 2 * g, :], ALU.mult)\
                    .then_inc(s_w, 1)
            dve.wait_ge(s_w, 7)
            dve.tensor_tensor(tot, rows[:, 1, :], rows[:, 3, :], ALU.add).then_inc(s_w, 1)
            dve.wait_ge(s_w, 9)
            dve.tensor_tensor(tot, tot, rows[:, 5, :], ALU.add).then_inc(s_w, 1)
            dve.wait_ge(s_w, 10)
            dve.reciprocal(tot, tot).then_inc(s_w, 1)
            dve.wait_ge(s_w, 11)
            for g in range(G1):
                dve.tensor_tensor(rows[:, 2 * g, :], rows[:, 2 * g, :], tot, ALU.mult).then_inc(s_w, 1)
            for hp in range(2):
                for g in range(G1):
                    j = 3 * hp + g
                    dve.wait_ge(s_wb, j + 1)
                    dve.tensor_tensor(og1[:, j, :], og1[:, j, :], ps[:, 2 + j, :], ALU.mult).then_inc(s_mix, 1)
                dve.wait_ge(s_mix, 5 * hp + 2)
                dve.tensor_tensor(attnT[:, hp, :], og1[:, 3 * hp, :], og1[:, 3 * hp + 1, :], ALU.add)\
                    .then_inc(s_mix, 1)
                dve.wait_ge(s_mix, 5 * hp + 4)
                dve.tensor_tensor(attnT[:, hp, :], attnT[:, hp, :], og1[:, 3 * hp + 2, :], ALU.add)\
                    .then_inc(s_mix, 1)
            dve.wait_ge(s_gate, 2 * NU)
            for m in range(KC):
                if m >= 2:
                    dve.wait_ge(s_merge, 3 * (m - 2) + 3)
                dve.wait_ge(tile_done, e1 + E_BR + 2 * m + 1)
                dve.tensor_tensor(act_t[:, m % 2, :], ps[:, m % 2, :], gates[:, KC + m, :], ALU.mult).then_inc(s_merge, 1)
                dve.wait_ge(tile_done, e1 + E_BR + 2 * m + 2)
                dve.tensor_tensor(act_t[:, 2 + m % 2, :], ps[:, 2 + m % 2, :], gates[:, m, :], ALU.mult)\
                    .then_inc(s_merge, 1)
                dve.wait_ge(s_merge, 3 * m + 2)
                dve.tensor_tensor(merged[:, m, :], act_t[:, m % 2, :], act_t[:, 2 + m % 2, :], ALU.add)\
                    .then_inc(s_merge, 1)
            residual_dve(dve, 2, e1 + E_OUT1, lambda m: 4 + m % 4, lambda m: 1.0)

        POOL_AT, n = [], 6
        for g in range(4):
            n += g + 1 + 3
            POOL_AT.append(n)

        def mix1_pool(pool):
            pool.wait_ge(s_pv, NU)
            pool.wait_ge(s_pt, NU)
            pool.wait_ge(s_sum, NU)
            for x in pool_x + pool_s:
                pool.memset(x[:, 0:PAD], 0.0).then_inc(s_pool, 1)
            n = 6
            pool.wait_ge(s_pool, n)
            for g, win in enumerate(POOLS):
                pool.wait_ge(evac1, E_PZ + g + 1)
                cur, lag, k = pool_x[g], 1, 0
                while lag < win:
                    dst = pool_s[k % 2]
                    pool.tensor_tensor(dst[:, PAD:], cur[:, PAD:], cur[:, PAD - lag:PAD + T - lag], ALU.add)\
                        .then_inc(s_pool, 1)
                    n += 1
                    pool.wait_ge(s_pool, n)
                    cur, lag, k = dst, 2 * lag, k + 1
                mean = pool_s[k % 2]
                pool.tensor_scalar(mean[:, PAD:], cur[:, PAD:], 1.0 / win, 0.0, ALU.mult, ALU.add).then_inc(s_pool, 1)
                pool.wait_ge(s_pool, n + 1)
                pool.tensor_tensor(mean[:, PAD:2 * PAD], cur[:, PAD:2 * PAD],
                                   C("pool_count")[:, g * PAD:(g + 1) * PAD], ALU.mult).then_inc(s_pool, 1)
                pool.wait_ge(s_pool, n + 2)
                pool.tensor_tensor(pool_x[g][:, PAD:], mean[:, PAD:], pool_x[g][:, PAD:], ALU.subtract)\
                    .then_inc(s_pool, 1)
                n += 3
                pool.wait_ge(s_pool, n)
                assert n == POOL_AT[g]


        TWO_PI = (6.28125, 8117.0 / 2 ** 22, float(np.float32(2 * np.pi - 6.28125 - 8117.0 / 2 ** 22)))
        MAGIC = 12582912.0
        PI = 3.1415925

        def reduce_angle(dve, ang, k, signal, at):
            dve.tensor_scalar(k, ang, 1 / (2 * np.pi), MAGIC, ALU.mult, ALU.add).then_inc(signal, 1)
            dve.wait_ge(signal, at + 1)
            dve.tensor_scalar(k, k, -MAGIC, None, ALU.add).then_inc(signal, 1)
            dve.wait_ge(signal, at + 2)
            for n, part in enumerate(TWO_PI):
                dve.scalar_tensor_tensor(ang, k, -part, ang, ALU.mult, ALU.add).then_inc(signal, 1)
                dve.wait_ge(signal, at + 3 + n)
            dve.tensor_scalar(ang, ang, PI, -PI, ALU.min, ALU.max).then_inc(signal, 1)
            dve.wait_ge(signal, at + 6)

        s_pos = sem("positions_loaded")
        s_ang = sem("angle_steps")
        s_sin = sem("sines_done")

        def tables_dve(dve):
            ang, k = act_t[:, 2, :], act_t[:, 3, :]
            dve.wait_ge(s_pos, 16)
            dve.tensor_copy(ang, k.bitcast(I32)).then_inc(s_ang, 1)
            dve.wait_ge(s_ang, 1)
            dve.tensor_scalar(ang, ang, C("inv_freq"), None, ALU.mult).then_inc(s_ang, 1)
            dve.wait_ge(s_ang, 2)
            reduce_angle(dve, ang, k, s_ang, 2)

        def tables_act(act):
            act.wait_ge(s_ang, 8)
            act.activation(C("sin"), act_t[:, 2, :], ACT.Sin).then_inc(s_sin, 1)
            act.activation(act_t[:, 3, :], act_t[:, 2, :], ACT.Abs).then_inc(s_sin, 1)
            act.wait_ge(s_sin, 2)
            act.activation(C("cos"), act_t[:, 3, :], ACT.Sin, bias=C("half_pi"), scale=-1.0).then_inc(s_sin, 1)

        r2 = Region()
        qk2 = r2.take(16 * T).rearrange("p (j t) -> p j t", j=16)
        v2 = r2.take(NB * D).rearrange("p (i d) -> p i d", i=NB)
        r_index = r2.at
        index_qk = r2.take(5 * T)
        iqk = index_qk.rearrange("p (j t) -> p j t", j=5)
        score = r2.take(SALL)
        work = r2.take(SALL)
        bias2 = r2.take(SALL)
        soft2 = [phase[:, r_index:][:, j * 2 * T:(j + 1) * 2 * T].rearrange("p (s k) -> p s k", s=2) for j in range(3)]
        pt2 = [r2.take(2 * T).rearrange("p (s k) -> p s k", s=2) for _ in range(2)]
        diag = [r2.take(2 * P).rearrange("p (s k) -> p s k", s=2) for _ in range(2)]
        wi = r2.take(NB * IDX)
        top8 = r2.take(NB * 8).rearrange("p (i k) -> p i k", i=NB)
        mx2 = r2.take(6)
        nm2 = r2.take(6)
        sum2 = r2.take(6)
        e2, n2 = TILE0["mix2"], SLOT0["mix2"]
        E2_K, E2_W, E2_QK, E2_V, E2_OUT = 4, 5, 6, 22, 38
        rbuf = (acc, rs)

        evac2 = sem("proj2_evacuated")
        rot2 = sem("index_rotated")
        roped2 = sem("index_roped")
        s_logit = sem("index_logits")
        s_relu = sem("index_relu")
        s_idx = sem("index_added")
        s_adm = sem("index_masked")
        s_top = sem("top_steps")
        s_bias = sem("bias_done")
        s_ss = sem("head_squares")
        s_hroot = sem("head_roots")
        s_hn = sem("head_norms")
        s_hrot = sem("head_rotated")
        s_hrope = sem("head_roped")
        s_qk2 = sem("scores2")
        s_mask2 = sem("masked2")
        s_exp2 = sem("exp2")
        s_diag = sem("diag2")
        s_t2 = sem("turned2")
        s_tca = sem("turned2_copied_act")
        s_tcd = sem("turned2_copied_dve")
        s_pv2 = sem("pv2")
        s_o2 = sem("outputs2")

        def mix2_loads(sp):
            w = feat(a["attn_w_in_2"][0])
            for s in range(2):
                load_slot(sp, n2 + s, w[:, :, 3 * D + s * WCOL:3 * D + (s + 1) * WCOL])
            load_slot(sp, n2 + 2, w[:, :, 3 * D + IDX * HD:3 * D + IDX * HD + HD + IDX])
            for s in range(8 + 4):
                load_slot(sp, n2 + 3 + s, w[:, :, s * WCOL:(s + 1) * WCOL])
            wo = feat(a["attn_w_out_2"][0])
            for s in range(4):
                load_slot(sp, n2 + 15 + s, wo[:, :, s * WCOL:(s + 1) * WCOL])

        UNITS2 = [(pair, i) for pair in range(H2 // 2) for i in range(NB)]
        NU2 = len(UNITS2)

        def head2(base, h):
            return qk2[(h % 2) * HD:(h % 2 + 1) * HD, base + h // 2, :]

        def mix2_pe(pe):
            hn = h_before(4)

            def gemm(out, n, t, src, first=None):
                for c in range(KC):
                    if first is not None:
                        first(c)
                    mm = pe.matmul(out, wtile(n, c, KC, t * P, (t + 1) * P), src(c),
                                   start=(c == 0), stop=(c == KC - 1))
                mm.then_inc(tile_done, 1)

            def rotate(t):
                pe.wait_ge(evac2, t + 1)
                if t >= 2:
                    pe.wait_ge(roped2, 3 * (t - 2) + 2)
                pe.matmul(ps[:, 5 + t % 2, :], C("rot32"), act_t[:, t % 2, :], start=True, stop=True)\
                    .then_inc(rot2, 1)

            for t in range(4):
                if t % 2 == 0:
                    slot_wait(pe, n2 + t // 2)
                gemm(ps[:, t, :], n2 + t // 2, t % 2, lambda c: hT[:, c, :],
                     first=(lambda c: pe.wait_ge(h_ready, hn + c + 1)) if t == 0 else None)
                if t >= 1:
                    rotate(t - 1)
            slot_wait(pe, n2 + 2)
            pe.wait_ge(evac2, 2)
            wk = ring[:, (n2 + 2) % RING, 0:KC * (HD + IDX)].rearrange("p (c w) -> p c w", c=KC)
            for half in range(2):
                for c in range(KC):
                    mm = pe.matmul(ps[half * HD:(half + 1) * HD, 0, :], wk[:, c, 0:HD], hT[:, c, :],
                                   start=(c == 0), stop=(c == KC - 1))
            mm.then_inc(tile_done, 1)
            rotate(3)
            for i in range(NB):
                for c in range(KC):
                    mm = pe.matmul(ps[:, 1, i * IDX:(i + 1) * IDX], hT[:, c, i * P:(i + 1) * P], wk[:, c, HD:],
                                   start=(c == 0), stop=(c == KC - 1))
            mm.then_inc(tile_done, 1)
            rotate(4)
            pe.wait_ge(roped2, 15)
            for i in range(NB):
                for x in range(IDX):
                    y = i * IDX + x
                    if y >= 4:
                        pe.wait_ge(s_relu, y - 3)
                    half = slice((x % 2) * HD, (x % 2 + 1) * HD)
                    pe.matmul(ps[:, 4 + y % 4, 0:(i + 1) * P], iqk[half, x // 2, i * P:(i + 1) * P],
                              iqk[half, 4, 0:(i + 1) * P], start=True, stop=True).then_inc(s_logit, 1)
            pe.wait_ge(evac2, E2_QK)
            pe.wait_ge(s_relu, NB * IDX)
            for t in range(18):
                if t < 16:
                    if t % 2 == 0:
                        slot_wait(pe, n2 + 3 + t // 2)
                    if t >= 4:
                        pe.wait_ge(evac2, E2_QK + 2 * (t - 4) + 2)
                    gemm(ps[:, t % 4, :], n2 + 3 + t // 2, t % 2, lambda c: hT[:, c, :])
                if 1 <= t <= 16:
                    v = t - 1
                    pe.wait_ge(evac2, E2_QK + 2 * v + 2)
                    if v >= 2:
                        pe.wait_ge(s_hroot, v - 1)
                    pe.matmul(ps[:, 4 + v % 2, :], C("head_ones"), sq[:, v % 2, :], start=True, stop=True)\
                        .then_inc(s_ss, 1)
                if t >= 2:
                    v = t - 2
                    pe.wait_ge(s_hn, 2 * v + 2)
                    if v >= 2:
                        pe.wait_ge(s_hrope, 3 * (v - 2) + 2)
                    pe.matmul(ps[:, 6 + v % 2, :], C("rot32"), act_t[:, v % 2, :], start=True, stop=True)\
                        .then_inc(s_hrot, 1)
            for k in range(16):
                s, i = k // 4, k % 4
                if i == 0:
                    slot_wait(pe, n2 + 11 + s)
                pe.wait_ge(evac2, E2_QK + 2 * (12 + k) + 2 if k < 4 else E2_QK + 32 + k - 3)
                for c in range(KC):
                    mm = pe.matmul(ps[:, k % 4, 0:256], hT[:, c, i * P:(i + 1) * P],
                                   wtile(n2 + 11 + s, c, KC, 0, 256), start=(c == 0), stop=(c == KC - 1))
                mm.then_inc(tile_done, 1)

            pe.wait_ge(s_hrope, 48)
            pe.wait_ge(evac2, E2_QK + 32 + 16)
            for st in range(NU2 + 3):
                if st < NU2:
                    u, (pair, i) = st, UNITS2[st]
                    if u >= 2:
                        pe.wait_ge(s_mask2, 3 * (u - 2) + 2)
                    for s in range(2):
                        mm = pe.matmul(ps[:, 2 * (u % 2) + s, 0:(i + 1) * P],
                                       head2(0, 2 * pair + s)[:, i * P:(i + 1) * P],
                                       head2(8, 2 * pair + s)[:, 0:(i + 1) * P], start=True, stop=True)
                    mm.then_inc(s_qk2, 1)
                if 2 <= st < NU2 + 2:
                    u, (pair, i) = st - 2, UNITS2[st - 2]
                    pe.wait_ge(s_diag, 2 * u + 2)
                    if u >= 1:
                        pe.wait_ge(s_tca, u)
                        pe.wait_ge(s_tcd, u)
                    for s in range(2):
                        for j in range(i + 1):
                            mm = pe.matmul(ps[:, 4 + s, j * P:(j + 1) * P], soft2[u % 3][:, s, j * P:(j + 1) * P],
                                           diag[u % 2][:, s, :], start=True, stop=True)
                    mm.then_inc(s_t2, 1)
                if st >= 3:
                    u, (pair, i) = st - 3, UNITS2[st - 3]
                    pe.wait_ge(s_tca, u + 1)
                    pe.wait_ge(s_tcd, u + 1)
                    if pair >= 2:
                        pe.wait_ge(s_o2, pair - 1)
                    for j in range(i + 1):
                        for s in range(2):
                            h = 2 * pair + s
                            mm = pe.matmul(ps[s * HD:(s + 1) * HD, 6 + pair % 2, i * P:(i + 1) * P],
                                           v2[:, j, h * HD:(h + 1) * HD], pt2[u % 2][:, s, j * P:(j + 1) * P],
                                           start=(j == 0), stop=(j == i))
                    mm.then_inc(s_pv2, 1)
            for m in range(KC):
                if m % 2 == 0:
                    slot_wait(pe, n2 + 15 + m // 2)
                if m >= 4:
                    pe.wait_ge(x_ready, 5 * KC + m - 3)
                gemm(ps[:, m % 4, :], n2 + 15 + m // 2, m % 2, lambda c: hT[:, c, :],
                     first=(lambda c: pe.wait_ge(s_o2, c + 1)) if m == 0 else None)

        def mix2_act(act):
            for t in range(5):
                act.wait_ge(tile_done, e2 + t + 1)
                if t >= 2:
                    act.wait_ge(roped2, 3 * (t - 2) + 2)
                act.activation(act_t[:, t % 2, :], ps[:, t % 4, :], ACT.Copy).then_inc(evac2, 1)
            act.wait_ge(tile_done, e2 + E2_W + 1)
            act.activation(wi, ps[:, 1, 0:NB * IDX], ACT.Copy, scale=IDX ** -0.5).then_inc(evac2, 1)
            act.wait_ge(roped2, 15)
            for y in range(NB * IDX):
                w = (y // IDX + 1) * P
                act.wait_ge(s_logit, y + 1)
                if y >= 4:
                    act.wait_ge(s_idx, y - 3)
                act.activation(act_t[:, y % 4, 0:w], ps[:, 4 + y % 4, 0:w], ACT.Relu, scale=HD ** -0.5)\
                    .then_inc(s_relu, 1)
            act.wait_ge(s_idx, NB * IDX)
            for t in range(17):
                if t >= 1:
                    v = t - 1
                    act.wait_ge(s_ss, v + 1)
                    if v >= 2:
                        act.wait_ge(s_hn, 2 * (v - 2) + 2)
                    act.activation(rbuf[v % 2][:, :], ps[:, 4 + v % 2, :], ACT.Sqrt, bias=C("eps"),
                                   scale=1.0 / HD).then_inc(s_hroot, 1)
                if t < 16:
                    act.wait_ge(tile_done, e2 + E2_QK + t + 1)
                    if t >= 2:
                        act.wait_ge(s_hrope, 3 * (t - 2) + 2)
                        act.wait_ge(s_ss, t - 1)
                    act.activation(act_t[:, t % 2, :], ps[:, t % 4, :], ACT.Copy).then_inc(evac2, 1)
                    act.activation(sq[:, t % 2, :], ps[:, t % 4, :], ACT.Square).then_inc(evac2, 1)
            for k in range(16):
                s, i = k // 4, k % 4
                act.wait_ge(tile_done, e2 + E2_V + k + 1)
                act.activation(v2[:, i, s * 256:(s + 1) * 256], ps[:, k % 4, 0:256], ACT.Copy).then_inc(evac2, 1)
            for st in range(NU2 + 3):
                if 2 <= st < NU2 + 2:
                    u, (pair, i) = st - 2, UNITS2[st - 2]
                    w = (i + 1) * P
                    act.wait_ge(s_t2, u + 1)
                    if u >= 2:
                        act.wait_ge(s_pv2, u - 1)
                    act.activation(pt2[u % 2][:, 0, 0:w], ps[:, 4, 0:w], ACT.Copy).then_inc(s_tca, 1)
                if st < NU2:
                    u, (pair, i) = st, UNITS2[st]
                    act.wait_ge(s_mask2, 3 * u + 3)
                    if u >= 3:
                        act.wait_ge(s_diag, 2 * (u - 3) + 1)
                    for s in range(2):
                        x, o = soft2[u % 3][:, s, 0:(i + 1) * P], 2 * (u % 3) + s
                        act.activation(x, x, ACT.Exp, bias=nm2[:, o:o + 1], scale=HD ** -0.5,
                                       accum_out=sum2[:, o:o + 1]).then_inc(s_exp2, 1)
                if st >= 3 and UNITS2[st - 3][1] == NB - 1:
                    pair = UNITS2[st - 3][0]
                    act.wait_ge(s_pv2, st - 2)
                    act.activation(hT[:, pair, :], ps[:, 6 + pair % 2, :], ACT.Copy).then_inc(s_o2, 1)

        def mix2_dve(dve):
            dve.wait_ge(s_sin, 3)
            for t in range(5):
                dve.wait_ge(evac2, t + 1)
                dve.tensor_tensor(iqk[:, t, :], act_t[:, t % 2, :], C("cos"), ALU.mult).then_inc(roped2, 1)
                dve.wait_ge(rot2, t + 1)
                if t >= 2:
                    dve.wait_ge(roped2, 3 * (t - 2) + 3)
                dve.tensor_tensor(act_t[:, 2 + t % 2, :], ps[:, 5 + t % 2, :], C("sin"), ALU.mult).then_inc(roped2, 1)
                dve.wait_ge(roped2, 3 * t + 2)
                dve.tensor_tensor(iqk[:, t, :], iqk[:, t, :], act_t[:, 2 + t % 2, :], ALU.add).then_inc(roped2, 1)
            dve.wait_ge(evac2, E2_W + 1)
            for i in range(NB):
                dst = score[:, SCOLS[i]:SCOLS[i] + (i + 1) * P]
                for x in range(IDX):
                    y = i * IDX + x
                    dve.wait_ge(s_relu, y + 1)
                    relu, w = act_t[:, y % 4, 0:(i + 1) * P], wi[:, y:y + 1]
                    if x == 0:
                        dve.tensor_scalar(dst, relu, w, None, ALU.mult).then_inc(s_idx, 1)
                    else:
                        dve.wait_ge(s_idx, y)
                        dve.scalar_tensor_tensor(dst, relu, w, dst, ALU.mult, ALU.add).then_inc(s_idx, 1)
            dve.tensor_copy(bias2[:, 0:P], C("admissible")).then_inc(s_adm, 1)
            dve.wait_ge(s_idx, NB * IDX)
            for i in range(1, NB):
                own = score[:, SCOLS[i] + i * P:SCOLS[i] + (i + 1) * P]
                dve.tensor_tensor(own, own, C("admissible"), ALU.add).then_inc(s_adm, 1)
            dve.wait_ge(s_adm, NB)

            def row(x, i):
                return x[:, SCOLS[i]:SCOLS[i] + (i + 1) * P]

            def top_round(n):
                for i in range(1, NB):
                    if n >= 1:
                        dve.wait_ge(s_top, 6 * (n - 1) + 3 + i)
                    dve.max(top8[:, i, :], row(work if n else score, i)).then_inc(s_top, 1)
                for i in range(1, NB):
                    dve.wait_ge(s_top, 6 * n + i)
                    dve.match_replace(row(work, i), top8[:, i, :], row(work if n else score, i), GONE)\
                        .then_inc(s_top, 1)

            for t in range(18):
                if t >= 2:
                    v = t - 2
                    dve.wait_ge(s_hrot, v + 1)
                    dve.tensor_tensor(qk2[:, v, :], act_t[:, v % 2, :], C("cos"), ALU.mult).then_inc(s_hrope, 1)
                    if v >= 2:
                        dve.wait_ge(s_hrope, 3 * (v - 2) + 3)
                    dve.tensor_tensor(act_t[:, 2 + v % 2, :], ps[:, 6 + v % 2, :], C("sin"), ALU.mult)\
                        .then_inc(s_hrope, 1)
                    dve.wait_ge(s_hrope, 3 * v + 2)
                    dve.tensor_tensor(qk2[:, v, :], qk2[:, v, :], act_t[:, 2 + v % 2, :], ALU.add)\
                        .then_inc(s_hrope, 1)
                if 1 <= t <= 16:
                    v = t - 1
                    gain = vec("attn_q_gain_2" if v < KC else "attn_k_gain_2", 0)
                    dve.wait_ge(s_hroot, v + 1)
                    dve.reciprocal(rbuf[v % 2][:, :], rbuf[v % 2][:, :]).then_inc(s_hn, 1)
                    dve.wait_ge(s_hn, 2 * v + 1)
                    dve.scalar_tensor_tensor(act_t[:, v % 2, :], act_t[:, v % 2, :], gain, rbuf[v % 2][:, :],
                                             ALU.mult, ALU.mult).then_inc(s_hn, 1)
                if t < ROUNDS:
                    top_round(t)
            dve.wait_ge(s_top, 6 * ROUNDS)
            dve.tensor_scalar(bias2[:, P:], work[:, P:], GONE, BIG, ALU.not_equal, ALU.mult).then_inc(s_bias, 1)
            dve.wait_ge(s_bias, 1)

            for st in range(NU2 + 2):
                if 1 <= st <= NU2:
                    u = st - 1
                    o = 2 * (u % 3)
                    dve.wait_ge(s_exp2, 2 * (u + 1))
                    dve.reciprocal(sum2[:, o:o + 2], sum2[:, o:o + 2]).then_inc(s_diag, 1)
                    dve.wait_ge(s_diag, 2 * u + 1)
                    if u >= 2:
                        dve.wait_ge(s_t2, u - 1)
                    dve.tensor_tensor(diag[u % 2], C("ident").unsqueeze(1).to_broadcast([P, 2, P]),
                                      sum2[:, o:o + 2].unsqueeze(2).to_broadcast([P, 2, P]), ALU.mult)\
                        .then_inc(s_diag, 1)
                if st < NU2:
                    u, (pair, i) = st, UNITS2[st]
                    w, o = (i + 1) * P, 2 * (u % 3)
                    dve.wait_ge(s_qk2, u + 1)
                    if u >= 3:
                        dve.wait_ge(s_t2, u - 2)
                    for s in range(2):
                        dve.tensor_tensor_reduce(soft2[u % 3][:, s, 0:w], ps[:, 2 * (u % 2) + s, 0:w], row(bias2, i),
                                                 1.0, GONE, ALU.add, ALU.max, mx2[:, o + s:o + s + 1])\
                            .then_inc(s_mask2, 1)
                    dve.wait_ge(s_mask2, 3 * u + 2)
                    dve.tensor_scalar(nm2[:, o:o + 2], mx2[:, o:o + 2], -HD ** -0.5, None, ALU.mult)\
                        .then_inc(s_mask2, 1)
                if st >= 2:
                    u, (pair, i) = st - 2, UNITS2[st - 2]
                    w = (i + 1) * P
                    dve.wait_ge(s_t2, u + 1)
                    if u >= 2:
                        dve.wait_ge(s_pv2, u - 1)
                    dve.tensor_copy(pt2[u % 2][:, 1, 0:w], ps[:, 5, 0:w]).then_inc(s_tcd, 1)
            residual_dve(dve, 5, e2 + E2_OUT, lambda m: m % 4, lambda m: shift_of(0, 2, m))

        def conv_weight(l, tap, half, p):
            row = l * 3 + tap
            at = (row % 2) * 2 * FC + half * FC
            return vcol[:, 2 + row // 2, bass.ds(p + at, 1)] if not isinstance(p, int) else \
                vcol[:, 2 + row // 2, at + p:at + p + 1]

        def conv_bias(l, half, p):
            at = l * 2 * FC + half * FC
            return vcol[:, 5, bass.ds(p + at, 1)] if not isinstance(p, int) else vcol[:, 5, at + p:at + p + 1]

        def conv_act(act, k):
            e0, p0, l = TILE0[f"ffn{k}"], FC * k, k - 2
            c0 = FC * l

            def base(i, p, loop):
                act.wait_ge(gated, i * 4 + (p0 + p - 1))
                chunk = i * 4 + p if loop else p
                for half in range(2):
                    act.wait_ge(tile_done, i * 8 + (e0 + 2 * p + half + 1))
                    act.activation(act_t[:, 2 * (p % 2) + half, :], ps[:, 2 * (p % 2) + half, :], ACT.Identity,
                                   bias=conv_bias(l, half, chunk), scale=conv_weight(l, 2, half, chunk))\
                        .then_inc(base_tap, 1)

            def silu(i, p):
                act.wait_ge(taps, i * 16 + 4 * (c0 + p + 1))
                g = act_t[:, 2 * (p % 2) + 1, :]
                act.activation(g, g, ACT.Silu).then_inc(silu_done, 1)

            base(0, 0, False)
            base(0, 1, False)
            silu(0, 0)
            with act.Fori(0, 5) as i:
                for p in range(2, 6):
                    base(i, p, True)
                    silu(i, p - 1)
            silu(0, FC - 1)

        def conv_dve(dve, k):
            e0, p0, l = TILE0[f"ffn{k}"], FC * k, k - 2
            c0 = FC * l

            def earlier(i, p, loop):
                chunk = i * 4 + p if loop else p
                for n, (lag, half) in enumerate(((1, 0), (1, 1), (2, 0), (2, 1))):
                    if lag == 1:
                        dve.wait_ge(base_tap, i * 8 + (2 * (c0 + p) + half + 1))
                    else:
                        dve.wait_ge(taps, i * 16 + (4 * (c0 + p) + half + 1))
                    t = act_t[:, 2 * (p % 2) + half, lag:]
                    dve.scalar_tensor_tensor(t, ps[:, 2 * (p % 2) + half, 0:T - lag],
                                             conv_weight(l, 2 - lag, half, chunk), t, ALU.mult, ALU.add)\
                        .then_inc(taps, 1)

            def product(i, p, loop):
                dve.wait_ge(silu_done, i * 4 + (p0 + p + 1))
                dst = gT[:, bass.ds(i * (4 * T) + p * T, T)] if loop else gT[:, p * T:(p + 1) * T]
                dve.tensor_tensor(dst, act_t[:, 2 * (p % 2), :], act_t[:, 2 * (p % 2) + 1, :], ALU.mult)\
                    .then_inc(gated, 1)

            earlier(0, 0, False)
            earlier(0, 1, False)
            product(0, 0, False)
            with dve.Fori(0, 5) as i:
                for p in range(2, 6):
                    earlier(i, p, True)
                    product(i, p - 1, True)
            product(0, FC - 1, False)

        r3 = Region(FC * T)
        BT = [r3.take(KC * P).rearrange("p (c s) -> p c s", c=KC) for _ in range(2)]
        CT = [r3.take(KC * P).rearrange("p (c s) -> p c s", c=KC) for _ in range(3)]
        par = r3.take(4 * PAIRS).rearrange("p (k j) -> p k j", k=4)
        steps = r3.take(T)
        start3 = r3.at
        b_in = [r3.take(PAIRS * 16).rearrange("p (j c) -> p j c", j=PAIRS) for _ in range(2)]
        c_in = [r3.take(KC * HD).rearrange("p (c s) -> p c s", c=KC) for _ in range(2)]
        bz = [r3.take(PAIRS * 32).rearrange("p (j g c) -> p j g c", j=PAIRS, g=2) for _ in range(2)]
        cz_flat = [r3.take(KC * P) for _ in range(2)]
        cz = [x.rearrange("p (c g s) -> p c g s", c=KC, g=2) for x in cz_flat]
        bt = [x[:, 0:PAIRS * 16].rearrange("p (j c) -> p j c", j=PAIRS) for x in cz_flat]
        sm = [r3.take(P)[0:PAIRS] for _ in range(10)]
        (ARE, AIM, DT, DEC, ANG, KK, SIN, COS, T1, T2) = range(10)
        r4 = Region()
        ssm_g = r4.take(KC * T).rearrange("p (c t) -> p c t", c=KC)
        ybuf = r4.take(2 * T).rearrange("p (c t) -> p c t", c=2)
        cosT = [r4.take(T) for _ in range(2)]
        sinT = [r4.take(T) for _ in range(2)]
        frac, near = act_t[:, 0:2, :], act_t[:, 2:4, :]
        zs = r4.take(4 * T).rearrange("p (c t) -> p c t", c=4)
        post = [r4.take(4 * T).rearrange("p (c t) -> p c t", c=4)]
        assert r4.at <= FC * T
        r5 = Region(start3)
        pre = r5.take(8 * T).rearrange("p (c t) -> p c t", c=8)
        post.append(r5.take(4 * T).rearrange("p (c t) -> p c t", c=4))
        cosT.append(r5.take(T))
        sinT.append(r5.take(T))

        s_sin3 = sem("ssm_loaded")
        s_small = sem("ssm_small")
        s_small_a = sem("ssm_small_act")
        s_par = sem("ssm_turned")
        s_parc = sem("ssm_turned_copied")
        s_bz = sem("ssm_matrices")
        s_zero = sem("ssm_zeroed")

        def ssm_loads(sp):
            sp.wait_ge(x_ready, 6 * KC)
            flat = "l (j g) s -> (l j) (g s)"
            sp.dma_start(sm[ARE], a["ssm_a_re_2"].rearrange(flat, g=2)).then_inc(s_sin3, 16)
            sp.dma_start(sm[AIM], a["ssm_a_im_2"].rearrange(flat, g=2)).then_inc(s_sin3, 16)
            sp.dma_start(sm[T1][:, 0:2], a["ssm_log_dt_2"].rearrange("l (j g) -> (l j) g", g=2)).then_inc(s_sin3, 16)
            sp.dma_start(steps, a["steps"]).then_inc(s_sin3, 16)
            for n, name in enumerate(("ssm_b_re_2", "ssm_b_im_2")):
                sp.dma_start(b_in[n], a[name][0].rearrange("(j g) s c -> (g s) j c", g=2)).then_inc(s_sin3, 16)
            for n, name in enumerate(("ssm_c_re_2", "ssm_c_im_2")):
                sp.dma_start(c_in[n], a[name][0].rearrange("(k g) c s -> (g c) k s", g=8)).then_inc(s_sin3, 16)

        def ssm_prepare_act(act):
            act.wait_ge(s_sin3, 16 * 8)
            act.activation(sm[T2][:, 0:2], sm[T1][:, 0:2], ACT.Exp).then_inc(s_small_a, 1)
            act.wait_ge(s_small, 2)
            act.activation(sm[DEC], sm[DEC], ACT.Exp).then_inc(s_small_a, 1)
            act.wait_ge(s_small, 9)
            act.activation(sm[SIN], sm[ANG], ACT.Sin).then_inc(s_small_a, 1)
            act.activation(sm[COS], sm[ANG], ACT.Abs).then_inc(s_small_a, 1)
            act.wait_ge(s_small_a, 4)
            act.activation(sm[COS], sm[COS], ACT.Sin, bias=C("half_pi", PAIRS), scale=-1.0).then_inc(s_small_a, 1)

        def ssm_prepare_dve(dve):
            at = [0]

            def step(ins):
                at[0] += 1
                ins.then_inc(s_small, 1)
                dve.wait_ge(s_small, at[0])

            dve.wait_ge(s_small_a, 1)
            dt = sm[T2][:, 0:2].unsqueeze(2).to_broadcast([PAIRS, 2, HD])

            def by_group(x):
                return x.rearrange("j (g s) -> j g s", g=2)

            step(dve.tensor_copy(by_group(sm[DT]), dt))
            step(dve.tensor_tensor(sm[DEC], sm[ARE], sm[DT], ALU.mult))
            step(dve.tensor_tensor(sm[ANG], sm[AIM], sm[DT], ALU.mult))
            reduce_angle(dve, sm[ANG], sm[KK], s_small, at[0])
            at[0] += 6
            dve.wait_ge(s_small_a, 5)
            step(dve.tensor_tensor(sm[COS], sm[COS], sm[DEC], ALU.mult))
            step(dve.tensor_tensor(sm[SIN], sm[SIN], sm[DEC], ALU.mult))
            step(dve.tensor_scalar(sm[COS], sm[COS], -1.0, None, ALU.add))
            step(dve.tensor_tensor(sm[T1], sm[ARE], sm[ARE], ALU.mult))
            step(dve.tensor_tensor(sm[T2], sm[AIM], sm[AIM], ALU.mult))
            step(dve.tensor_tensor(sm[T1], sm[T1], sm[T2], ALU.add))
            step(dve.reciprocal(sm[KK], sm[T1]))
            step(dve.tensor_tensor(sm[T1], sm[COS], sm[ARE], ALU.mult))
            step(dve.tensor_tensor(sm[T2], sm[SIN], sm[AIM], ALU.mult))
            step(dve.tensor_tensor(sm[T1], sm[T1], sm[T2], ALU.add))
            step(dve.tensor_tensor(sm[DT], sm[T1], sm[KK], ALU.mult))
            step(dve.tensor_tensor(sm[T1], sm[SIN], sm[ARE], ALU.mult))
            step(dve.tensor_tensor(sm[T2], sm[COS], sm[AIM], ALU.mult))
            step(dve.tensor_tensor(sm[T1], sm[T1], sm[T2], ALU.subtract))
            step(dve.tensor_tensor(sm[T2], sm[T1], sm[KK], ALU.mult))
            step(dve.tensor_scalar(sm[ANG], sm[ANG], 1 / (2 * np.pi), None, ALU.mult))
            assert at[0] == SMALL_STEPS

        SMALL_STEPS = 25

        def ssm_prepare_pe(pe, q):
            if q == 0:
                pe.wait_ge(s_small, SMALL_STEPS)
                for k, x in enumerate((DEC, ANG, DT, T2)):
                    mm = pe.transpose(ps[:, 4, k * PAIRS:(k + 1) * PAIRS], sm[x], C("ident", PAIRS)[:, 0:PAIRS])
                mm.then_inc(s_par, 1)
            if q == 3:
                pe.wait_ge(s_bz, 8)
                pe.wait_ge(s_parc, 1)
                for n in range(2):
                    flat = bz[n].rearrange("p j g c -> p (j g c)")
                    for c in range(KC):
                        mm = pe.transpose(ps[:, 4 + 2 * n + c // 4, (c % 4) * P:(c % 4 + 1) * P],
                                          flat[:, c * P:(c + 1) * P], C("ident"))
                    mm.then_inc(s_par, 1)
                pe.wait_ge(s_bz, 12)
                for n in range(2):
                    pe.wait_ge(s_parc, 2 * n + 3)
                    for c in range(KC):
                        mm = pe.transpose(ps[:, 4 + 2 * n + c // 4, (c % 4) * P:(c % 4 + 1) * P],
                                          cz_flat[n][:, c * P:(c + 1) * P], C("ident"))
                    mm.then_inc(s_par, 1)

        def ssm_turned_act(act, first):
            if first:
                act.wait_ge(s_par, 1)
                act.activation(par, ps[:, 4, 0:4 * PAIRS].rearrange("p (k j) -> p k j", k=4), ACT.Copy)\
                    .then_inc(s_parc, 1)
                return
            def both(n):
                return [ps[:, 4 + 2 * n + b, :].rearrange("p (c s) -> p c s", c=4) for b in range(2)]

            for n in range(2):
                act.wait_ge(s_par, 2 + n)
                for b in range(2):
                    act.activation(BT[n][:, 4 * b:4 * b + 4, :], both(n)[b], ACT.Copy).then_inc(s_parc, 1)
            for n in range(2):
                act.wait_ge(s_par, 4 + n)
                for b in range(2):
                    if n == 0:
                        act.activation(CT[0][:, 4 * b:4 * b + 4, :], both(n)[b], ACT.Copy).then_inc(s_parc, 1)
                    act.activation(CT[1 + n][:, 4 * b:4 * b + 4, :], both(n)[b], ACT.Copy, scale=-1.0)\
                        .then_inc(s_parc, 1)

        PARC = 1 + 4 + 4 + 2

        def ssm_matrices_dve(dve):
            cre, cim = (par[:, k, :].unsqueeze(2).to_broadcast([P, PAIRS, 16]) for k in (2, 3))
            dve.wait_ge(s_parc, 1)
            dve.wait_ge(s_zero, 2)
            n = 0
            for out, (x, y), op in ((bz[0], (b_in[0], b_in[1]), ALU.subtract), (bz[1], (b_in[1], b_in[0]), ALU.add)):
                if n:
                    dve.wait_ge(s_bz, n)
                dve.tensor_tensor(bt[0], x, cre, ALU.mult).then_inc(s_bz, 1)
                dve.tensor_tensor(bt[1], y, cim, ALU.mult).then_inc(s_bz, 1)
                dve.wait_ge(s_bz, n + 2)
                for g in range(2):
                    rows_of = slice(g * HD, (g + 1) * HD)
                    dve.tensor_tensor(out[rows_of, :, g, :], bt[0][rows_of], bt[1][rows_of], op).then_inc(s_bz, 1)
                n += 4
            dve.wait_ge(s_bz, 8)
            for k in range(2):
                for g, name in enumerate(("group_even", "group_odd")):
                    dve.tensor_scalar(cz[k][:, :, g, :], c_in[k], C(name), None, ALU.mult).then_inc(s_bz, 1)

        s_bu = sem("ssm_input")
        s_near = sem("ssm_near")
        s_frac = sem("ssm_frac")
        s_tab = sem("ssm_tables")
        s_pre = sem("ssm_rotated")
        s_add = sem("ssm_rotated_sum")
        s_scan = sem("ssm_scanned")
        s_postd = sem("ssm_back_dve")
        s_postp = sem("ssm_back_pool")
        s_y = sem("ssm_output")
        s_yd = sem("ssm_skipped")
        s_g = sem("ssm_gelu")
        s_sig = sem("glu_sigmoid")
        s_glu = sem("glu_product")
        n3, e3 = SLOT0["ssm"], TILE0["ssm"]

        def ssm_glu_loads(sp):
            w = feat(a["ssm_w_glu_2"][0])
            for b in range(4):
                load_slot(sp, n3 + 2 * b, w[:, :, b * WCOL:(b + 1) * WCOL])
                load_slot(sp, n3 + 2 * b + 1, w[:, :, D + b * WCOL:D + (b + 1) * WCOL])

        def ssm_pe(pe):
            pe.wait_ge(s_parc, PARC)
            for j in range(PAIRS + 2):
                if j < PAIRS:
                    c, q = j // 4, j % 4
                    if q == 0:
                        pe.wait_ge(h_ready, h_before(6) + c + 1)
                    if j >= 2:
                        pe.wait_ge(s_pre, 4 * (j - 2) + 4)
                    rows_of = slice(32 * q, 32 * q + 32)
                    for n in range(2):
                        mm = pe.matmul(ps[:, 2 * (j % 2) + n, :], BT[n][rows_of, c, :], hT[rows_of, c, :],
                                       start=True, stop=True)
                    mm.then_inc(s_bu, 1)
                if j >= 2:
                    v = j - 2
                    c, q = v // 4, v % 4
                    if q == 0 and c >= 2:
                        pe.wait_ge(s_yd, c - 1)
                    pe.wait_ge(s_postd, 2 * v + 2)
                    pe.wait_ge(s_postp, 2 * v + 2)
                    out = ps[32 * q:32 * q + 32, 5 + c % 2, :]
                    for n, m in enumerate((0, 1, 2, 2)):
                        mm = pe.matmul(out, CT[m][:, c, 32 * q:32 * q + 32], post[v % 2][:, n, :],
                                       start=(n == 0), stop=(n == 3))
                    mm.then_inc(s_y, 1)
            for b in range(4):
                slot_wait(pe, n3 + 2 * b)
                slot_wait(pe, n3 + 2 * b + 1)
                for j in range(2):
                    p = 2 * b + j
                    if p >= 2:
                        pe.wait_ge(s_glu, p - 1)
                    for w in range(2):
                        for c in range(KC):
                            if p == 0 and w == 0:
                                pe.wait_ge(s_g, c + 1)
                            mm = pe.matmul(ps[:, 2 * (p % 2) + w, :], wtile(n3 + 2 * b + w, c, KC, j * P, (j + 1) * P),
                                           ssm_g[:, c, :], start=(c == 0), stop=(c == KC - 1))
                        mm.then_inc(tile_done, 1)

        TURN = 6.283185

        def ssm_act(act):
            def gelu(c):
                act.wait_ge(s_yd, c + 1)
                act.activation(ssm_g[:, c, :], ybuf[:, c % 2, :], ACT.Gelu_apprx_tanh).then_inc(s_g, 1)

            def nearest(j):
                b = j % 2
                if j >= 2:
                    act.wait_ge(s_tab, 3 * (j - 2) + 3)
                act.activation(near[:, b, :], steps, ACT.Identity, bias=C("magic")[:, 0:1], scale=par[:, 1, j:j + 1])\
                    .then_inc(s_near, 1)
                act.wait_ge(s_near, 2 * j + 1)
                act.activation(near[:, b, :], near[:, b, :], ACT.Identity, bias=C("magic")[:, 1:2])\
                    .then_inc(s_near, 1)

            nearest(0)
            nearest(1)
            for j in range(PAIRS):
                b = j % 2
                act.wait_ge(s_frac, j + 1)
                if j >= 3:
                    act.wait_ge(s_postd, 2 * (j - 3) + 2)
                    act.wait_ge(s_postp, 2 * (j - 3) + 2)
                act.activation(sinT[j % 3], frac[:, b, :], ACT.Sin, scale=TURN).then_inc(s_tab, 1)
                act.activation(near[:, b, :], frac[:, b, :], ACT.Abs).then_inc(s_tab, 1)
                act.wait_ge(s_tab, 3 * j + 2)
                act.activation(cosT[j % 3], near[:, b, :], ACT.Sin, bias=C("half_pi"), scale=-TURN).then_inc(s_tab, 1)
                if j + 2 < PAIRS:
                    nearest(j + 2)
                if j % 4 == 2 and j >= 6:
                    gelu(j // 4 - 1)
            gelu(KC - 1)
            for p in range(KC):
                act.wait_ge(tile_done, e3 + 2 * p + 2)
                if p >= 2:
                    act.wait_ge(s_glu, p - 1)
                act.activation(act_t[:, p % 2, :], ps[:, 2 * (p % 2) + 1, :], ACT.Sigmoid).then_inc(s_sig, 1)
                if p >= 1:
                    square(act, 7, p - 1)
            square(act, 7, KC - 1)

        def ssm_dve(dve):
            def fraction(j):
                b = j % 2
                dve.wait_ge(s_near, 2 * j + 2)
                if j >= 2:
                    dve.wait_ge(s_tab, 3 * (j - 2) + 3)
                dve.scalar_tensor_tensor(frac[:, b, :], steps, par[:, 1, j:j + 1], near[:, b, :], ALU.mult,
                                         ALU.subtract).then_inc(s_frac, 1)

            def rotate_in(j):
                b = j % 2
                dve.wait_ge(s_bu, j + 1)
                dve.wait_ge(s_tab, 3 * j + 3)
                if j >= 2:
                    dve.wait_ge(s_add, 2 * (j - 2) + 2)
                for n, (part, table) in enumerate(((0, cosT), (1, sinT), (1, cosT), (0, sinT))):
                    dve.tensor_tensor(pre[:, 4 * b + n, :], ps[:, 2 * b + part, :], table[j % 3], ALU.mult)\
                        .then_inc(s_pre, 1)

            def scan(j):
                b = j % 2
                decay = par[:, 0, j:j + 1].to_broadcast([P, T])
                for n in range(2):
                    dve.wait_ge(s_add, 2 * j + n + 1)
                    if j >= 2:
                        dve.wait_ge(s_postp, 2 * (j - 2) + 2)
                        dve.wait_ge(s_postd, 2 * (j - 2) + 2)
                    dve.tensor_tensor_scan(zs[:, 2 * b + n, :], decay, pre[:, 4 * b + 2 * n, :], 0.0, ALU.mult,
                                           ALU.add).then_inc(s_scan, 1)

            def rotate_back(j):
                b = j % 2
                dve.wait_ge(s_scan, 2 * j + 2)
                if j >= 2:
                    dve.wait_ge(s_y, j - 1)
                dve.tensor_tensor(post[b][:, 0, :], zs[:, 2 * b, :], cosT[j % 3], ALU.mult).then_inc(s_postd, 1)
                dve.tensor_tensor(post[b][:, 1, :], zs[:, 2 * b + 1, :], sinT[j % 3], ALU.mult).then_inc(s_postd, 1)

            def skip(c):
                dve.wait_ge(s_y, 4 * c + 4)
                if c >= 2:
                    dve.wait_ge(s_g, c - 1)
                dve.scalar_tensor_tensor(ybuf[:, c % 2, :], hT[:, c, :], vec("ssm_d_2", c), ps[:, 5 + c % 2, :],
                                         ALU.mult, ALU.add).then_inc(s_yd, 1)

            dve.wait_ge(s_parc, PARC)
            dve.wait_ge(h_ready, h_before(6) + KC)
            fraction(0)
            fraction(1)
            for j in range(PAIRS + 1):
                if j < PAIRS:
                    rotate_in(j)
                if j >= 1:
                    scan(j - 1)
                if j + 2 < PAIRS:
                    fraction(j + 2)
                if j >= 1:
                    rotate_back(j - 1)
                if j % 4 == 1 and j >= 5:
                    skip(j // 4 - 1)
            skip(KC - 1)
            for p in range(KC):
                dve.wait_ge(s_sig, p + 1)
                dve.tensor_tensor(act_t[:, p % 2, :], ps[:, 2 * (p % 2), :], act_t[:, p % 2, :], ALU.mult)\
                    .then_inc(s_glu, 1)
                dve.wait_ge(s_glu, p + 1)
                dve.scalar_tensor_tensor(xT[:, p, :], act_t[:, p % 2, :], shift_of(1, 2, p), xT[:, p, :], ALU.mult,
                                         ALU.add).then_inc(x_ready, 1)
                if p >= 1:
                    add_square(dve, 7, p - 1)
            add_square(dve, 7, KC - 1)

        def ssm_pool(pool):
            for j in range(PAIRS + 1):
                if j < PAIRS:
                    b = j % 2
                    for n, op in enumerate((ALU.add, ALU.subtract)):
                        pool.wait_ge(s_pre, 4 * j + 2 * n + 2)
                        x = pre[:, 4 * b + 2 * n, :]
                        pool.tensor_tensor(x, x, pre[:, 4 * b + 2 * n + 1, :], op).then_inc(s_add, 1)
                if j >= 1:
                    v, b = j - 1, (j - 1) % 2
                    pool.wait_ge(s_scan, 2 * v + 2)
                    if v >= 2:
                        pool.wait_ge(s_y, v - 1)
                    pool.tensor_tensor(post[b][:, 2, :], zs[:, 2 * b, :], sinT[v % 3], ALU.mult).then_inc(s_postp, 1)
                    pool.tensor_tensor(post[b][:, 3, :], zs[:, 2 * b + 1, :], cosT[v % 3], ALU.mult)\
                        .then_inc(s_postp, 1)

        out_rows = [phase[:, (FC + j) * T:(FC + j + 1) * T].rearrange("p (i d) -> p i d", i=NB) for j in range(2)]

        def out_pe(pe, q):
            for m in () if q == 0 else range(2 * q - 2, 2 * q) if q < 4 else range(6, 8):
                pe.wait_ge(x_ready, 8 * KC + m + 1)
                if m >= 4:
                    pe.wait_ge(s_out_c, m - 3)
                for i in range(NB):
                    mm = pe.transpose(ps[:, 4 + m % 4, i * P:(i + 1) * P], xT[:, m, i * P:(i + 1) * P], C("ident"))
                mm.then_inc(s_out_t, 1)

        def out_act(act):
            for m in range(KC):
                act.wait_ge(s_out_t, m + 1)
                if m >= 2:
                    act.wait_ge(s_out[m % 2], 16 * (m // 2))
                act.activation(out_rows[m % 2], ps[:, 4 + m % 4, :].rearrange("p (i d) -> p i d", i=NB), ACT.Copy)\
                    .then_inc(s_out_c, 1)

        def out_stores(sp):
            dst = out[0].rearrange("(i p) d -> p i d", p=P)
            for m in range(KC):
                sp.wait_ge(s_out_c, m + 1)
                sp.dma_start(dst[:, :, m * P:(m + 1) * P], out_rows[m % 2]).then_inc(s_out[m % 2], 16)
            for j in range(2):
                sp.wait_ge(s_out[j], 16 * KC // 2)


        block = ctx.enter_context(nc.Block())

        def on(stage):
            return stop is None or stage <= stop

        @block.sync
        def _(sp):
            sp.dma_start(const[:, :], a["shape_constants"]).then_inc(s_const, 16)
            loads = []
            for name in ("ffn1_norm", "mix_norm", "ffn2_norm", "norm_mix_2", "norm_ffn_2", "pool_scale",
                         "ssm_d_2", "c_2"):
                src = a[name].rearrange("l (r q) -> (l r) q", q=P)
                loads.append((v_rows[VROWS[name]:VROWS[name] + src.shape[0], 0, :], src))
            src = a["final_norm"].rearrange("(r q) -> r q", q=P)
            loads.append((v_rows[VROWS["final_norm"]:VROWS["final_norm"] + 8, 0, :], src))
            for name in ("attn_q_gain_2", "attn_k_gain_2"):
                for half in range(2):
                    loads.append((v_rows[VROWS[name]:VROWS[name] + 1, 0, half * HD:(half + 1) * HD], a[name]))
            loads.append((v_rows[0:96, 1, :], a["ada_b_2"].rearrange("l (r q) -> (l r) q", q=P)))
            conv = a["ffn_conv_w_2"].rearrange("l k (r q) -> (l k r) q", q=P)
            for j in range(3):
                loads.append((v_rows[0:CONV_ROWS, 2 + j, :], conv[j * CONV_ROWS:(j + 1) * CONV_ROWS, :]))
            loads.append((v_rows[0:CONV_ROWS, 5, :], a["ffn_conv_b_2"].rearrange("l (r q) -> (l r) q", q=P)))
            assert len(loads) == VLOADS
            for i in range(NB):
                sp.dma_start(x_rows[:, i, :], a["x"][0, i * P:(i + 1) * P, :]).then_inc(s_xrows, 16)
            sp.wait_ge(v_cleared, VTILES)
            for dst, src in loads:
                sp.dma_start(dst, src).then_inc(s_vrows, 16)
            sp.dma_start(poolw[:, :, :], a["pool_w"][0].rearrange("g c d -> c g d")).then_inc(s_const, 16)
            ffn_loads(sp, 0, a["ffn1_w1"][0], a["ffn1_w3"][0], a["ffn1_w2"][0], 0)
            if on(1):
                mix1_loads(sp)
                sp.wait_ge(s_merge, 3 * KC)
                sp.dma_start(act_t[:, 3, :].bitcast(I32), a["positions_2"].to_broadcast([P, T])).then_inc(s_pos, 16)
            if on(2):
                ffn_loads(sp, 1, a["ffn2_w1"][0], a["ffn2_w3"][0], a["ffn2_w2"][0], 0)
            if on(3):
                mix2_loads(sp)
            if on(4):
                up = a["ffn_w_up_2"]
                ffn_loads(sp, 2, up[0], up[0], a["ffn_w_down_2"][0], F, before_down=lambda: ssm_loads(sp))
            if on(5):
                ssm_glu_loads(sp)
            if on(6):
                ffn_loads(sp, 3, up[1], up[1], a["ffn_w_down_2"][1], F)
            if stop is None:
                out_stores(sp)
            if stop is not None:
                sp.wait_ge(x_ready, KC * {0: 2, 1: 3, 2: 4, 3: 6, 4: 7, 5: 8}[stop])

        @block.tensor
        def _(pe):
            pe.wait_ge(s_const, 16)
            for m in range(KC):
                if m == 0:
                    pe.wait_ge(s_xrows, 16 * NB)
                if m >= 4:
                    pe.wait_ge(x_ready, m - 3)
                for i in range(NB):
                    mm = pe.transpose(ps[:, m % 4, i * P:(i + 1) * P], x_rows[:, i, m * P:(m + 1) * P],
                                      C("ident"))
                mm.then_inc(x_turned, 1)
            pe.wait_ge(v_cleared, VTILES)
            pe.wait_ge(s_vrows, 16 * VLOADS)
            for j in range(VTILES):
                mm = pe.transpose(ps[:, 5 + j // 4, (j % 4) * P:(j % 4 + 1) * P], v_rows[:, j, :], C("ident"))
            mm.then_inc(s_vbank, 1)
            norm_pe(pe, 0)
            ffn_pe(pe, 0)
            ada_pe(pe)
            norm_pe(pe, 1)
            if on(1):
                mix1_pe(pe)
                norm_pe(pe, 2)
            if on(2):
                ffn_pe(pe, 1)
                norm_pe(pe, 3)
            if on(3):
                norm_pe(pe, 4)
                mix2_pe(pe)
                norm_pe(pe, 5)
            if on(4):
                ffn_pe(pe, 2, lambda q: ssm_prepare_pe(pe, q))
                pe.wait_ge(s_parc, PARC)
                norm_pe(pe, 6)
            if on(5):
                ssm_pe(pe)
                norm_pe(pe, 7)
            if on(6):
                ffn_pe(pe, 3, lambda q: out_pe(pe, q))
                out_pe(pe, 4)

        @block.scalar
        def _(act):
            for m in range(KC):
                square(act, 0, m)
            act.wait_ge(s_vbank, 1)
            act.activation(vcol[:, 0:4, :], ps[:, 5, :].rearrange("p (j d) -> p j d", j=4), ACT.Copy).then_inc(s_vcol, 1)
            act.activation(vcol[:, 4:6, :], ps[:, 6, 0:2 * P].rearrange("p (j d) -> p j d", j=2),
                           ACT.Copy).then_inc(s_vcol, 1)
            act.wait_ge(s_vcol, 2)
            act.activation(cond[:, :], vcol[:, 0, VROWS["c_2"]:VROWS["c_2"] + KC], ACT.Silu).then_inc(cond_done, 1)
            norm_act(act, 0)
            ffn_act(act, 0)
            for m in range(KC):
                square(act, 1, m)
            norm_act(act, 1)
            if on(1):
                mix1_act(act)
                for m in range(KC):
                    square(act, 2, m)
                norm_act(act, 2)
            if on(2):
                tables_act(act)
                ffn_act(act, 1)
                for m in range(KC):
                    square(act, 3, m)
                norm_act(act, 3)
            if on(3):
                for m in range(KC):
                    square(act, 4, m)
                norm_act(act, 4)
                shift_act(act, 4, 0, lambda c: shift_of(0, 0, c))
                mix2_act(act)
                for m in range(KC):
                    square(act, 5, m)
                norm_act(act, 5)
                shift_act(act, 5, KC, lambda c: shift_of(0, 3, c))
            if on(4):
                conv_act(act, 2)
                ssm_prepare_act(act)
                for m in range(KC):
                    square(act, 6, m)
                    if m == 2:
                        ssm_turned_act(act, True)
                ssm_turned_act(act, False)
                norm_act(act, 6)
                shift_act(act, 6, 2 * KC, lambda c: shift_of(1, 0, c))
            if on(5):
                ssm_act(act)
                norm_act(act, 7)
                shift_act(act, 7, 3 * KC, lambda c: shift_of(1, 3, c))
            if on(6):
                conv_act(act, 3)
                out_act(act)

        @block.vector
        def _(dve):
            for m in range(KC):
                dve.wait_ge(x_turned, m + 1)
                dve.tensor_copy(xT[:, m, :], ps[:, m % 4, :]).then_inc(x_ready, 1)
                if m >= 1:
                    add_square(dve, 0, m - 1)
            add_square(dve, 0, KC - 1)
            dve.wait_ge(s_vcol, 2)
            norm_dve(dve, 0, lambda c: vec("ffn1_norm", c))
            ffn_dve(dve, 0)
            residual_dve(dve, 1, TILE0["ffn0"] + 2 * FC, lambda m: m % 4, lambda m: 0.5)
            norm_dve(dve, 1, lambda c: vec("mix_norm", c))
            ada_dve(dve)
            if on(1):
                mix1_dve(dve)
                norm_dve(dve, 2, lambda c: vec("ffn2_norm", c))
            if on(2):
                tables_dve(dve)
                ffn_dve(dve, 1)
                residual_dve(dve, 3, TILE0["ffn1"] + 2 * FC, lambda m: m % 4, lambda m: 0.5)
            if on(3):
                norm_dve(dve, 3, lambda c: vec("final_norm", c), dst=xT, signal=x_ready)
                for m in range(KC):
                    add_square(dve, 4, m)
                norm_dve(dve, 4, lambda c: modg[:, c:c + 1], shifted=True)
                mix2_dve(dve)
                norm_dve(dve, 5, lambda c: modg[:, KC + c:KC + c + 1], shifted=True)
            if on(4):
                conv_dve(dve, 2)
                ssm_prepare_dve(dve)
                residual_dve(dve, 6, TILE0["ffn2"] + 2 * FC, lambda m: m % 4, lambda m: shift_of(0, 5, m),
                             after={3: lambda: ssm_matrices_dve(dve)})
                norm_dve(dve, 6, lambda c: modg[:, 2 * KC + c:2 * KC + c + 1], shifted=True)
            if on(5):
                ssm_dve(dve)
                norm_dve(dve, 7, lambda c: modg[:, 3 * KC + c:3 * KC + c + 1], shifted=True)
            if on(6):
                conv_dve(dve, 3)
                residual_dve(dve, 8, TILE0["ffn3"] + 2 * FC, lambda m: m % 4, lambda m: shift_of(1, 5, m),
                             squares=False)

        @block.gpsimd
        def _(pool):
            for j in range(VTILES):
                pool.memset(v_rows[:, j, :], 0.0).then_inc(v_cleared, 1)
            ada_pool(pool)
            if on(1):
                mix1_pool(pool)
            if on(4):
                pool.wait_ge(x_ready, 6 * KC)
                for k in range(2):
                    pool.memset(bz[k].rearrange("p j g c -> p (j g c)"), 0.0).then_inc(s_zero, 1)
            if on(5):
                ssm_pool(pool)


VLOADS = 8 + 1 + 4 + 1 + 3 + 1


INPUTS = ["x", "ffn1_norm", "ffn1_w1", "ffn1_w3", "ffn1_w2", "mix_norm", "w_in", "w_branch_attn", "w_branch_pool",
          "pool_w", "pool_scale", "w_out", "ffn2_norm", "ffn2_w1", "ffn2_w3", "ffn2_w2", "final_norm", "c_2",
          "positions_2", "ada_w_2", "ada_b_2", "norm_mix_2", "norm_ffn_2", "attn_w_in_2", "attn_q_gain_2",
          "attn_k_gain_2", "attn_w_out_2", "ssm_a_re_2", "ssm_a_im_2", "ssm_log_dt_2", "ssm_b_re_2", "ssm_b_im_2",
          "ssm_c_re_2", "ssm_c_im_2", "ssm_d_2", "ssm_w_glu_2", "ffn_w_up_2", "ffn_conv_w_2", "ffn_conv_b_2",
          "ffn_w_down_2"]


def kernel(**inputs):
    import concourse.bacc as _bacc
    from concourse.bass_utils import run_bass_kernel_spmd as _run

    nc = _bacc.Bacc("TRN2", target_bir_lowering=False, num_devices=1)
    of_shapes = {"shape_constants": SHAPE_CONSTANTS, "steps": STEPS}
    arrays, args = {}, {}
    for name in INPUTS + list(of_shapes):
        x = of_shapes[name] if name in of_shapes else np.ascontiguousarray(inputs[name])
        arrays[f"in_{name}"] = x
        args[name] = nc.dram_tensor(f"in_{name}", x.shape, mybir.dt.from_np(x.dtype), kind="ExternalInput").ap()
    out = nc.dram_tensor("out", (1, T, D), F32, kind="ExternalOutput").ap()
    build(nc, args, out)
    result = _run(nc, [arrays], core_ids=[0])
    return result.results[0]["out"]
```

```python
from contextlib import ExitStack

import numpy as np

import concourse.bass as bass
from concourse import mybir

F32 = mybir.dt.float32
I32 = mybir.dt.int32
ALU = mybir.AluOpType
ACT = mybir.ActivationFunctionType
AX = mybir.AxisListType

P = 128
T = 512
D = 1024
KC = D // P
F = 2816
FC = F // P
NB = T // P
EPS = 1e-6
RING = 4
WCOL = 256
SLOT = (FC // 2) * WCOL

HD = 64
G1, HPG = 3, 4
DILATIONS = (1, 4, 16)
AW = G1 * HPG * HD
QT = AW // P
POOLS = (2, 4, 8, 16)
PAD = 16
H2 = D // HD
IDX = 8
TOPK = min(256, T // 4)
ROUNDS = TOPK // 8
CHUNK = 64
BIG = -1e30
GONE = -3e38
SCOLS = [0, 128, 384, 768]
SALL = 1280
PAIRS = 32

CONST = {}


def shape_constants():
    parts = []

    def add(name, a):
        a = np.asarray(a, np.float32)
        if a.ndim == 1:
            a = a[:, None]
        full = np.zeros((P, a.shape[1]), np.float32)
        full[:a.shape[0]] = a
        start = sum(x.shape[1] for x in parts)
        CONST[name] = (start, start + full.shape[1])
        parts.append(full)

    i = np.arange(P)
    add("ident", np.eye(P))
    add("ones", np.ones((P, P)))
    add("eps", np.full(P, EPS))
    add("head_ones", (i[:, None] // HD == i[None, :] // HD))
    for name, half in (("rot8", 8), ("rot32", 32)):
        r = np.zeros((P, P))
        for p in range(P):
            d = p % HD
            if d < half:
                r[p + half, p] = -1
            elif d < 2 * half:
                r[p - half, p] = 1
        add(name, r)
    pos = np.arange(T, dtype=np.float32)
    inv = (np.float32(500000.0) ** (-np.arange(0, 16, 2, dtype=np.float32) / np.float32(16))).astype(np.float32)
    ang = (pos[:, None] * inv[None, :]).astype(np.float32)
    cos, sin = np.ones((P, T)), np.zeros((P, T))
    for p in range(P):
        if p % HD < 16:
            cos[p] = np.cos(ang[:, p % HD % 8])
            sin[p] = np.sin(ang[:, p % HD % 8])
    add("cos", cos)
    add("sin", sin)
    qi, kj = np.arange(P)[:, None], np.arange(2 * P)[None, :]
    dist = qi + P - kj
    band = (dist >= 0) & (dist <= P)
    first = band & (kj >= P)
    add("mask_band0", np.where(np.concatenate([first, band], 1), 0, BIG))
    add("mask_band1", np.where(np.concatenate([band, band], 1), 0, BIG))
    d = i[:, None] - i[None, :]
    add("mask_step4", np.where(d >= 0, 0, BIG))
    add("mask_step16", np.where((d >= 0) & (d % 4 == 0), 0, BIG))
    sel = np.zeros((HPG, 2, P))
    for h in range(HPG):
        sel[h, h // 2, (h % 2) * HD:(h % 2 + 1) * HD] = 1
    add("pair_select", sel.reshape(HPG, 2 * P))
    cnt = np.zeros((P, len(POOLS), PAD))
    for g, w in enumerate(POOLS):
        cnt[:, g] = (np.float32(1) / np.minimum(np.arange(1, PAD + 1), w).astype(np.float32))[None]
    add("pool_count", cnt.reshape(P, -1))
    add("admissible", np.where((i[:, None] // CHUNK) >= (i[None, :] // CHUNK), 0, BIG))
    add("inv_freq", np.float32(10000.0) ** (-(i % 32).astype(np.float32) / np.float32(32)))
    add("group_even", i // 16 % 2 == 0)
    add("group_odd", i // 16 % 2 == 1)
    add("half_pi", np.full(P, np.pi / 2))
    add("magic", np.broadcast_to([12582912.0, -12582912.0], (P, 2)))
    return np.concatenate(parts, 1)


SHAPE_CONSTANTS = shape_constants()
NCONST = SHAPE_CONSTANTS.shape[1]
FIRST_CONST = CONST["eps"][1]
STEPS = np.broadcast_to(np.arange(2, T + 1, 2), (P, T // 2)).astype(np.float32)

VROWS = {}
VTILES = 6


def vector_rows():
    at = 0
    for name, n in (("ffn1_norm", 8), ("mix_norm", 8), ("ffn2_norm", 8), ("final_norm", 8), ("norm_mix_2", 16),
                    ("norm_ffn_2", 16), ("pool_scale", 4), ("ssm_d_2", 8), ("c_2", 8), ("attn_q_gain_2", 1),
                    ("attn_k_gain_2", 1)):
        VROWS[name] = at
        at += n
    VROWS["ada_b_2"] = P
    VROWS["ffn_conv_w_2"] = 2 * P
    VROWS["ffn_conv_b_2"] = 5 * P
    return at


VFIRST = vector_rows()
CONV_ROWS = 88

FFN_SLOTS, FFN_TILES = 2 * (FC // 2) + 8, 2 * FC + KC
M1_SLOTS, M1_TILES = 6 + 3 + 8 + 2 + 3 + 4, 12 + 12 + 16 + 4 + 16 + 8
M2_SLOTS, M2_TILES = 2 + 1 + 8 + 4 + 4, 4 + 1 + 1 + 16 + 16 + 8
SSM_SLOTS, SSM_TILES = 8, 16
_order = [("ffn0", FFN_SLOTS, FFN_TILES), ("mix1", M1_SLOTS, M1_TILES), ("ffn1", FFN_SLOTS, FFN_TILES),
          ("mix2", M2_SLOTS, M2_TILES), ("ffn2", FFN_SLOTS, FFN_TILES), ("ssm", SSM_SLOTS, SSM_TILES),
          ("ffn3", FFN_SLOTS, FFN_TILES)]
SLOT0, TILE0 = {}, {}
_n = _e = 0
for _name, _s, _t in _order:
    SLOT0[_name], TILE0[_name] = _n, _e
    _n += _s
    _e += _t
NSLOTS = _n
NORM_OF_FFN = (0, 2, 5, 7)
STAGES = ("ffn0", "mix1", "ffn1", "mix2", "ffn2", "ssm", "ffn3")


def slot_frees():
    frees = {}

    def put(n, e):
        frees[n] = e

    for k in range(4):
        n, e = SLOT0[f"ffn{k}"], TILE0[f"ffn{k}"]
        for b in range(FC // 2):
            put(n + 2 * b, e + 4 * b + 3)
            put(n + 2 * b + 1, e + 4 * b + 4)
        n, e = n + FC, e + 2 * FC
        for q in range(4):
            put(n + 2 * q, e + 2 * q + 1)
            put(n + 2 * q + 1, e + 2 * q + 2)
    n, e = SLOT0["mix1"], TILE0["mix1"]
    for s in range(6):
        put(n + s, e + 2 * s + 2)
    n, e = n + 6, e + 12
    for s in range(3):
        put(n + s, e + 4 * s + 4)
    n, e = n + 3, e + 12
    for s in range(8 + 2):
        put(n + s, e + 2 * s + 2)
    n, e = n + 10, e + 20
    for s in range(3):
        put(n + s, e + 16)
    n, e = n + 3, e + 16
    for s in range(4):
        put(n + s, e + 2 * s + 2)
    n, e = SLOT0["mix2"], TILE0["mix2"]
    put(n, e + 2)
    put(n + 1, e + 4)
    put(n + 2, e + 6)
    n, e = n + 3, e + 6
    for s in range(8):
        put(n + s, e + 2 * s + 2)
    n, e = n + 8, e + 16
    for s in range(4):
        put(n + s, e + 4 * s + 4)
    n, e = n + 4, e + 16
    for s in range(4):
        put(n + s, e + 2 * s + 2)
    n, e = SLOT0["ssm"], TILE0["ssm"]
    for b in range(4):
        put(n + 2 * b, e + 4 * b + 3)
        put(n + 2 * b + 1, e + 4 * b + 4)
    return frees


FREES = slot_frees()


def attention_units():
    units = []
    for hp in range(2):
        for h in (2 * hp, 2 * hp + 1):
            units += [(0, h, 0), (0, h, 1)]
        for g in (1, 2):
            units += [(g, 2 * hp, 0), (g, 2 * hp + 1, 0)]
    return units


UNITS = attention_units()


def build(nc, a, out, stop=None):
    ctx = ExitStack()
    with ctx:
        def sb(name, shape, dt=F32):
            return ctx.enter_context(nc.sbuf_tensor(name, shape, dt))

        def sem(name):
            return ctx.enter_context(nc.semaphore(name))

        xT = sb("xT", [P, KC, T])
        hT = sb("hT", [P, KC, T])
        ring = sb("ring", [P, RING, SLOT])
        const = sb("const", [P, NCONST])
        vcol = sb("vcol", [P, VTILES, P])
        mod = sb("mod", [P, 96])
        modg = sb("modg", [P, 32])
        poolw = sb("poolw", [P, 4, P])
        acc = sb("acc", [P, T])
        sq = sb("sq", [P, 2, T])
        rs = sb("rs", [P, T])
        norm_small = sb("norm_small", [P, 6 * NB])
        gains2 = sb("gains2", [P, KC])
        act_t = sb("act_t", [P, 4, T])
        phase = sb("phase", [P, 24576])
        ps = ctx.enter_context(nc.psum_tensor("ps", [P, 8, T], F32))

        def C(name, rows=P):
            lo, hi = CONST[name]
            return const[0:rows, lo:hi]

        def vec(name, k):
            row = VROWS[name] + k
            if name == "ffn_conv_w_2":
                row = VROWS[name] + P * (k // CONV_ROWS) + k % CONV_ROWS
            return vcol[:, row // P, row % P:row % P + 1]

        def small(name):
            k = ("mean", "root", "rinv", "mean2", "root2", "rinv2").index(name)
            return norm_small[:, k * NB:(k + 1) * NB]

        sq2, acc2 = act_t[:, 0:2, :], act_t[:, 2, :]

        class Region:

            def __init__(self, start=0):
                self.at = start

            def take(self, n):
                self.at += n
                assert self.at <= 24576, self.at
                return phase[:, self.at - n:self.at]

        gT = phase[:, 0:FC * T]
        x_rows = phase[:, 0:NB * D].rearrange("p (i d) -> p i d", i=NB)
        v_rows = phase[:, NB * D:NB * D + VTILES * P].rearrange("p (i d) -> p i d", i=VTILES)
        ada_acc = phase[:, FC * T:FC * T + 12 * D].rearrange("p (j d) -> p j d", j=12)
        ada_slab = [phase[:, 24576 - D:], act_t[:, 2:4, :].rearrange("p j t -> p (j t)")]
        cond = sb("cond", [P, KC])

        r = Region()
        qk1 = r.take(12 * T).rearrange("p (j t) -> p j t", j=12)
        gates = r.take(16 * T).rearrange("p (j t) -> p j t", j=16)
        v1 = r.take(12 * 256).rearrange("p (j t) -> p j t", j=12)
        og1 = r.take(6 * T).rearrange("p (j t) -> p j t", j=6)
        s1 = r.take(2 * T).rearrange("p (j t) -> p j t", j=2)
        pt1 = r.take(2 * T).rearrange("p (j t) -> p j t", j=2)
        mst = r.take(48).rearrange("p (j t) -> p j t", j=12)
        lst = r.take(48).rearrange("p (j t) -> p j t", j=12)
        z = Region()
        merged = z.take(8 * T).rearrange("p (j t) -> p j t", j=8)
        attnT = z.take(2 * T).rearrange("p (j t) -> p j t", j=2)
        rows = merged[0:HPG]
        pool_x = [v1.rearrange("p j t -> p (j t)")[:, g * (PAD + T):(g + 1) * (PAD + T)] for g in range(4)]
        pool_s = [v1.rearrange("p j t -> p (j t)")[:, 4 * (PAD + T):5 * (PAD + T)],
                  s1.rearrange("p j t -> p (j t)")[:, 0:PAD + T]]

        s_const = sem("const_loaded")
        s_late = sem("late_const_loaded")
        s_vrows = sem("vector_rows_loaded")
        s_vbank = sem("vectors_turned")
        s_vcol = sem("vector_columns")
        s_xrows = [sem(f"x_loaded{i}") for i in range(KC // 2)]
        w_loaded = [sem(f"w_loaded{i}") for i in range(RING)]
        tile_done = sem("tile_done")
        x_turned = sem("x_turned")
        v_cleared = sem("vector_rows_cleared")
        x_ready = sem("x_ready")
        sq_ready = sem("sq_ready")
        sq_added = sem("sq_added")
        sum_done = sem("sum_done")
        root_done = sem("root_done")
        rinv_done = sem("rinv_done")
        spread_done = sem("spread_done")
        sq2_ready = sem("sq2_ready")
        sq2_added = sem("sq2_added")
        gains2_done = sem("gains2_done")
        h_scaled = sem("h_scaled")
        h_ready = sem("h_ready")
        silu_done = sem("silu_done")
        gated = sem("gated")
        slab_loaded = [sem(f"slab_loaded{i}") for i in range(2)]
        cond_done = sem("cond_done")
        ada_step = sem("ada_step")
        ada_sum = sem("ada_sum")
        mod_done = sem("mod_done")
        evac1 = sem("proj1_evacuated")
        rot_done = sem("rot_done")
        roped = sem("roped")
        s_scores = sem("scores1")
        s_soft = sem("soft1")
        s_sum = sem("sum1")
        s_gate = sem("gates1")
        s_exp = sem("exp1")
        s_pt = sem("turned1")
        s_ptc = sem("turned1_copied")
        s_pv = sem("pv1")
        s_og = sem("outputs1")
        s_strow = sem("stat_rows")
        s_stc = sem("stat_rows_copied")
        s_w = sem("weights1")
        s_wexp = sem("weights1_exp")
        s_wb = sem("weights1_spread")
        s_mix = sem("mixed1")
        s_pool = sem("pool_steps")
        s_py = sem("pool_done")
        s_pyc = sem("pool_scaled")
        s_merge = sem("merged")
        s_out_t = sem("out_turned")
        s_out_c = sem("out_copied")
        s_out = [sem(f"out_stored{j}") for j in range(2)]

        def feat(w):
            return w.rearrange("(c p) n -> p c n", p=P)

        def slot_wait(pe, n):
            pe.wait_ge(w_loaded[n % RING], 16 * (n // RING + 1))

        def load_slot(sp, n, src, dst_cols=None):
            if n >= RING:
                sp.wait_ge(tile_done, FREES[n - RING])
            _, c, w = src.shape
            dst = ring[:, n % RING, 0:c * w].rearrange("p (c w) -> p c w", c=c)
            sp.dma_start(dst, src).then_inc(w_loaded[n % RING], 16)

        def ffn_loads(sp, k, wa, wb, wd, b_off, before_down=None):
            n0, e0 = SLOT0[f"ffn{k}"], TILE0[f"ffn{k}"]
            wa, wb, wd = feat(wa), feat(wb), feat(wd)

            def up(b):
                load_slot(sp, n0 + 2 * b, wa[:, :, b * WCOL:(b + 1) * WCOL])
                load_slot(sp, n0 + 2 * b + 1, wb[:, :, b_off + b * WCOL:b_off + (b + 1) * WCOL])

            for b in range(3):
                up(b)
            with sp.Fori(0, 4) as i:
                for j in range(4):
                    n = n0 + 6 + j
                    w, off = (wa, 0) if j % 2 == 0 else (wb, b_off)
                    sp.wait_ge(tile_done, i * 8 + FREES[n - RING])
                    src = w[:, :, bass.ds(i * (2 * WCOL) + (off + (3 + j // 2) * WCOL), WCOL)]
                    dst = ring[:, n % RING, 0:KC * WCOL].rearrange("p (c w) -> p c w", c=KC)
                    sp.dma_start(dst, src).then_inc(w_loaded[n % RING], 16)
            if before_down is not None:
                before_down()
            for q in range(4):
                for s in range(2):
                    load_slot(sp, n0 + FC + 2 * q + s,
                              wd[:, s * (FC // 2):(s + 1) * (FC // 2), q * WCOL:(q + 1) * WCOL])

        def wtile(n, c, chunks, lo, hi):
            width = {KC: WCOL, FC // 2: WCOL}[chunks]
            return ring[:, n % RING, c * width + lo:c * width + hi]

        def h_before(norm):
            return KC * (norm - (norm > 3))

        def ffn_pe(pe, k, after_half=None):
            n0, e0 = SLOT0[f"ffn{k}"], TILE0[f"ffn{k}"]
            norm = NORM_OF_FFN[k]
            p0 = FC * k

            def pair(nb, j, bank, first):
                for w in range(2):
                    if first and w == 1:
                        slot_wait(pe, nb + 1)
                    for c in range(KC):
                        if first and w == 0:
                            pe.wait_ge(h_ready, h_before(norm) + c + 1)
                        mm = pe.matmul(ps[:, bank + w, :], wtile(nb + w, c, KC, j * P, (j + 1) * P),
                                       hT[:, c, :], start=(c == 0), stop=(c == KC - 1))
                    mm.then_inc(tile_done, 1)

            slot_wait(pe, n0)
            pair(n0, 0, 0, True)
            pair(n0, 1, 2, False)
            with pe.Fori(0, 5) as i:
                for b in range(2):
                    nb = n0 + 2 + 2 * b
                    for w in range(2):
                        pe.wait_ge(w_loaded[(nb + w) % RING], i * 16 + 16 * ((nb + w) // RING + 1))
                    for j in range(2):
                        pr = p0 + 2 + 2 * b + j
                        if k < 2:
                            pe.wait_ge(silu_done, i * 4 + (pr - 1))
                            pe.wait_ge(gated, i * 4 + (pr - 1))
                        else:
                            pe.wait_ge(taps, i * 16 + 4 * (pr - 2 * FC - 1))
                        pair(nb, j, 2 * j, False)
            nd = n0 + FC
            for q in range(4):
                for s in range(2):
                    slot_wait(pe, nd + 2 * q + s)
                    for t in range(2):
                        m = 2 * q + t
                        if s == 0:
                            if q == 0 and t == 0:
                                if k < 2:
                                    pe.wait_ge(gated, p0 + FC - 1)
                                else:
                                    pe.wait_ge(taps, 4 * (p0 - 2 * FC + FC - 1))
                                    pe.wait_ge(gated, p0 + FC - 3)
                            if q >= 2:
                                pe.wait_ge(x_ready, KC * (norm + 1) + m - 3)
                        for c in range(FC // 2):
                            f = s * (FC // 2) + c
                            if q == 0 and t == 0 and f >= FC - 3:
                                pe.wait_ge(gated, p0 + f + 1)
                            mm = pe.matmul(ps[:, (q % 2) * 2 + t, :],
                                           wtile(nd + 2 * q + s, c, FC // 2, t * P, (t + 1) * P),
                                           gT[:, f * T:(f + 1) * T], start=(f == 0), stop=(f == FC - 1))
                        if s == 1:
                            mm.then_inc(tile_done, 1)
                    if after_half is not None:
                        after_half(q, s)

        def ffn_act(act, k):
            e0, p0 = TILE0[f"ffn{k}"], FC * k

            def one(i, p):
                act.wait_ge(tile_done, i * 8 + (e0 + 2 * p + 1))
                if p0 + p >= 2:
                    act.wait_ge(gated, i * 4 + (p0 + p - 1))
                act.activation(act_t[:, p % 2, :], ps[:, 2 * (p % 2), :], ACT.Silu).then_inc(silu_done, 1)

            one(0, 0)
            one(0, 1)
            with act.Fori(0, 5) as i:
                for p in range(2, 6):
                    one(i, p)

        def ffn_dve(dve, k):
            e0, p0 = TILE0[f"ffn{k}"], FC * k

            def one(i, p, loop):
                dve.wait_ge(silu_done, i * 4 + (p0 + p + 1))
                dve.wait_ge(tile_done, i * 8 + (e0 + 2 * p + 2))
                dst = gT[:, bass.ds(i * (4 * T) + p * T, T)] if loop else gT[:, p * T:(p + 1) * T]
                dve.tensor_tensor(dst, act_t[:, p % 2, :], ps[:, 2 * (p % 2) + 1, :], ALU.mult).then_inc(gated, 1)

            one(0, 0, False)
            one(0, 1, False)
            with dve.Fori(0, 5) as i:
                for p in range(2, 6):
                    one(i, p, True)

        def nth(n):
            return n if n < 4 else n - 1

        def square(act, n, m):
            o = nth(n)
            act.wait_ge(x_ready, KC * n + m + 1)
            if m >= 2:
                act.wait_ge(sq_added, (KC - 1) * o + m - 1)
            elif o:
                act.wait_ge(*((sq_added, (KC - 1) * o) if m == 0 else (sum_done, o)))
            act.activation(sq[:, m % 2, :], xT[:, m, :], ACT.Square).then_inc(sq_ready, 1)

        def add_square(dve, n, m):
            if m == KC - 1:
                return
            o = nth(n)
            dve.wait_ge(sq_ready, KC * o + m + 1)
            if m == 0:
                if o:
                    dve.wait_ge(sum_done, o)
                    dve.wait_ge(sq_added, (KC - 1) * o)
                dve.tensor_copy(acc[:, :], sq[:, 0, :]).then_inc(sq_added, 1)
            else:
                dve.wait_ge(sq_added, (KC - 1) * o + m)
                dve.tensor_tensor(acc[:, :], acc[:, :], sq[:, m % 2, :], ALU.add).then_inc(sq_added, 1)

        def residual_dve(dve, n, tile, bank_of, factor, after=None, squares=True):
            for m in range(KC):
                dve.wait_ge(tile_done, tile + m + 1)
                dve.scalar_tensor_tensor(xT[:, m, :], ps[:, bank_of(m), :], factor(m), xT[:, m, :],
                                         ALU.mult, ALU.add).then_inc(x_ready, 1)
                if m >= 1 and squares:
                    add_square(dve, n, m - 1)
                if after is not None and m in after:
                    after[m]()
            if squares:
                add_square(dve, n, KC - 1)

        WARM_COLS = 128
        WARM = (0, 3, 3, 1)
        NORM_BANK = 4

        def sum_columns(pe, src, at):
            for i in range(NB):
                mm = pe.matmul(ps[:, NORM_BANK, at + i:at + i + 1], src[:, i * P:(i + 1) * P], C("ones")[:, 0:1],
                               start=True, stop=True)
            return mm

        def keep_warm(pe, bank, count):
            for _ in range(count):
                pe.matmul(ps[:, bank, P:P + WARM_COLS], C("ones"), const[:, 0:WARM_COLS], start=True, stop=True)

        def norm_sums_pe(pe, n):
            o = nth(n)
            pe.wait_ge(sq_added, (KC - 1) * (o + 1))
            sum_columns(pe, acc, 0)
            if n == 3:
                pe.wait_ge(sq2_added, KC - 1)
                sum_columns(pe, acc2, 2 * NB)
            keep_warm(pe, NORM_BANK, WARM[0])
            pe.wait_ge(sq_ready, KC * (o + 1))
            mm = sum_columns(pe, sq[:, (KC - 1) % 2, :], NB)
            if n == 3:
                pe.wait_ge(sq2_ready, KC)
                mm = sum_columns(pe, sq2[:, (KC - 1) % 2, :], 3 * NB)
            mm.then_inc(sum_done, 1)

        def norm_pe(pe, n):
            if n == 0:
                pe.wait_ge(s_vcol, 2)
            norm_sums_pe(pe, n)
            keep_warm(pe, NORM_BANK + 1, WARM[1])
            pe.wait_ge(rinv_done, RINV[nth(n)])
            pe.matmul(ps[:, NORM_BANK + 1, :], C("ones"), rs[:, :], start=True, stop=True).then_inc(spread_done, 1)
            keep_warm(pe, NORM_BANK, WARM[2] if n in (5, 6, 7) else WARM[3])

        def norm_act(act, n):
            act.wait_ge(rinv_done, RINV[nth(n)] - 2)
            act.activation(small("root"), small("mean"), ACT.Sqrt, bias=C("eps"), scale=1.0 / D)\
                .then_inc(root_done, 1)

        def spread_dve(dve, dst, x):
            return dve.tensor_tensor(dst[:, :].rearrange("p (i t) -> p i t", i=NB),
                                     C("ident").unsqueeze(1).to_broadcast([P, NB, P]),
                                     small(x).unsqueeze(2).to_broadcast([P, NB, P]), ALU.mult)

        def total_dve(dve, dst, at):
            return dve.tensor_reduce(small(dst), ps[:, NORM_BANK, at:at + 2 * NB].rearrange("p (s i) -> p i s", s=2),
                                     mybir.AxisListType.X, ALU.add)

        def norm_dve(dve, n, gain, shifted=False, by_parity=False):

            def from_natural(x):
                return x.rearrange("p (k r) -> p r k", r=2) if by_parity else x

            def to_order(x):
                return x.rearrange("p (r k) -> p r k", r=2) if by_parity else x

            signal = h_scaled if shifted else h_ready
            o, r = nth(n), RINV[nth(n)]
            dve.wait_ge(sum_done, o + 1)
            total_dve(dve, "mean", 0).then_inc(rinv_done, 1)
            dve.wait_ge(root_done, ROOTS[o])
            dve.reciprocal(small("rinv"), small("root")).then_inc(rinv_done, 1)
            dve.wait_ge(rinv_done, r - 1)
            if o:
                dve.wait_ge(spread_done, SPREADS[o] - 1)
            spread_dve(dve, rs, "rinv").then_inc(rinv_done, 1)
            dve.wait_ge(spread_done, SPREADS[o])
            for c in range(KC):
                dve.scalar_tensor_tensor(to_order(hT[:, c, :]), from_natural(xT[:, c, :]), gain(c),
                                         from_natural(ps[:, NORM_BANK + 1, :]), ALU.mult, ALU.mult)\
                    .then_inc(signal, 1)

        def square_final(act, m):
            if m == 0:
                act.wait_ge(gated, 2 * FC)
            if m >= 2:
                act.wait_ge(sq2_added, m - 1)
            act.activation(sq2[:, m % 2, :], xT[:, m, :], ACT.Square, scale=vec("final_norm", m))\
                .then_inc(sq2_ready, 1)

        def add_square_final(dve, m):
            dve.wait_ge(sq2_ready, m + 1)
            if m == 0:
                dve.tensor_copy(acc2, sq2[:, 0, :]).then_inc(sq2_added, 1)
            else:
                dve.wait_ge(sq2_added, m)
                dve.tensor_tensor(acc2, acc2, sq2[:, m % 2, :], ALU.add).then_inc(sq2_added, 1)

        def norms_pe(pe):
            norm_sums_pe(pe, 3)
            keep_warm(pe, NORM_BANK + 1, 2 * WARM[1])
            pe.wait_ge(rinv_done, RINV[3] - 1)
            pe.matmul(ps[:, NORM_BANK + 1, :], C("ones"), rs[:, :], start=True, stop=True).then_inc(spread_done, 1)
            pe.wait_ge(rinv_done, RINV[3])
            pe.matmul(ps[:, NORM_BANK + 3, :], C("ones"), acc[:, :], start=True, stop=True).then_inc(spread_done, 1)

        def norms_act(act):
            act.wait_ge(rinv_done, RINV[2] + 2)
            act.activation(small("root"), small("mean"), ACT.Sqrt, bias=C("eps"), scale=1.0 / D)\
                .then_inc(root_done, 1)
            act.wait_ge(rinv_done, RINV[2] + 5)
            act.activation(small("root2"), small("mean2"), ACT.Sqrt, bias=C("eps"), scale=1.0 / D)\
                .then_inc(root_done, 1)

        def norms_dve(dve):
            at = [RINV[2]]

            def step(ins):
                at[0] += 1
                ins.then_inc(rinv_done, 1)
                dve.wait_ge(rinv_done, at[0])

            dve.wait_ge(sum_done, 4)
            total_dve(dve, "mean2", 2 * NB).then_inc(rinv_done, 1)
            total_dve(dve, "mean", 0).then_inc(rinv_done, 1)
            at[0] += 2
            dve.wait_ge(root_done, 4)
            step(dve.reciprocal(small("rinv"), small("root")))
            step(dve.tensor_tensor(small("mean2"), small("mean2"), small("rinv"), ALU.mult))
            step(dve.tensor_tensor(small("mean2"), small("mean2"), small("rinv"), ALU.mult))
            dve.tensor_tensor(gains2[:, :], vcol[:, VROWS["final_norm"] // P, VROWS["final_norm"] % P:][:, 0:KC],
                              modg[:, 0:KC], ALU.mult).then_inc(gains2_done, 1)
            dve.wait_ge(root_done, 5)
            step(dve.reciprocal(small("rinv2"), small("root2")))
            step(dve.tensor_tensor(small("rinv2"), small("rinv2"), small("rinv"), ALU.mult))
            step(spread_dve(dve, rs, "rinv2"))
            step(spread_dve(dve, acc, "rinv"))
            assert at[0] == RINV[3]
            dve.wait_ge(gains2_done, 1)
            dve.wait_ge(spread_done, 4)
            for c in range(KC):
                dve.scalar_tensor_tensor(hT[:, c, :], xT[:, c, :], gains2[:, c:c + 1], ps[:, NORM_BANK + 1, :],
                                         ALU.mult, ALU.mult).then_inc(h_scaled, 1)
            dve.wait_ge(spread_done, 5)
            for c in range(KC):
                dve.scalar_tensor_tensor(xT[:, c, :], xT[:, c, :], vec("final_norm", c), ps[:, NORM_BANK + 3, :],
                                         ALU.mult, ALU.mult).then_inc(x_ready, 1)

        RINV = [3, 6, 9, 18, 21, 24, 27]
        ROOTS = [1, 2, 3, 5, 6, 7, 8]
        SPREADS = [1, 2, 3, 5, 6, 7, 8]

        def shift_act(act, n, first, shift, after=None):
            for c in range(KC):
                act.wait_ge(h_scaled, first + c + 1)
                act.activation(hT[:, c, :], hT[:, c, :], ACT.Identity, bias=shift(c)).then_inc(h_ready, 1)
                if after is not None:
                    after(c)

        taps = sem("conv_taps")
        base_tap = sem("conv_base")

        ADA_STEPS = 15

        def ada_pool(pool):
            w = a["ada_w_2"]

            def load(s):
                j, c = s // KC, s % KC
                pool.dma_start(ada_slab[s % 2], w[j // 6, c * P:(c + 1) * P, (j % 6) * D:(j % 6 + 1) * D])\
                    .then_inc(slab_loaded[s % 2], 16)

            load(0)
            load(1)
            pool.wait_ge(cond_done, 1)
            pool.wait_ge(x_ready, KC)
            pool.wait_ge(s_vcol, 2)
            for s in range(12 * KC):
                j, c = s // KC, s % KC
                base = ADA_STEPS * j
                scaled = base + (1 if c == 0 else 2 * c)
                slab = ada_slab[s % 2]
                pool.wait_ge(slab_loaded[s % 2], 16 * (s // 2 + 1))
                pool.tensor_scalar(slab, slab, cond[:, c:c + 1], 0.0, ALU.mult, ALU.add).then_inc(ada_step, 1)
                if c == 0:
                    continue
                pool.wait_ge(ada_step, scaled)
                before = ada_slab[0] if c == 1 else ada_acc[:, j, :]
                pool.tensor_tensor(ada_acc[:, j, :], before, slab, ALU.add).then_inc(ada_step, 1)
                pool.wait_ge(ada_step, scaled + 1)
                for nxt in ((s + 1, s + 2) if c == 1 else (s + 2,)):
                    if nxt < 12 * KC:
                        load(nxt)

        def ada_pe(pe):
            for j in range(12):
                pe.wait_ge(ada_step, ADA_STEPS * (j + 1))
                for m in range(KC):
                    mm = pe.matmul(ps[:, 7, j * KC + m:j * KC + m + 1], ada_acc[:, j, m * P:(m + 1) * P],
                                   C("ones")[:, 0:1], start=True, stop=True)
            mm.then_inc(ada_sum, 1)

        def ada_dve(dve):
            dve.wait_ge(ada_sum, 1)
            dve.tensor_tensor(mod[:, :], ps[:, 7, 0:96], vcol[:, 1, 0:96], ALU.add).then_inc(mod_done, 1)
            dve.wait_ge(mod_done, 1)
            for l in range(2):
                for part, name in ((1, "norm_mix_2"), (4, "norm_ffn_2")):
                    row = VROWS[name] + KC * l
                    dve.scalar_tensor_tensor(modg[:, KC * (2 * l + part // 4):KC * (2 * l + part // 4 + 1)],
                                             mod[:, (6 * l + part) * KC:(6 * l + part + 1) * KC], 1.0,
                                             vcol[:, 0, row:row + KC], ALU.add, ALU.mult).then_inc(mod_done, 1)

        def shift_of(l, part, c):
            at = (6 * l + part) * KC + c
            return mod[:, at:at + 1]

        e1, n1 = TILE0["mix1"], SLOT0["mix1"]
        E_V, E_GATE, E_PZ, E_BR, E_OUT1 = 12, 24, 40, 44, 60
        NU = len(UNITS)

        def mix1_loads(sp):
            w = feat(a["w_in"][0])
            for s in range(6 + 3):
                load_slot(sp, n1 + s, w[:, :, s * WCOL:(s + 1) * WCOL])
            gate0, pool0 = 3 * AW + 4 * P, 3 * AW
            for s in range(8):
                load_slot(sp, n1 + 9 + s, w[:, :, gate0 + s * WCOL:gate0 + (s + 1) * WCOL])
            for s in range(2):
                load_slot(sp, n1 + 17 + s, w[:, :, pool0 + s * WCOL:pool0 + (s + 1) * WCOL])
            load_slot(sp, n1 + 19, feat(a["w_branch_attn"][0]))
            wp = feat(a["w_branch_pool"][0])
            for s in range(2):
                load_slot(sp, n1 + 20 + s, wp[:, 2 * s:2 * s + 2, :])
            wo = feat(a["w_out"][0])
            for s in range(4):
                load_slot(sp, n1 + 22 + s, wo[:, :, s * WCOL:(s + 1) * WCOL])

        def head1(base, g, h):
            hh = g * HPG + h
            return qk1[(hh % 2) * HD:(hh % 2 + 1) * HD, base + hh // 2, :]

        def mix1_pe(pe):
            def gemm(out, n, t, src, chunks=KC, first=None):
                for c in range(chunks):
                    if first is not None:
                        first(c)
                    mm = pe.matmul(out, wtile(n, c, KC, t * P, (t + 1) * P), src(c),
                                   start=(c == 0), stop=(c == chunks - 1))
                mm.then_inc(tile_done, 1)

            def rotate(t):
                pe.wait_ge(evac1, t + 1)
                if t >= 2:
                    pe.wait_ge(roped, 3 * (t - 2) + 2)
                pe.matmul(ps[:, 5 + t % 2, :], C("rot8"), act_t[:, t % 2, :], start=True, stop=True)\
                    .then_inc(rot_done, 1)

            for t in range(12):
                if t % 2 == 0:
                    slot_wait(pe, n1 + t // 2)
                if t >= 4:
                    pe.wait_ge(evac1, t - 3)
                gemm(ps[:, t % 4, :], n1 + t // 2, t % 2, lambda c: hT[:, c, :],
                     first=(lambda c: pe.wait_ge(h_ready, KC + c + 1)) if t == 0 else None)
                if t >= 1:
                    rotate(t - 1)
            for k in range(12):
                g, i = k // 4, k % 4
                if i == 0:
                    slot_wait(pe, n1 + 6 + g)
                pe.wait_ge(evac1, E_V + k - 3)
                tok = slice(i * P, (i + 1) * P) if g == 0 else slice(i, T, 4)
                for c in range(KC):
                    mm = pe.matmul(ps[:, k % 4, 0:256], hT[:, c, tok], wtile(n1 + 6 + g, c, KC, 0, 256),
                                   start=(c == 0), stop=(c == KC - 1))
                mm.then_inc(tile_done, 1)
                if k == 0:
                    rotate(11)

            def scores(u):
                g, h, w = UNITS[u]
                bank = 5 + u % 2
                if u == 0:
                    pe.wait_ge(roped, 36)
                if u >= 2:
                    pe.wait_ge(s_soft, 3 * (u - 2) + 1)
                q, k = head1(0, g, h), head1(6, g, h)
                if g == 0:
                    for b in (2 * w, 2 * w + 1):
                        at = (b % 2) * 2 * P
                        qb = q[:, b * P:(b + 1) * P]
                        if b == 0:
                            for half in range(2):
                                mm = pe.matmul(ps[:, bank, at + half * P:at + (half + 1) * P], qb, k[:, 0:P],
                                               start=True, stop=True)
                        else:
                            mm = pe.matmul(ps[:, bank, at:at + 2 * P], qb, k[:, (b - 1) * P:(b + 1) * P],
                                           start=True, stop=True)
                else:
                    for r in range(4):
                        mm = pe.matmul(ps[:, bank, r * P:(r + 1) * P], q[:, r:T:4], k[:, r:T:4],
                                       start=True, stop=True)
                mm.then_inc(s_scores, 1)

            def turn(u):
                pe.wait_ge(s_exp, u + 1)
                if u >= 2:
                    pe.wait_ge(s_ptc, u - 1)
                for part in range(4):
                    mm = pe.transpose(ps[:, 7 if u % 2 == 0 else 4, part * P:(part + 1) * P],
                                      s1[:, u % 2, part * P:(part + 1) * P], C("ident"))
                mm.then_inc(s_pt, 1)

            def values(u):
                g, h, w = UNITS[u]
                o = 3 * (h // 2) + g
                pe.wait_ge(s_ptc, u + 1)
                if o >= 2:
                    pe.wait_ge(s_og, o - 1)
                rows_of = ps[(h % 2) * HD:(h % 2 + 1) * HD, 2 + o % 2, :]
                for part in range(4):
                    p_t = pt1[:, u % 2, part * P:(part + 1) * P]
                    if g == 0:
                        b = 2 * w + part // 2
                        keys = b if part % 2 else max(b - 1, 0)
                        mm = pe.matmul(rows_of[:, b * P:(b + 1) * P], v1[:, keys, h * HD:(h + 1) * HD], p_t,
                                       start=(part % 2 == 0), stop=(part % 2 == 1))
                    else:
                        mm = pe.matmul(rows_of[:, part * P:(part + 1) * P],
                                       v1[:, 4 * g + part, h * HD:(h + 1) * HD], p_t, start=True, stop=True)
                mm.then_inc(s_pv, 1)

            pe.wait_ge(evac1, E_GATE)
            for u in range(NU + 2):
                if u < NU:
                    scores(u)
                if 1 <= u <= NU:
                    turn(u - 1)
                if u >= 2:
                    values(u - 2)
                if u < NU:
                    if u % 2 == 0:
                        slot_wait(pe, n1 + 9 + u // 2)
                    if u >= 2:
                        pe.wait_ge(evac1, E_GATE + u - 1)
                    gemm(ps[:, u % 2, :], n1 + 9 + u // 2, u % 2, lambda c: hT[:, c, :])
            for k in range(4):
                if k == 1:
                    pe.wait_ge(s_sum, NU)
                    pe.wait_ge(s_og, 6)
                    for j in range(6):
                        stat = mst if j % 2 == 0 else lst
                        g = j // 2
                        for i in range(NB):
                            mm = pe.transpose(ps[0:HPG, 2 + j, i * P:(i + 1) * P],
                                              stat[:, g * HPG:(g + 1) * HPG, i], C("ident"))
                    mm.then_inc(s_strow, 1)
                if k % 2 == 0:
                    slot_wait(pe, n1 + 17 + k // 2)
                pe.wait_ge(evac1, E_PZ + k - 1)
                gemm(ps[:, k % 2, :], n1 + 17 + k // 2, k % 2, lambda c: hT[:, c, :])
            pe.wait_ge(s_stc, 6)
            for hp in range(2):
                for g in range(G1):
                    pe.wait_ge(s_w, 12 + g)
                    pe.matmul(ps[:, 2 + 3 * hp + g, :], C("pair_select", HPG)[:, hp * P:(hp + 1) * P],
                              rows[:, 2 * g, :], start=True, stop=True).then_inc(s_wb, 1)
            pe.wait_ge(evac1, E_PZ + 4)
            for g in range(4):
                pe.wait_ge(s_pool, POOL_AT[g])
                if g >= 2:
                    pe.wait_ge(s_pyc, g - 1)
                pe.matmul(ps[:, g % 2, :], poolw[:, g, :], pool_x[g][:, PAD:], start=True, stop=True)\
                    .then_inc(s_py, 1)
            for s in range(3):
                slot_wait(pe, n1 + 19 + s)
            pe.wait_ge(s_pyc, 4)
            for m in range(KC):
                if m >= 2:
                    pe.wait_ge(s_merge, 3 * (m - 2) + 2)
                for c in range(4):
                    mm = pe.matmul(ps[:, m % 2, :], ring[:, (n1 + 20 + c // 2) % RING,
                                                         (c % 2) * D + m * P:(c % 2) * D + (m + 1) * P],
                                   hT[:, c, :], start=(c == 0), stop=(c == 3))
                mm.then_inc(tile_done, 1)
                if m == 0:
                    pe.wait_ge(s_mix, 10)
                for c in range(2):
                    mm = pe.matmul(ps[:, 2 + m % 2, :], ring[:, (n1 + 19) % RING, c * D + m * P:c * D + (m + 1) * P],
                                   attnT[:, c, :], start=(c == 0), stop=(c == 1))
                mm.then_inc(tile_done, 1)
            for m in range(KC):
                if m % 2 == 0:
                    slot_wait(pe, n1 + 22 + m // 2)
                if m >= 4:
                    pe.wait_ge(x_ready, 2 * KC + m - 3)
                gemm(ps[:, 4 + m % 4, :], n1 + 22 + m // 2, m % 2, lambda c: merged[:, c, :],
                     first=(lambda c: pe.wait_ge(s_merge, 3 * (c + 1))) if m == 0 else None)

        def natural(x):
            return x.rearrange("p (r q) -> p r q", r=4)

        def by_residue(x):
            return x.rearrange("p (q r) -> p r q", r=4)

        def mix1_act(act):
            for t in range(12):
                act.wait_ge(tile_done, e1 + t + 1)
                if t >= 2:
                    act.wait_ge(roped, 3 * (t - 2) + 2)
                act.activation(act_t[:, t % 2, :], ps[:, t % 4, :], ACT.Copy).then_inc(evac1, 1)
            for k in range(12):
                act.wait_ge(tile_done, e1 + E_V + k + 1)
                act.activation(v1[:, k, :], ps[:, k % 4, 0:256], ACT.Copy).then_inc(evac1, 1)
            for u in range(NU + 1):
                if u >= 1:
                    act.wait_ge(s_pt, u)
                    if u >= 3:
                        act.wait_ge(s_pv, u - 2)
                    v = u - 1
                    act.activation(pt1[:, v % 2, :], ps[:, 7 if v % 2 == 0 else 4, :], ACT.Copy).then_inc(s_ptc, 1)
                if u < NU:
                    act.wait_ge(s_soft, 3 * u + 3)
                    act.activation(s1[:, u % 2, :], s1[:, u % 2, :], ACT.Exp, scale=HD ** -0.5).then_inc(s_exp, 1)
                    act.wait_ge(tile_done, e1 + E_GATE + u + 1)
                    act.activation(gates[:, u, :], ps[:, u % 2, :], ACT.Exp, scale=-1.0).then_inc(evac1, 1)
            act.wait_ge(s_strow, 1)
            for k in range(6):
                dst, src = rows[:, k, :], ps[0:HPG, 2 + k, :]
                if k >= 2:
                    dst, src = by_residue(dst), natural(src)
                act.activation(dst, src, ACT.Copy).then_inc(s_stc, 1)
            for g in range(G1):
                act.wait_ge(s_w, 3 + g)
                act.activation(rows[:, 2 * g, :], rows[:, 2 * g, :], ACT.Exp, scale=HD ** -0.5).then_inc(s_wexp, 1)
            for k in range(4):
                act.wait_ge(tile_done, e1 + E_PZ + k + 1)
                act.activation(pool_x[k][:, PAD:], ps[:, k % 2, :], ACT.Copy).then_inc(evac1, 1)
            for g in range(4):
                act.wait_ge(s_py, g + 1)
                act.activation(hT[:, g, :], ps[:, g % 2, :], ACT.Identity, scale=vec("pool_scale", g)).then_inc(s_pyc, 1)

        def mix1_dve(dve):
            for t in range(12):
                dve.wait_ge(evac1, t + 1)
                dve.tensor_tensor(qk1[:, t, :], act_t[:, t % 2, :], C("cos"), ALU.mult).then_inc(roped, 1)
                dve.wait_ge(rot_done, t + 1)
                if t >= 2:
                    dve.wait_ge(roped, 3 * (t - 2) + 3)
                dve.tensor_tensor(act_t[:, 2 + t % 2, :], ps[:, 5 + t % 2, :], C("sin"), ALU.mult).then_inc(roped, 1)
                dve.wait_ge(roped, 3 * t + 2)
                dve.tensor_tensor(qk1[:, t, :], qk1[:, t, :], act_t[:, 2 + t % 2, :], ALU.add).then_inc(roped, 1)

            def parts(u):
                g, h, w = UNITS[u]
                hh = g * HPG + h
                if g == 0:
                    return (s1[:, u % 2, :].rearrange("p (b k) -> p b k", b=2), mst[:, hh, 2 * w:2 * w + 2],
                            lst[:, hh, 2 * w:2 * w + 2], C(f"mask_band{w}").rearrange("p (b k) -> p b k", b=2), 2)
                mask = C("mask_step4" if g == 1 else "mask_step16").unsqueeze(1).to_broadcast([P, 4, P])
                return (s1[:, u % 2, :].rearrange("p (b k) -> p b k", b=4), mst[:, hh, :], lst[:, hh, :], mask, 4)

            def soft(u):
                s, m, _, mask, b = parts(u)
                dve.wait_ge(s_scores, u + 1)
                if u >= 2:
                    dve.wait_ge(s_pt, u - 1)
                    dve.wait_ge(s_sum, u - 1)
                dve.tensor_tensor(s, ps[:, 5 + u % 2, :].rearrange("p (b k) -> p b k", b=b), mask, ALU.add)\
                    .then_inc(s_soft, 1)
                dve.wait_ge(s_soft, 3 * u + 1)
                dve.tensor_reduce(m, s, AX.X, ALU.max).then_inc(s_soft, 1)
                dve.wait_ge(s_soft, 3 * u + 2)
                dve.tensor_tensor(s, s, m.unsqueeze(2).to_broadcast([P, b, T // b]), ALU.subtract).then_inc(s_soft, 1)

            def total(u):
                s, _, l, _, _ = parts(u)
                dve.wait_ge(s_exp, u + 1)
                dve.tensor_reduce(l, s, AX.X, ALU.add).then_inc(s_sum, 1)

            def gate(u):
                dve.wait_ge(evac1, E_GATE + u + 1)
                dve.tensor_scalar(gates[:, u, :], gates[:, u, :], 1.0, None, ALU.add).then_inc(s_gate, 1)
                dve.wait_ge(s_gate, 2 * u + 1)
                dve.reciprocal(gates[:, u, :], gates[:, u, :]).then_inc(s_gate, 1)

            for u in range(NU + 2):
                if u < NU:
                    soft(u)
                if 1 <= u <= NU:
                    total(u - 1)
                    gate(u - 1)
                if u >= 2 and (u == NU + 1 or (UNITS[u - 2][0], UNITS[u - 2][1] // 2) !=
                               (UNITS[u - 1][0], UNITS[u - 1][1] // 2)):
                    g, h, _ = UNITS[u - 2]
                    o = 3 * (h // 2) + g
                    dve.wait_ge(s_pv, u - 1)
                    dst, src = og1[:, o, :], ps[:, 2 + o % 2, :]
                    if g:
                        dst, src = by_residue(dst), natural(src)
                    dve.tensor_copy(dst, src).then_inc(s_og, 1)
            dve.wait_ge(s_stc, 6)
            mx, tot = rows[:, 6, :], rows[:, 7, :]
            dve.tensor_tensor(mx, rows[:, 0, :], rows[:, 2, :], ALU.max).then_inc(s_w, 1)
            dve.wait_ge(s_w, 1)
            dve.tensor_tensor(mx, mx, rows[:, 4, :], ALU.max).then_inc(s_w, 1)
            dve.wait_ge(s_w, 2)
            for g in range(G1):
                dve.tensor_tensor(rows[:, 2 * g, :], rows[:, 2 * g, :], mx, ALU.subtract).then_inc(s_w, 1)
            for g in range(G1):
                dve.wait_ge(s_wexp, g + 1)
                dve.tensor_tensor(rows[:, 2 * g + 1, :], rows[:, 2 * g + 1, :], rows[:, 2 * g, :], ALU.mult)\
                    .then_inc(s_w, 1)
            dve.wait_ge(s_w, 7)
            dve.tensor_tensor(tot, rows[:, 1, :], rows[:, 3, :], ALU.add).then_inc(s_w, 1)
            dve.wait_ge(s_w, 9)
            dve.tensor_tensor(tot, tot, rows[:, 5, :], ALU.add).then_inc(s_w, 1)
            dve.wait_ge(s_w, 10)
            dve.reciprocal(tot, tot).then_inc(s_w, 1)
            dve.wait_ge(s_w, 11)
            for g in range(G1):
                dve.tensor_tensor(rows[:, 2 * g, :], rows[:, 2 * g, :], tot, ALU.mult).then_inc(s_w, 1)
            for hp in range(2):
                for g in range(G1):
                    j = 3 * hp + g
                    dve.wait_ge(s_wb, j + 1)
                    dve.tensor_tensor(og1[:, j, :], og1[:, j, :], ps[:, 2 + j, :], ALU.mult).then_inc(s_mix, 1)
                dve.wait_ge(s_mix, 5 * hp + 2)
                dve.tensor_tensor(attnT[:, hp, :], og1[:, 3 * hp, :], og1[:, 3 * hp + 1, :], ALU.add)\
                    .then_inc(s_mix, 1)
                dve.wait_ge(s_mix, 5 * hp + 4)
                dve.tensor_tensor(attnT[:, hp, :], attnT[:, hp, :], og1[:, 3 * hp + 2, :], ALU.add)\
                    .then_inc(s_mix, 1)
            dve.wait_ge(s_gate, 2 * NU)
            for m in range(KC):
                if m >= 2:
                    dve.wait_ge(s_merge, 3 * (m - 2) + 3)
                dve.wait_ge(tile_done, e1 + E_BR + 2 * m + 1)
                dve.tensor_tensor(act_t[:, m % 2, :], ps[:, m % 2, :], gates[:, KC + m, :], ALU.mult).then_inc(s_merge, 1)
                dve.wait_ge(tile_done, e1 + E_BR + 2 * m + 2)
                dve.tensor_tensor(act_t[:, 2 + m % 2, :], ps[:, 2 + m % 2, :], gates[:, m, :], ALU.mult)\
                    .then_inc(s_merge, 1)
                dve.wait_ge(s_merge, 3 * m + 2)
                dve.tensor_tensor(merged[:, m, :], act_t[:, m % 2, :], act_t[:, 2 + m % 2, :], ALU.add)\
                    .then_inc(s_merge, 1)
            residual_dve(dve, 2, e1 + E_OUT1, lambda m: 4 + m % 4, lambda m: 1.0)

        POOL_AT, n = [], 6
        for g in range(4):
            n += g + 1 + 3
            POOL_AT.append(n)

        def mix1_pool(pool):
            pool.wait_ge(s_pv, NU)
            pool.wait_ge(s_pt, NU)
            pool.wait_ge(s_sum, NU)
            for x in pool_x + pool_s:
                pool.memset(x[:, 0:PAD], 0.0).then_inc(s_pool, 1)
            n = 6
            pool.wait_ge(s_pool, n)
            for g, win in enumerate(POOLS):
                pool.wait_ge(evac1, E_PZ + g + 1)
                cur, lag, k = pool_x[g], 1, 0
                while lag < win:
                    dst = pool_s[k % 2]
                    pool.tensor_tensor(dst[:, PAD:], cur[:, PAD:], cur[:, PAD - lag:PAD + T - lag], ALU.add)\
                        .then_inc(s_pool, 1)
                    n += 1
                    pool.wait_ge(s_pool, n)
                    cur, lag, k = dst, 2 * lag, k + 1
                mean = pool_s[k % 2]
                pool.tensor_scalar(mean[:, PAD:], cur[:, PAD:], 1.0 / win, 0.0, ALU.mult, ALU.add).then_inc(s_pool, 1)
                pool.wait_ge(s_pool, n + 1)
                pool.tensor_tensor(mean[:, PAD:2 * PAD], cur[:, PAD:2 * PAD],
                                   C("pool_count")[:, g * PAD:(g + 1) * PAD], ALU.mult).then_inc(s_pool, 1)
                pool.wait_ge(s_pool, n + 2)
                pool.tensor_tensor(pool_x[g][:, PAD:], mean[:, PAD:], pool_x[g][:, PAD:], ALU.subtract)\
                    .then_inc(s_pool, 1)
                n += 3
                pool.wait_ge(s_pool, n)
                assert n == POOL_AT[g]


        TWO_PI = (6.28125, 8117.0 / 2 ** 22, float(np.float32(2 * np.pi - 6.28125 - 8117.0 / 2 ** 22)))
        MAGIC = 12582912.0
        PI = 3.1415925

        def reduce_angle(dve, ang, k, signal, at):
            dve.tensor_scalar(k, ang, 1 / (2 * np.pi), MAGIC, ALU.mult, ALU.add).then_inc(signal, 1)
            dve.wait_ge(signal, at + 1)
            dve.tensor_scalar(k, k, -MAGIC, None, ALU.add).then_inc(signal, 1)
            dve.wait_ge(signal, at + 2)
            for n, part in enumerate(TWO_PI):
                dve.scalar_tensor_tensor(ang, k, -part, ang, ALU.mult, ALU.add).then_inc(signal, 1)
                dve.wait_ge(signal, at + 3 + n)
            dve.tensor_scalar(ang, ang, PI, -PI, ALU.min, ALU.max).then_inc(signal, 1)
            dve.wait_ge(signal, at + 6)

        s_pos = sem("positions_loaded")
        s_ang = sem("angle_steps")
        s_sin = sem("sines_done")

        def tables_dve(dve):
            ang, k = act_t[:, 2, :], act_t[:, 3, :]
            dve.wait_ge(s_pos, 16)
            dve.tensor_copy(ang, k.bitcast(I32)).then_inc(s_ang, 1)
            dve.wait_ge(s_ang, 1)
            dve.tensor_scalar(ang, ang, C("inv_freq"), None, ALU.mult).then_inc(s_ang, 1)
            dve.wait_ge(s_ang, 2)
            reduce_angle(dve, ang, k, s_ang, 2)

        def tables_act(act):
            act.wait_ge(s_ang, 8)
            act.activation(C("sin"), act_t[:, 2, :], ACT.Sin).then_inc(s_sin, 1)
            act.activation(act_t[:, 3, :], act_t[:, 2, :], ACT.Abs).then_inc(s_sin, 1)
            act.wait_ge(s_sin, 2)
            act.activation(C("cos"), act_t[:, 3, :], ACT.Sin, bias=C("half_pi"), scale=-1.0).then_inc(s_sin, 1)

        r2 = Region()
        qk2 = r2.take(16 * T).rearrange("p (j t) -> p j t", j=16)
        v2 = r2.take(NB * D).rearrange("p (i d) -> p i d", i=NB)
        r_index = r2.at
        index_qk = r2.take(5 * T)
        iqk = index_qk.rearrange("p (j t) -> p j t", j=5)
        score = r2.take(SALL)
        work = r2.take(SALL)
        bias2 = r2.take(SALL)
        soft2 = [phase[:, r_index:][:, j * 2 * T:(j + 1) * 2 * T].rearrange("p (s k) -> p s k", s=2) for j in range(3)]
        pt2 = [r2.take(2 * T).rearrange("p (s k) -> p s k", s=2) for _ in range(2)]
        wi = r2.take(NB * IDX)
        top8 = r2.take(NB * 8).rearrange("p (i k) -> p i k", i=NB)
        mx2 = r2.take(6)
        nm2 = r2.take(6)
        sum2 = r2.take(6)
        e2, n2 = TILE0["mix2"], SLOT0["mix2"]
        E2_K, E2_W, E2_QK, E2_V, E2_OUT = 4, 5, 6, 22, 38
        rbuf = (acc, rs)

        evac2 = sem("proj2_evacuated")
        rot2 = sem("index_rotated")
        roped2 = sem("index_roped")
        s_logit = sem("index_logits")
        s_relu = sem("index_relu")
        s_idx = sem("index_added")
        s_adm = sem("index_masked")
        s_top = sem("top_steps")
        s_bias = sem("bias_done")
        s_ss = sem("head_squares")
        s_hroot = sem("head_roots")
        s_hn = sem("head_norms")
        s_hrot = sem("head_rotated")
        s_hrope = sem("head_roped")
        s_qk2 = sem("scores2")
        s_mask2 = sem("masked2")
        s_exp2 = sem("exp2")
        s_inv2 = sem("inverse_sums2")
        s_norm2 = sem("normalised2")
        s_t2 = sem("turned2")
        s_tca = sem("turned2_copied_act")
        s_tcd = sem("turned2_copied_dve")
        s_pv2 = sem("pv2")
        s_o2 = sem("outputs2")

        def mix2_loads(sp):
            w = feat(a["attn_w_in_2"][0])
            for s in range(2):
                load_slot(sp, n2 + s, w[:, :, 3 * D + s * WCOL:3 * D + (s + 1) * WCOL])
            load_slot(sp, n2 + 2, w[:, :, 3 * D + IDX * HD:3 * D + IDX * HD + HD + IDX])
            for s in range(8 + 4):
                load_slot(sp, n2 + 3 + s, w[:, :, s * WCOL:(s + 1) * WCOL])
            wo = feat(a["attn_w_out_2"][0])
            for s in range(4):
                load_slot(sp, n2 + 15 + s, wo[:, :, s * WCOL:(s + 1) * WCOL])

        UNITS2 = [(pair, i) for pair in range(H2 // 2) for i in range(NB)]
        NU2 = len(UNITS2)

        def head2(base, h):
            return qk2[(h % 2) * HD:(h % 2 + 1) * HD, base + h // 2, :]

        def mix2_pe(pe):
            hn = h_before(4)

            def gemm(out, n, t, src, first=None):
                for c in range(KC):
                    if first is not None:
                        first(c)
                    mm = pe.matmul(out, wtile(n, c, KC, t * P, (t + 1) * P), src(c),
                                   start=(c == 0), stop=(c == KC - 1))
                mm.then_inc(tile_done, 1)

            def rotate(t):
                pe.wait_ge(evac2, t + 1)
                if t >= 2:
                    pe.wait_ge(roped2, 3 * (t - 2) + 2)
                pe.matmul(ps[:, 5 + t % 2, :], C("rot32"), act_t[:, t % 2, :], start=True, stop=True)\
                    .then_inc(rot2, 1)

            for t in range(4):
                if t % 2 == 0:
                    slot_wait(pe, n2 + t // 2)
                gemm(ps[:, t, :], n2 + t // 2, t % 2, lambda c: hT[:, c, :],
                     first=(lambda c: pe.wait_ge(h_ready, hn + c + 1)) if t == 0 else None)
                if t >= 1:
                    rotate(t - 1)
            slot_wait(pe, n2 + 2)
            pe.wait_ge(evac2, 2)
            wk = ring[:, (n2 + 2) % RING, 0:KC * (HD + IDX)].rearrange("p (c w) -> p c w", c=KC)
            for half in range(2):
                for c in range(KC):
                    mm = pe.matmul(ps[half * HD:(half + 1) * HD, 0, :], wk[:, c, 0:HD], hT[:, c, :],
                                   start=(c == 0), stop=(c == KC - 1))
            mm.then_inc(tile_done, 1)
            rotate(3)
            for i in range(NB):
                for c in range(KC):
                    mm = pe.matmul(ps[:, 1, i * IDX:(i + 1) * IDX], hT[:, c, i * P:(i + 1) * P], wk[:, c, HD:],
                                   start=(c == 0), stop=(c == KC - 1))
            mm.then_inc(tile_done, 1)
            rotate(4)
            pe.wait_ge(roped2, 15)
            for i in range(NB):
                for x in range(IDX):
                    y = i * IDX + x
                    if y >= 4:
                        pe.wait_ge(s_relu, y - 3)
                    half = slice((x % 2) * HD, (x % 2 + 1) * HD)
                    pe.matmul(ps[:, 4 + y % 4, 0:(i + 1) * P], iqk[half, x // 2, i * P:(i + 1) * P],
                              iqk[half, 4, 0:(i + 1) * P], start=True, stop=True).then_inc(s_logit, 1)
                    keep_warm(pe, 2, 1)
            pe.wait_ge(evac2, E2_QK)
            pe.wait_ge(s_relu, NB * IDX)
            def values(k):
                s, i = k // 4, k % 4
                if i == 0:
                    slot_wait(pe, n2 + 11 + s)
                pe.wait_ge(evac2, E2_QK + 2 * (12 + k) + 2 if k < 4 else E2_QK + 32 + k - 3)
                for c in range(KC):
                    mm = pe.matmul(ps[:, k % 4, 0:256], hT[:, c, i * P:(i + 1) * P],
                                   wtile(n2 + 11 + s, c, KC, 0, 256), start=(c == 0), stop=(c == KC - 1))
                mm.then_inc(tile_done, 1)

            for t in range(18):
                if t >= 16:
                    values(2 * t - 32)
                    if t == 17:
                        values(2 * t - 31)
                if t < 16:
                    if t % 2 == 0:
                        slot_wait(pe, n2 + 3 + t // 2)
                    if t >= 4:
                        pe.wait_ge(evac2, E2_QK + 2 * (t - 4) + 2)
                    gemm(ps[:, t % 4, :], n2 + 3 + t // 2, t % 2, lambda c: hT[:, c, :])
                if 1 <= t <= 16:
                    v = t - 1
                    pe.wait_ge(evac2, E2_QK + 2 * v + 2)
                    if v >= 2:
                        pe.wait_ge(s_hroot, v - 1)
                    pe.matmul(ps[:, 4 + v % 2, :], C("head_ones"), sq[:, v % 2, :], start=True, stop=True)\
                        .then_inc(s_ss, 1)
                if t >= 2:
                    v = t - 2
                    if t == 16:
                        values(1)
                    pe.wait_ge(s_hn, 2 * v + 2)
                    if v >= 2:
                        pe.wait_ge(s_hrope, 3 * (v - 2) + 2)
                    pe.matmul(ps[:, 6 + v % 2, :], C("rot32"), act_t[:, v % 2, :], start=True, stop=True)\
                        .then_inc(s_hrot, 1)
            for k in range(4, 16):
                values(k)

            pe.wait_ge(s_hrope, 48)
            pe.wait_ge(evac2, E2_QK + 32 + 16)
            for st in range(NU2 + 3):
                if st < NU2:
                    u, (pair, i) = st, UNITS2[st]
                    if u >= 2:
                        pe.wait_ge(s_mask2, 3 * (u - 2) + 2)
                    for s in range(2):
                        mm = pe.matmul(ps[:, 2 * (u % 2) + s, 0:(i + 1) * P],
                                       head2(0, 2 * pair + s)[:, i * P:(i + 1) * P],
                                       head2(8, 2 * pair + s)[:, 0:(i + 1) * P], start=True, stop=True)
                    mm.then_inc(s_qk2, 1)
                if 2 <= st < NU2 + 2:
                    u, (pair, i) = st - 2, UNITS2[st - 2]
                    pe.wait_ge(s_norm2, 2 * u + 2)
                    if u >= 1:
                        pe.wait_ge(s_tca, u)
                        pe.wait_ge(s_tcd, u)
                    for s in range(2):
                        for j in range(i + 1):
                            mm = pe.transpose(ps[:, 4 + s, j * P:(j + 1) * P], soft2[u % 3][:, s, j * P:(j + 1) * P],
                                              C("ident"))
                    mm.then_inc(s_t2, 1)
                if st >= 3:
                    u, (pair, i) = st - 3, UNITS2[st - 3]
                    pe.wait_ge(s_tca, u + 1)
                    pe.wait_ge(s_tcd, u + 1)
                    if pair >= 2:
                        pe.wait_ge(s_o2, pair - 1)
                    for j in range(i + 1):
                        for s in range(2):
                            h = 2 * pair + s
                            mm = pe.matmul(ps[s * HD:(s + 1) * HD, 6 + pair % 2, i * P:(i + 1) * P],
                                           v2[:, j, h * HD:(h + 1) * HD], pt2[u % 2][:, s, j * P:(j + 1) * P],
                                           start=(j == 0), stop=(j == i))
                    mm.then_inc(s_pv2, 1)
            for m in range(KC):
                if m % 2 == 0:
                    slot_wait(pe, n2 + 15 + m // 2)
                if m >= 4:
                    pe.wait_ge(x_ready, 5 * KC + m - 3)
                gemm(ps[:, m % 4, :], n2 + 15 + m // 2, m % 2, lambda c: hT[:, c, :],
                     first=(lambda c: pe.wait_ge(s_o2, c + 1)) if m == 0 else None)

        def mix2_act(act):
            for t in range(5):
                act.wait_ge(tile_done, e2 + t + 1)
                if t >= 2:
                    act.wait_ge(roped2, 3 * (t - 2) + 2)
                act.activation(act_t[:, t % 2, :], ps[:, t % 4, :], ACT.Copy).then_inc(evac2, 1)
            act.wait_ge(tile_done, e2 + E2_W + 1)
            act.activation(wi, ps[:, 1, 0:NB * IDX], ACT.Copy, scale=IDX ** -0.5).then_inc(evac2, 1)
            act.wait_ge(roped2, 15)
            for y in range(NB * IDX):
                w = (y // IDX + 1) * P
                act.wait_ge(s_logit, y + 1)
                if y >= 4:
                    act.wait_ge(s_idx, y - 3)
                act.activation(act_t[:, y % 4, 0:w], ps[:, 4 + y % 4, 0:w], ACT.Relu, scale=HD ** -0.5)\
                    .then_inc(s_relu, 1)
            act.wait_ge(s_idx, NB * IDX)
            for t in range(17):
                if t >= 1:
                    v = t - 1
                    act.wait_ge(s_ss, v + 1)
                    if v >= 2:
                        act.wait_ge(s_hn, 2 * (v - 2) + 2)
                    act.activation(rbuf[v % 2][:, :], ps[:, 4 + v % 2, :], ACT.Sqrt, bias=C("eps"),
                                   scale=1.0 / HD).then_inc(s_hroot, 1)
                if t < 16:
                    act.wait_ge(tile_done, e2 + E2_QK + t + 1)
                    if t >= 2:
                        act.wait_ge(s_hrope, 3 * (t - 2) + 2)
                        act.wait_ge(s_ss, t - 1)
                    act.activation(act_t[:, t % 2, :], ps[:, t % 4, :], ACT.Copy).then_inc(evac2, 1)
                    act.activation(sq[:, t % 2, :], ps[:, t % 4, :], ACT.Square).then_inc(evac2, 1)
            for k in range(16):
                s, i = k // 4, k % 4
                act.wait_ge(tile_done, e2 + E2_V + k + 1)
                act.activation(v2[:, i, s * 256:(s + 1) * 256], ps[:, k % 4, 0:256], ACT.Copy).then_inc(evac2, 1)
            for st in range(NU2 + 3):
                if 2 <= st < NU2 + 2:
                    u, (pair, i) = st - 2, UNITS2[st - 2]
                    w = (i + 1) * P
                    act.wait_ge(s_t2, u + 1)
                    if u >= 2:
                        act.wait_ge(s_pv2, u - 1)
                    act.activation(pt2[u % 2][:, 0, 0:w], ps[:, 4, 0:w], ACT.Copy).then_inc(s_tca, 1)
                if st < NU2:
                    u, (pair, i) = st, UNITS2[st]
                    act.wait_ge(s_mask2, 3 * u + 3)
                    if u >= 3:
                        act.wait_ge(s_norm2, 2 * (u - 3) + 2)
                    for s in range(2):
                        x, o = soft2[u % 3][:, s, 0:(i + 1) * P], 2 * (u % 3) + s
                        act.activation(x, x, ACT.Exp, bias=nm2[:, o:o + 1], scale=HD ** -0.5,
                                       accum_out=sum2[:, o:o + 1]).then_inc(s_exp2, 1)
                if st >= 3 and UNITS2[st - 3][1] == NB - 1:
                    pair = UNITS2[st - 3][0]
                    act.wait_ge(s_pv2, st - 2)
                    act.activation(hT[:, pair, :], ps[:, 6 + pair % 2, :], ACT.Copy).then_inc(s_o2, 1)

        def mix2_dve(dve):
            dve.wait_ge(s_sin, 3)
            for t in range(5):
                dve.wait_ge(evac2, t + 1)
                dve.tensor_tensor(iqk[:, t, :], act_t[:, t % 2, :], C("cos"), ALU.mult).then_inc(roped2, 1)
                dve.wait_ge(rot2, t + 1)
                if t >= 2:
                    dve.wait_ge(roped2, 3 * (t - 2) + 3)
                dve.tensor_tensor(act_t[:, 2 + t % 2, :], ps[:, 5 + t % 2, :], C("sin"), ALU.mult).then_inc(roped2, 1)
                dve.wait_ge(roped2, 3 * t + 2)
                dve.tensor_tensor(iqk[:, t, :], iqk[:, t, :], act_t[:, 2 + t % 2, :], ALU.add).then_inc(roped2, 1)
            dve.wait_ge(evac2, E2_W + 1)
            for i in range(NB):
                dst = score[:, SCOLS[i]:SCOLS[i] + (i + 1) * P]
                for x in range(IDX):
                    y = i * IDX + x
                    dve.wait_ge(s_relu, y + 1)
                    relu, w = act_t[:, y % 4, 0:(i + 1) * P], wi[:, y:y + 1]
                    if x == 0:
                        dve.tensor_scalar(dst, relu, w, None, ALU.mult).then_inc(s_idx, 1)
                    else:
                        dve.wait_ge(s_idx, y)
                        dve.scalar_tensor_tensor(dst, relu, w, dst, ALU.mult, ALU.add).then_inc(s_idx, 1)
            dve.tensor_copy(bias2[:, 0:P], C("admissible")).then_inc(s_adm, 1)
            dve.wait_ge(s_idx, NB * IDX)
            for i in range(1, NB):
                own = score[:, SCOLS[i] + i * P:SCOLS[i] + (i + 1) * P]
                dve.tensor_tensor(own, own, C("admissible"), ALU.add).then_inc(s_adm, 1)
            dve.wait_ge(s_adm, NB)

            def row(x, i):
                return x[:, SCOLS[i]:SCOLS[i] + (i + 1) * P]

            def top_round(n):
                for i in range(1, NB):
                    if n >= 1:
                        dve.wait_ge(s_top, 6 * (n - 1) + 3 + i)
                    dve.max(top8[:, i, :], row(work if n else score, i)).then_inc(s_top, 1)
                for i in range(1, NB):
                    dve.wait_ge(s_top, 6 * n + i)
                    dve.match_replace(row(work, i), top8[:, i, :], row(work if n else score, i), GONE)\
                        .then_inc(s_top, 1)

            for t in range(18):
                if t >= 2:
                    v = t - 2
                    dve.wait_ge(s_hrot, v + 1)
                    dve.tensor_tensor(qk2[:, v, :], act_t[:, v % 2, :], C("cos"), ALU.mult).then_inc(s_hrope, 1)
                    if v >= 2:
                        dve.wait_ge(s_hrope, 3 * (v - 2) + 3)
                    dve.tensor_tensor(act_t[:, 2 + v % 2, :], ps[:, 6 + v % 2, :], C("sin"), ALU.mult)\
                        .then_inc(s_hrope, 1)
                    dve.wait_ge(s_hrope, 3 * v + 2)
                    dve.tensor_tensor(qk2[:, v, :], qk2[:, v, :], act_t[:, 2 + v % 2, :], ALU.add)\
                        .then_inc(s_hrope, 1)
                if 1 <= t <= 16:
                    v = t - 1
                    gain = vec("attn_q_gain_2" if v < KC else "attn_k_gain_2", 0)
                    dve.wait_ge(s_hroot, v + 1)
                    dve.reciprocal(rbuf[v % 2][:, :], rbuf[v % 2][:, :]).then_inc(s_hn, 1)
                    dve.wait_ge(s_hn, 2 * v + 1)
                    dve.scalar_tensor_tensor(act_t[:, v % 2, :], act_t[:, v % 2, :], gain, rbuf[v % 2][:, :],
                                             ALU.mult, ALU.mult).then_inc(s_hn, 1)
                if t < ROUNDS:
                    top_round(t)
            dve.wait_ge(s_top, 6 * ROUNDS)
            dve.tensor_scalar(bias2[:, P:], work[:, P:], GONE, BIG, ALU.not_equal, ALU.mult).then_inc(s_bias, 1)
            dve.wait_ge(s_bias, 1)

            for st in range(NU2 + 2):
                if 1 <= st <= NU2:
                    u = st - 1
                    o = 2 * (u % 3)
                    dve.wait_ge(s_exp2, 2 * (u + 1))
                    dve.reciprocal(sum2[:, o:o + 2], sum2[:, o:o + 2]).then_inc(s_inv2, 1)
                if st < NU2:
                    u, (pair, i) = st, UNITS2[st]
                    w, o = (i + 1) * P, 2 * (u % 3)
                    dve.wait_ge(s_qk2, u + 1)
                    if u >= 3:
                        dve.wait_ge(s_t2, u - 2)
                    for s in range(2):
                        dve.tensor_tensor_reduce(soft2[u % 3][:, s, 0:w], ps[:, 2 * (u % 2) + s, 0:w], row(bias2, i),
                                                 1.0, GONE, ALU.add, ALU.max, mx2[:, o + s:o + s + 1])\
                            .then_inc(s_mask2, 1)
                    dve.wait_ge(s_mask2, 3 * u + 2)
                    dve.tensor_scalar(nm2[:, o:o + 2], mx2[:, o:o + 2], -HD ** -0.5, None, ALU.mult)\
                        .then_inc(s_mask2, 1)
                if st >= 2:
                    u, (pair, i) = st - 2, UNITS2[st - 2]
                    w = (i + 1) * P
                    dve.wait_ge(s_t2, u + 1)
                    if u >= 2:
                        dve.wait_ge(s_pv2, u - 1)
                    dve.tensor_copy(pt2[u % 2][:, 1, 0:w], ps[:, 5, 0:w]).then_inc(s_tcd, 1)
            residual_dve(dve, 5, e2 + E2_OUT, lambda m: m % 4, lambda m: shift_of(0, 2, m))

        def mix2_pool(pool):
            for u, (pair, i) in enumerate(UNITS2):
                pool.wait_ge(s_inv2, u + 1)
                for s in range(2):
                    x, o = soft2[u % 3][:, s, 0:(i + 1) * P], 2 * (u % 3) + s
                    pool.tensor_scalar(x, x, sum2[:, o:o + 1], 0.0, ALU.mult, ALU.add).then_inc(s_norm2, 1)

        def conv_weight(l, tap, half, p):
            row = l * 3 + tap
            at = (row % 2) * 2 * FC + half * FC
            return vcol[:, 2 + row // 2, bass.ds(p + at, 1)] if not isinstance(p, int) else \
                vcol[:, 2 + row // 2, at + p:at + p + 1]

        def conv_bias(l, half, p):
            at = l * 2 * FC + half * FC
            return vcol[:, 5, bass.ds(p + at, 1)] if not isinstance(p, int) else vcol[:, 5, at + p:at + p + 1]

        def conv_act(act, k):
            e0, p0, l = TILE0[f"ffn{k}"], FC * k, k - 2
            c0 = FC * l

            def base(i, p, loop):
                act.wait_ge(gated, i * 4 + (p0 + p - 1))
                chunk = i * 4 + p if loop else p
                for half in range(2):
                    act.wait_ge(tile_done, i * 8 + (e0 + 2 * p + half + 1))
                    act.activation(act_t[:, 2 * (p % 2) + half, :], ps[:, 2 * (p % 2) + half, :], ACT.Identity,
                                   bias=conv_bias(l, half, chunk), scale=conv_weight(l, 2, half, chunk))\
                        .then_inc(base_tap, 1)

            def silu(i, p):
                act.wait_ge(taps, i * 16 + 4 * (c0 + p + 1))
                g = act_t[:, 2 * (p % 2) + 1, :]
                act.activation(g, g, ACT.Silu).then_inc(silu_done, 1)

            base(0, 0, False)
            base(0, 1, False)
            silu(0, 0)
            with act.Fori(0, 5) as i:
                for p in range(2, 6):
                    base(i, p, True)
                    silu(i, p - 1)
            silu(0, FC - 1)

        def conv_dve(dve, k):
            e0, p0, l = TILE0[f"ffn{k}"], FC * k, k - 2
            c0 = FC * l

            def earlier(i, p, loop):
                chunk = i * 4 + p if loop else p
                for n, (lag, half) in enumerate(((1, 0), (1, 1), (2, 0), (2, 1))):
                    if lag == 1:
                        dve.wait_ge(base_tap, i * 8 + (2 * (c0 + p) + half + 1))
                    else:
                        dve.wait_ge(taps, i * 16 + (4 * (c0 + p) + half + 1))
                    t = act_t[:, 2 * (p % 2) + half, lag:]
                    dve.scalar_tensor_tensor(t, ps[:, 2 * (p % 2) + half, 0:T - lag],
                                             conv_weight(l, 2 - lag, half, chunk), t, ALU.mult, ALU.add)\
                        .then_inc(taps, 1)

            def product(i, p, loop):
                dve.wait_ge(silu_done, i * 4 + (p0 + p + 1))
                dst = gT[:, bass.ds(i * (4 * T) + p * T, T)] if loop else gT[:, p * T:(p + 1) * T]
                dve.tensor_tensor(dst, act_t[:, 2 * (p % 2), :], act_t[:, 2 * (p % 2) + 1, :], ALU.mult)\
                    .then_inc(gated, 1)

            earlier(0, 0, False)
            earlier(0, 1, False)
            product(0, 0, False)
            with dve.Fori(0, 5) as i:
                for p in range(2, 6):
                    earlier(i, p, True)
                    product(i, p - 1, True)
            product(0, FC - 1, False)

        NK = T // 2
        SSM_UNITS = PAIRS // 2
        r3 = Region(FC * T)
        BT = [r3.take(SSM_UNITS * P).rearrange("p (u s) -> p u s", u=SSM_UNITS) for _ in range(2)]
        CT = [r3.take(KC * P).rearrange("p (c s) -> p c s", c=KC) for _ in range(2)]
        ca_flat = r3.take(2 * KC * P)
        CA = [ca_flat[:, n * KC * P:(n + 1) * KC * P].rearrange("p (c s) -> p c s", c=KC) for n in range(2)]
        CB = r3.take(KC * P).rearrange("p (c s) -> p c s", c=KC)
        par = r3.take(8 * PAIRS).rearrange("p (k j) -> p k j", k=8)
        (DECAY2, TURNS, COEF_RE, COEF_IM, ACOEF_RE, ACOEF_IM, POLE_RE, POLE_IM) = range(8)
        steps = r3.take(NK)
        r5 = Region(r3.at)
        b_in = [r3.take(PAIRS * 16).rearrange("p (j c) -> p j c", j=PAIRS) for _ in range(2)]
        c_in = [r3.take(KC * HD).rearrange("p (c s) -> p c s", c=KC) for _ in range(2)]
        bz_flat = [hT[:, 4 * n:4 * n + 4, :].rearrange("p a t -> p (a t)") for n in range(2)]
        bz = [bz_flat[n].rearrange("p (j k g c) -> p k j g c", j=PAIRS, k=2, g=2)[:, k] for k in (1, 0)
              for n in range(2)]
        cz_flat = [act_t[:, 2 * n:2 * n + 2, :].rearrange("p a t -> p (a t)") for n in range(2)]
        cz = [x.rearrange("p (c g s) -> p c g s", c=KC, g=2) for x in cz_flat]
        bt = [x[:, 0:PAIRS * 16].rearrange("p (j c) -> p j c", j=PAIRS) for x in cz_flat]
        ca_part = [x.rearrange("p (c s) -> p c s", c=KC) for x in cz_flat]
        sm = [ca_flat[0:PAIRS, n * P:(n + 1) * P] for n in range(14)]
        (ARE, AIM, DT, DEC, ANG, KK, SIN, COS, T1, T2, AR, AI, ABR, ABI) = range(14)
        cosT, sinT = ([r5.take(T) for _ in range(3)] for _ in range(2))
        r4 = Region()
        ybuf = [r4.take(T) for _ in range(3)] + [r5.take(T)]
        pre = r4.take(8 * T).rearrange("p (c t) -> p c t", c=8)
        zs = r4.take(4 * T).rearrange("p (c t) -> p c t", c=4)
        zpart = r4.take(2 * T).rearrange("p (c t) -> p c t", c=2)
        state = [r4.take(4 * (NK + 1)).rearrange("p (n j t) -> p n j t", n=2, j=2) for _ in range(2)]
        assert r4.at <= FC * T
        frac, near = act_t[:, 0:2, :], act_t[:, 2:4, :]

        def by_pair(x):
            return x.rearrange("p (j t) -> p j t", j=2)

        s_sin3 = sem("ssm_loaded")
        s_small = sem("ssm_small")
        s_small_a = sem("ssm_small_act")
        s_par = sem("ssm_turned")
        s_parc = sem("ssm_turned_copied")
        s_bz = sem("ssm_matrices")
        s_ca = sem("ssm_ca_re")
        s_cap = sem("ssm_ca_im")
        s_zero = sem("ssm_zeroed")

        def ssm_loads(sp):
            sp.wait_ge(x_ready, 6 * KC)
            flat = "l (j g) s -> (l j) (g s)"
            sp.dma_start(sm[ARE], a["ssm_a_re_2"].rearrange(flat, g=2)).then_inc(s_sin3, 16)
            sp.dma_start(sm[AIM], a["ssm_a_im_2"].rearrange(flat, g=2)).then_inc(s_sin3, 16)
            sp.dma_start(sm[T1][:, 0:2], a["ssm_log_dt_2"].rearrange("l (j g) -> (l j) g", g=2)).then_inc(s_sin3, 16)
            sp.dma_start(steps, a["steps"]).then_inc(s_sin3, 16)
            for n, name in enumerate(("ssm_b_re_2", "ssm_b_im_2")):
                sp.dma_start(b_in[n], a[name][0].rearrange("(j g) s c -> (g s) j c", g=2)).then_inc(s_sin3, 16)
            for n, name in enumerate(("ssm_c_re_2", "ssm_c_im_2")):
                sp.dma_start(c_in[n], a[name][0].rearrange("(k g) c s -> (g c) k s", g=8)).then_inc(s_sin3, 16)

        def ssm_prepare_act(act):
            act.wait_ge(s_sin3, 16 * 8)
            act.activation(sm[T2][:, 0:2], sm[T1][:, 0:2], ACT.Exp).then_inc(s_small_a, 1)
            act.wait_ge(s_small, 2)
            act.activation(sm[DEC], sm[DEC], ACT.Exp).then_inc(s_small_a, 1)
            act.wait_ge(s_small, 9)
            act.activation(sm[SIN], sm[ANG], ACT.Sin).then_inc(s_small_a, 1)
            act.activation(sm[COS], sm[ANG], ACT.Abs).then_inc(s_small_a, 1)
            act.wait_ge(s_small_a, 4)
            act.activation(sm[COS], sm[COS], ACT.Sin, bias=C("half_pi", PAIRS), scale=-1.0).then_inc(s_small_a, 1)

        def ssm_prepare_dve(dve):
            at = [0]

            def step(ins):
                at[0] += 1
                ins.then_inc(s_small, 1)
                dve.wait_ge(s_small, at[0])

            dve.wait_ge(s_small_a, 1)
            dt = sm[T2][:, 0:2].unsqueeze(2).to_broadcast([PAIRS, 2, HD])

            def by_group(x):
                return x.rearrange("j (g s) -> j g s", g=2)

            step(dve.tensor_copy(by_group(sm[DT]), dt))
            step(dve.tensor_tensor(sm[DEC], sm[ARE], sm[DT], ALU.mult))
            step(dve.tensor_tensor(sm[ANG], sm[AIM], sm[DT], ALU.mult))
            reduce_angle(dve, sm[ANG], sm[KK], s_small, at[0])
            at[0] += 6
            dve.wait_ge(s_small_a, 5)
            step(dve.tensor_tensor(sm[AR], sm[COS], sm[DEC], ALU.mult))
            step(dve.tensor_tensor(sm[AI], sm[SIN], sm[DEC], ALU.mult))
            step(dve.tensor_scalar(sm[COS], sm[AR], -1.0, None, ALU.add))
            step(dve.tensor_tensor(sm[T1], sm[ARE], sm[ARE], ALU.mult))
            step(dve.tensor_tensor(sm[T2], sm[AIM], sm[AIM], ALU.mult))
            step(dve.tensor_tensor(sm[T1], sm[T1], sm[T2], ALU.add))
            step(dve.reciprocal(sm[KK], sm[T1]))
            step(dve.tensor_tensor(sm[T1], sm[COS], sm[ARE], ALU.mult))
            step(dve.tensor_tensor(sm[T2], sm[AI], sm[AIM], ALU.mult))
            step(dve.tensor_tensor(sm[T1], sm[T1], sm[T2], ALU.add))
            step(dve.tensor_tensor(sm[DT], sm[T1], sm[KK], ALU.mult))
            step(dve.tensor_tensor(sm[T1], sm[AI], sm[ARE], ALU.mult))
            step(dve.tensor_tensor(sm[T2], sm[COS], sm[AIM], ALU.mult))
            step(dve.tensor_tensor(sm[T1], sm[T1], sm[T2], ALU.subtract))
            step(dve.tensor_tensor(sm[T2], sm[T1], sm[KK], ALU.mult))
            step(dve.tensor_scalar(sm[ANG], sm[ANG], 1 / (2 * np.pi), None, ALU.mult))
            step(dve.tensor_tensor(sm[T1], sm[DT], sm[AR], ALU.mult))
            step(dve.tensor_tensor(sm[KK], sm[T2], sm[AI], ALU.mult))
            step(dve.tensor_tensor(sm[ABR], sm[T1], sm[KK], ALU.subtract))
            step(dve.tensor_tensor(sm[T1], sm[DT], sm[AI], ALU.mult))
            step(dve.tensor_tensor(sm[KK], sm[T2], sm[AR], ALU.mult))
            step(dve.tensor_tensor(sm[ABI], sm[T1], sm[KK], ALU.add))
            step(dve.tensor_tensor(sm[DEC], sm[DEC], sm[DEC], ALU.mult))
            assert at[0] == SMALL_STEPS

        SMALL_STEPS = 32

        def turn(pe, srcs, bank, blocks=KC):
            for c in range(blocks):
                mm = pe.transpose(ps[:, bank + c // 4, (c % 4) * P:(c % 4 + 1) * P], srcs[:, c * P:(c + 1) * P],
                                  C("ident"))
            mm.then_inc(s_par, 1)

        def ssm_prepare_pe(pe, q, half):
            if (q, half) == (0, 1):
                pe.wait_ge(s_small, SMALL_STEPS)
                for k, x in enumerate((DEC, ANG, DT, T2, ABR, ABI, AR, AI)):
                    mm = pe.transpose(ps[:, 4, k * PAIRS:(k + 1) * PAIRS], sm[x], C("ident", PAIRS)[:, 0:PAIRS])
                mm.then_inc(s_par, 1)
            if (q, half) in ((1, 1), (2, 0)):
                pe.wait_ge(s_bz, 16)
                pe.wait_ge(s_parc, 1 if q == 1 else 5)
                turn(pe, bz_flat[q - 1], 4, SSM_UNITS)
            if (q, half) == (2, 1):
                pe.wait_ge(s_bz, 20)
                for n in range(2):
                    pe.wait_ge(s_parc, 2 * n + 7)
                    turn(pe, cz_flat[n], 4 + 2 * n)
            if (q, half) == (3, 0):
                pe.wait_ge(s_parc, 13)
                for j in range(PAIRS):
                    c, g = j // 4, j % 4
                    rows_of = slice(32 * g, 32 * g + 32)
                    for n in range(2):
                        mm = pe.matmul(ps[rows_of, 4 + c // 4, (c % 4) * P + 32 * g:(c % 4) * P + 32 * g + 32],
                                       bz_flat[n][:, 64 * j + 32:64 * j + 64], CT[n][:, c, rows_of],
                                       start=(n == 0), stop=(n == 1))
                mm.then_inc(s_par, 1)

        PARC = 1 + 4 + 4 + 4 + 4

        def ssm_turned_act(act, step):
            if step == 0:
                act.wait_ge(s_par, 1)
                act.activation(par, ps[:, 4, 0:8 * PAIRS].rearrange("p (k j) -> p k j", k=8), ACT.Copy)\
                    .then_inc(s_parc, 1)
            elif step < 3:
                act.wait_ge(s_par, 1 + step)
                for b in range(4):
                    act.activation(BT[step - 1][:, 4 * b:4 * b + 4, :],
                                   ps[:, 4 + b, :].rearrange("p (c s) -> p c s", c=4), ACT.Copy).then_inc(s_parc, 1)
            elif step == 3:
                for n in range(2):
                    act.wait_ge(s_par, 4 + n)
                    for b in range(2):
                        act.activation(CT[n][:, 4 * b:4 * b + 4, :],
                                       ps[:, 4 + 2 * n + b, :].rearrange("p (c s) -> p c s", c=4), ACT.Copy,
                                       scale=1.0 - 2.0 * n).then_inc(s_parc, 1)
            else:
                act.wait_ge(s_par, 6)
                act.wait_ge(s_zero, 5)
                for g in range(4):
                    rows_of = slice(32 * g, 32 * g + 32)
                    act.activation(CB[rows_of, :, rows_of],
                                   ps[rows_of, 4:6, :].rearrange("p b (c s) -> p (b c) s", c=4)[:, :, rows_of],
                                   ACT.Copy).then_inc(s_parc, 1)

        def ssm_matrices_dve(dve):
            dve.wait_ge(s_parc, 1)
            dve.wait_ge(s_zero, 4)
            dve.wait_ge(gated, 3 * FC)
            n = 0
            for k, re, im in ((0, COEF_RE, COEF_IM), (2, ACOEF_RE, ACOEF_IM)):
                cre, cim = (par[:, r, :].unsqueeze(2).to_broadcast([P, PAIRS, 16]) for r in (re, im))
                for out, (x, y), op in ((bz[k], (b_in[0], b_in[1]), ALU.subtract),
                                        (bz[k + 1], (b_in[1], b_in[0]), ALU.add)):
                    if n:
                        dve.wait_ge(s_bz, n)
                    dve.tensor_tensor(bt[0], x, cre, ALU.mult).then_inc(s_bz, 1)
                    dve.tensor_tensor(bt[1], y, cim, ALU.mult).then_inc(s_bz, 1)
                    dve.wait_ge(s_bz, n + 2)
                    for g in range(2):
                        rows_of = slice(g * HD, (g + 1) * HD)
                        dve.tensor_tensor(out[rows_of, :, g, :], bt[0][rows_of], bt[1][rows_of], op)\
                            .then_inc(s_bz, 1)
                    n += 4
            dve.wait_ge(s_bz, 16)
            for k in range(2):
                for g, name in enumerate(("group_even", "group_odd")):
                    dve.tensor_scalar(cz[k][:, :, g, :], c_in[k], C(name), None, ALU.mult).then_inc(s_bz, 1)

        def ssm_ca(eng, n, signal):
            eng.wait_ge(s_parc, 13)
            re, im = (par[:, r, :].unsqueeze(2).to_broadcast([P, PAIRS, 32]) for r in (POLE_RE, POLE_IM))

            def of_pairs(x):
                return x.rearrange("p c (q s) -> p (c q) s", q=4)

            eng.tensor_tensor(of_pairs(CA[n]), of_pairs(CT[n]), re, ALU.mult).then_inc(signal, 1)
            eng.tensor_tensor(of_pairs(ca_part[n]), of_pairs(CT[1 - n]), im, ALU.mult).then_inc(signal, 1)
            eng.wait_ge(signal, 2)
            eng.tensor_tensor(CA[n], CA[n], ca_part[n], ALU.add if n == 0 else ALU.subtract).then_inc(signal, 1)

        s_stack = sem("ssm_stacked")
        s_bu = sem("ssm_input")
        s_near = sem("ssm_near")
        s_frac = sem("ssm_frac")
        s_tab = sem("ssm_tables")
        s_pre = sem("ssm_rotated")
        s_add = sem("ssm_rotated_sum")
        s_scan = sem("ssm_scanned")
        s_postd = sem("ssm_state_re")
        s_postp = sem("ssm_state_im")
        s_y = sem("ssm_output")
        s_yd = sem("ssm_skipped")
        s_g = sem("ssm_gelu")
        s_sig = sem("glu_sigmoid")
        s_glu = sem("glu_product")
        n3, e3 = SLOT0["ssm"], TILE0["ssm"]

        def ssm_glu_loads(sp):
            w = feat(a["ssm_w_glu_2"][0])
            for b in range(4):
                load_slot(sp, n3 + 2 * b, w[:, :, b * WCOL:(b + 1) * WCOL])
                load_slot(sp, n3 + 2 * b + 1, w[:, :, D + b * WCOL:D + (b + 1) * WCOL])

        def tokens(x, odd):
            return x.rearrange("p (k r) -> p r k", r=2)[:, odd, :]

        GLU_EARLY = 6

        def ssm_pe(pe):
            def glu(p, chunks, halves=(0, 1)):
                b, j = p // 2, p % 2
                for w in halves:
                    if j == 0 and chunks[0] == 0:
                        slot_wait(pe, n3 + 2 * b + w)
                    for c in chunks:
                        if p == 0:
                            pe.wait_ge(s_g, c + 1)
                        mm = pe.matmul(ps[:, 2 * (p % 2) + w, :], wtile(n3 + 2 * b + w, c, KC, j * P, (j + 1) * P),
                                       hT[:, c, :], start=(c == 0), stop=(c == KC - 1))
                    if chunks[-1] == KC - 1:
                        mm.then_inc(tile_done, 1)

            pe.wait_ge(s_ca, 3)
            pe.wait_ge(s_cap, 3)
            pe.wait_ge(s_zero, 7)
            for u in range(SSM_UNITS + 2):
                if u < SSM_UNITS:
                    c = u // 2
                    if u % 2 == 0:
                        pe.wait_ge(s_stack, 8 * (c + 1))
                    if u >= 2:
                        pe.wait_ge(s_pre, 4 * (u - 2) + 4)
                    for n in range(2):
                        for j in range(2):
                            rows_of = slice(64 * j, 64 * j + 64)
                            mm = pe.matmul(ps[:, 2 * (u % 2) + j, n * NK:(n + 1) * NK], BT[n][rows_of, u, :],
                                           sq[rows_of, c % 2, (u % 2) * NK:(u % 2 + 1) * NK], start=True, stop=True)
                    mm.then_inc(s_bu, 1)
                if u >= 2:
                    v = u - 2
                    c = v // 2
                    even, odd = (ps[:, 4 + 2 * (c % 2) + k, 0:NK] for k in range(2))
                    if v % 2 == 0:
                        if c >= 2:
                            pe.wait_ge(s_yd, 2 * (c - 2) + 2)
                        pe.matmul(even, CB[:, c, :], hT[:, c, 0:NK], start=True, stop=False)
                    if v >= SSM_UNITS - 2:
                        pe.wait_ge(s_pre, 4 * SSM_UNITS)
                        glu(0, range(GLU_EARLY), (v - (SSM_UNITS - 2),))
                    pe.wait_ge(s_postd, 3 * v + 3)
                    pe.wait_ge(s_postp, 3 * v + 3)
                    for k, (y, matrix) in enumerate(((even, CA), (odd, CT))):
                        for n in range(2):
                            for j in range(2):
                                q = 2 * (v % 2) + j
                                rows_of = slice(32 * q, 32 * q + 32)
                                mm = pe.matmul(y[rows_of], matrix[n][:, c, rows_of],
                                               state[v % 2][:, n, j, k:k + NK], start=(k == 1 and n == 0),
                                               stop=(n == 1))
                    mm.then_inc(s_y, 1)
            glu(0, range(GLU_EARLY, KC))
            for p in range(1, KC):
                if p >= 2:
                    pe.wait_ge(s_glu, p - 1)
                glu(p, range(KC))

        GELU_AFTER = 9
        def stack(act, c):
            if c >= 2:
                act.wait_ge(s_bu, 2 * (c - 2) + 2)
            act.wait_ge(h_ready, h_before(6) + c + 1)
            for q in range(4):
                for k in range(2):
                    to = 32 * (2 * (q % 2) + k)
                    act.activation(sq[to:to + 32, c % 2, (q // 2) * NK:(q // 2 + 1) * NK],
                                   hT[32 * q:32 * q + 32, c, k * NK:(k + 1) * NK], ACT.Copy).then_inc(s_stack, 1)

        TURN = 6.283185

        def nearest(act, u):
            b = u % 2
            if u >= 2:
                act.wait_ge(s_tab, 3 * (u - 2) + 3)
            for j in range(2):
                act.activation(near[:, b, j * NK:(j + 1) * NK], steps, ACT.Identity, bias=C("magic")[:, 0:1],
                               scale=par[:, TURNS, 2 * u + j:2 * u + j + 1]).then_inc(s_near, 1)
            act.wait_ge(s_near, 3 * u + 2)
            act.activation(near[:, b, :], near[:, b, :], ACT.Identity, bias=C("magic")[:, 1:2]).then_inc(s_near, 1)

        def table(act, u):
            b = u % 2
            act.wait_ge(s_frac, 2 * u + 2)
            if u >= 3:
                act.wait_ge(s_postd, 3 * (u - 3) + 3)
                act.wait_ge(s_postp, 3 * (u - 3) + 3)
            act.activation(sinT[u % 3], frac[:, b, :], ACT.Sin, scale=TURN).then_inc(s_tab, 1)
            act.activation(near[:, b, :], frac[:, b, :], ACT.Abs).then_inc(s_tab, 1)
            act.wait_ge(s_tab, 3 * u + 2)
            act.activation(cosT[u % 3], near[:, b, :], ACT.Sin, bias=C("half_pi"), scale=-TURN).then_inc(s_tab, 1)

        def ssm_begin_act(act):
            act.wait_ge(s_ca, 3)
            act.wait_ge(s_cap, 3)
            nearest(act, 0)
            nearest(act, 1)
            table(act, 0)

        def fraction(dve, u):
            b = u % 2
            dve.wait_ge(s_near, 3 * u + 3)
            if u >= 2:
                dve.wait_ge(s_tab, 3 * (u - 2) + 3)
            for j in range(2):
                cols = slice(j * NK, (j + 1) * NK)
                dve.scalar_tensor_tensor(frac[:, b, cols], steps, par[:, TURNS, 2 * u + j:2 * u + j + 1],
                                         near[:, b, cols], ALU.mult, ALU.subtract).then_inc(s_frac, 1)

        def ssm_begin_dve(dve):
            ssm_ca(dve, 0, s_ca)
            fraction(dve, 0)
            fraction(dve, 1)

        def ssm_act(act):
            def gelu(c):
                act.wait_ge(s_yd, 2 * c + 2)
                act.activation(hT[:, c, :], ybuf[c % 4], ACT.Gelu_apprx_tanh).then_inc(s_g, 1)

            for u in range(SSM_UNITS):
                if u:
                    table(act, u)
                if u % 2 == 1 and u >= 3 and u // 2 + 1 < KC:
                    stack(act, u // 2 + 1)
                if u + 2 < SSM_UNITS:
                    nearest(act, u + 2)
                if u % 4 == GELU_AFTER % 4 and u >= GELU_AFTER:
                    for c in range(2):
                        gelu((u - GELU_AFTER) // 2 + c)
            for c in range((SSM_UNITS - 1 - GELU_AFTER) // 4 * 2 + 2, KC):
                gelu(c)
            for p in range(KC):
                act.wait_ge(tile_done, e3 + 2 * p + 2)
                if p >= 2:
                    act.wait_ge(s_glu, p - 1)
                act.activation(act_t[:, p % 2, :], ps[:, 2 * (p % 2) + 1, :], ACT.Sigmoid).then_inc(s_sig, 1)
                if p >= 1:
                    square(act, 7, p - 1)
            square(act, 7, KC - 1)

        def ssm_dve(dve):
            def rotate_in(u):
                b = u % 2
                dve.wait_ge(s_bu, u + 1)
                dve.wait_ge(s_tab, 3 * u + 3)
                if u >= 2:
                    dve.wait_ge(s_add, 2 * (u - 2) + 2)
                for n, (source, tab) in enumerate(((0, cosT), (1, sinT), (1, cosT), (0, sinT))):
                    dve.tensor_tensor(by_pair(pre[:, 4 * b + n, :]),
                                      ps[:, 2 * b:2 * b + 2, source * NK:(source + 1) * NK], by_pair(tab[u % 3]),
                                      ALU.mult)\
                        .then_inc(s_pre, 1)

            def scan(u):
                b = u % 2
                for n in range(2):
                    dve.wait_ge(s_add, 2 * u + n + 1)
                    if u >= 2:
                        dve.wait_ge(s_postp, 3 * (u - 2) + 2)
                        dve.wait_ge(s_postd, 3 * (u - 2) + 2)
                    for j in range(2):
                        decay = par[:, DECAY2, 2 * u + j:2 * u + j + 1].to_broadcast([P, NK])
                        cols = slice(j * NK, (j + 1) * NK)
                        dve.tensor_tensor_scan(zs[:, 2 * b + n, cols], decay, pre[:, 4 * b + 2 * n, cols], 0.0,
                                               ALU.mult, ALU.add).then_inc(s_scan, 1)

            def rotate_back(u):
                b = u % 2
                dve.wait_ge(s_scan, 4 * u + 4)
                if u >= 1:
                    dve.wait_ge(s_postd, 3 * u)
                if u >= 2:
                    dve.wait_ge(s_y, u - 1)
                x = state[b][:, 0, :, 1:]
                dve.tensor_tensor(x, by_pair(zs[:, 2 * b, :]), by_pair(cosT[u % 3]), ALU.mult).then_inc(s_postd, 1)
                dve.tensor_tensor(zpart[:, 0, :], zs[:, 2 * b + 1, :], sinT[u % 3], ALU.mult).then_inc(s_postd, 1)
                dve.wait_ge(s_postd, 3 * u + 2)
                dve.tensor_tensor(x, x, by_pair(zpart[:, 0, :]), ALU.subtract).then_inc(s_postd, 1)

            def skip(c):
                dve.wait_ge(s_y, 2 * c + 2)
                if c >= 4:
                    dve.wait_ge(s_g, c - 3)
                for k in range(2):
                    dve.scalar_tensor_tensor(tokens(ybuf[c % 4], k), hT[:, c, k * NK:(k + 1) * NK], vec("ssm_d_2", c),
                                             ps[:, 4 + 2 * (c % 2) + k, 0:NK], ALU.mult, ALU.add).then_inc(s_yd, 1)

            dve.wait_ge(h_ready, h_before(6) + KC)
            for u in range(SSM_UNITS + 1):
                if u < SSM_UNITS:
                    rotate_in(u)
                if u >= 1:
                    scan(u - 1)
                if u + 2 < SSM_UNITS:
                    fraction(dve, u + 2)
                if u >= 1:
                    rotate_back(u - 1)
                if u % 2 == 0 and u >= 4:
                    skip(u // 2 - 2)
            skip(KC - 1)
            for p in range(KC):
                dve.wait_ge(s_sig, p + 1)
                dve.tensor_tensor(act_t[:, p % 2, :], ps[:, 2 * (p % 2), :], act_t[:, p % 2, :], ALU.mult)\
                    .then_inc(s_glu, 1)
                dve.wait_ge(s_glu, p + 1)
                dve.scalar_tensor_tensor(xT[:, p, :], act_t[:, p % 2, :], shift_of(1, 2, p), xT[:, p, :], ALU.mult,
                                         ALU.add).then_inc(x_ready, 1)
                if p >= 1:
                    add_square(dve, 7, p - 1)
            add_square(dve, 7, KC - 1)

        def ssm_prepare_pool(pool):
            pool.wait_ge(x_ready, 6 * KC)
            pool.wait_ge(tile_done, TILE0["ffn2"] + 2 * FC)
            for n in range(4):
                pool.memset(hT[:, 2 * n:2 * n + 2, :], 0.0).then_inc(s_zero, 1)
            pool.memset(CB, 0.0).then_inc(s_zero, 1)
            ssm_ca(pool, 1, s_cap)

        def ssm_pool(pool):
            pool.wait_ge(x_ready, 7 * KC)
            for b in range(2):
                pool.memset(state[b][:, :, :, 0:1], 0.0).then_inc(s_zero, 1)
            for u in range(SSM_UNITS + 1):
                if u < SSM_UNITS:
                    b = u % 2
                    for n, op in enumerate((ALU.add, ALU.subtract)):
                        pool.wait_ge(s_pre, 4 * u + 2 * n + 2)
                        x = pre[:, 4 * b + 2 * n, :]
                        pool.tensor_tensor(x, x, pre[:, 4 * b + 2 * n + 1, :], op).then_inc(s_add, 1)
                if u >= 1:
                    v, b = u - 1, (u - 1) % 2
                    pool.wait_ge(s_scan, 4 * v + 4)
                    if v >= 2:
                        pool.wait_ge(s_y, v - 1)
                    if v >= 1:
                        pool.wait_ge(s_postp, 3 * v)
                    x = state[b][:, 1, :, 1:]
                    pool.tensor_tensor(x, by_pair(zs[:, 2 * b, :]), by_pair(sinT[v % 3]), ALU.mult).then_inc(s_postp, 1)
                    pool.tensor_tensor(zpart[:, 1, :], zs[:, 2 * b + 1, :], cosT[v % 3], ALU.mult)\
                        .then_inc(s_postp, 1)
                    pool.wait_ge(s_postp, 3 * v + 2)
                    pool.tensor_tensor(x, x, by_pair(zpart[:, 1, :]), ALU.add).then_inc(s_postp, 1)

        out_rows = [phase[:, (FC + j) * T:(FC + j + 1) * T].rearrange("p (i d) -> p i d", i=NB) for j in range(2)]

        def out_pe(pe, q):
            for m in () if q == 0 else range(2 * q - 2, 2 * q) if q < 4 else range(6, 8):
                pe.wait_ge(x_ready, 8 * KC + m + 1)
                if m >= 4:
                    pe.wait_ge(s_out_c, m - 3)
                for i in range(NB):
                    mm = pe.transpose(ps[:, 4 + m % 4, i * P:(i + 1) * P], xT[:, m, i * P:(i + 1) * P], C("ident"))
                mm.then_inc(s_out_t, 1)

        def out_act(act):
            for m in range(KC):
                act.wait_ge(s_out_t, m + 1)
                if m >= 2:
                    act.wait_ge(s_out[m % 2], 16 * (m // 2))
                act.activation(out_rows[m % 2], ps[:, 4 + m % 4, :].rearrange("p (i d) -> p i d", i=NB), ACT.Copy)\
                    .then_inc(s_out_c, 1)

        def out_stores(sp):
            dst = out[0].rearrange("(i p) d -> p i d", p=P)
            for m in range(KC):
                sp.wait_ge(s_out_c, m + 1)
                sp.dma_start(dst[:, :, m * P:(m + 1) * P], out_rows[m % 2]).then_inc(s_out[m % 2], 16)
            for j in range(2):
                sp.wait_ge(s_out[j], 16 * KC // 2)


        def vector_loads(sp):
            loads = []
            for name in ("ffn1_norm", "mix_norm", "ffn2_norm", "norm_mix_2", "norm_ffn_2", "pool_scale",
                         "ssm_d_2", "c_2"):
                src = a[name].rearrange("l (r q) -> (l r) q", q=P)
                loads.append((v_rows[VROWS[name]:VROWS[name] + src.shape[0], 0, :], src))
            src = a["final_norm"].rearrange("(r q) -> r q", q=P)
            loads.append((v_rows[VROWS["final_norm"]:VROWS["final_norm"] + 8, 0, :], src))
            for name in ("attn_q_gain_2", "attn_k_gain_2"):
                for half in range(2):
                    loads.append((v_rows[VROWS[name]:VROWS[name] + 1, 0, half * HD:(half + 1) * HD], a[name]))
            loads.append((v_rows[0:96, 1, :], a["ada_b_2"].rearrange("l (r q) -> (l r) q", q=P)))
            conv = a["ffn_conv_w_2"].rearrange("l k (r q) -> (l k r) q", q=P)
            for j in range(3):
                loads.append((v_rows[0:CONV_ROWS, 2 + j, :], conv[j * CONV_ROWS:(j + 1) * CONV_ROWS, :]))
            loads.append((v_rows[0:CONV_ROWS, 5, :], a["ffn_conv_b_2"].rearrange("l (r q) -> (l r) q", q=P)))
            assert len(loads) == VLOADS
            sp.wait_ge(v_cleared, VTILES)
            for dst, src in loads:
                sp.dma_start(dst, src).then_inc(s_vrows, 16)

        def late_loads(act):
            act.dma_start(const[:, FIRST_CONST:], a["shape_constants"][:, FIRST_CONST:]).then_inc(s_late, 16)
            act.dma_start(poolw[:, :, :], a["pool_w"][0].rearrange("g c d -> c g d")).then_inc(s_late, 16)

        block = ctx.enter_context(nc.Block())

        def on(stage):
            return stop is None or stage <= stop

        @block.sync
        def _(sp):
            sp.dma_start(const[:, 0:FIRST_CONST], a["shape_constants"][:, 0:FIRST_CONST]).then_inc(s_const, 16)
            for m in range(0, KC, 2):
                cols = slice(m * P, (m + 2) * P)
                sp.dma_start(x_rows[:, :, cols], a["x"][0].rearrange("(i p) d -> p i d", p=P)[:, :, cols])\
                    .then_inc(s_xrows[m // 2], 16)
            vector_loads(sp)
            ffn_loads(sp, 0, a["ffn1_w1"][0], a["ffn1_w3"][0], a["ffn1_w2"][0], 0)
            if on(1):
                mix1_loads(sp)
                sp.wait_ge(s_merge, 3 * KC)
                sp.dma_start(act_t[:, 3, :].bitcast(I32), a["positions_2"].to_broadcast([P, T])).then_inc(s_pos, 16)
            if on(2):
                ffn_loads(sp, 1, a["ffn2_w1"][0], a["ffn2_w3"][0], a["ffn2_w2"][0], 0)
            if on(3):
                mix2_loads(sp)
            if on(4):
                up = a["ffn_w_up_2"]
                ffn_loads(sp, 2, up[0], up[0], a["ffn_w_down_2"][0], F, before_down=lambda: ssm_loads(sp))
            if on(5):
                ssm_glu_loads(sp)
            if on(6):
                ffn_loads(sp, 3, up[1], up[1], a["ffn_w_down_2"][1], F)
            if stop is None:
                out_stores(sp)
            if stop is not None:
                sp.wait_ge(x_ready, KC * {0: 2, 1: 3, 2: 4, 3: 6, 4: 7, 5: 8}[stop])

        @block.tensor
        def _(pe):
            pe.wait_ge(s_const, 16)
            for m in range(KC):
                if m % 2 == 0:
                    pe.wait_ge(s_xrows[m // 2], 16)
                if m >= 4:
                    pe.wait_ge(x_ready, m - 3)
                for i in range(NB):
                    mm = pe.transpose(ps[:, m % 4, i * P:(i + 1) * P], x_rows[:, i, m * P:(m + 1) * P],
                                      C("ident"))
                mm.then_inc(x_turned, 1)
            pe.wait_ge(v_cleared, VTILES)
            pe.wait_ge(s_vrows, 16 * VLOADS)
            for j in range(VTILES):
                mm = pe.transpose(ps[:, 5 + j // 4, (j % 4) * P:(j % 4 + 1) * P], v_rows[:, j, :], C("ident"))
            mm.then_inc(s_vbank, 1)
            norm_pe(pe, 0)
            ffn_pe(pe, 0)
            ada_pe(pe)
            norm_pe(pe, 1)
            if on(1):
                pe.wait_ge(s_late, 32)
                mix1_pe(pe)
                norm_pe(pe, 2)
            if on(2):
                ffn_pe(pe, 1)
            if on(3):
                norms_pe(pe)
                mix2_pe(pe)
                norm_pe(pe, 5)
            if on(4):
                ffn_pe(pe, 2, lambda q, half: ssm_prepare_pe(pe, q, half))
                pe.wait_ge(s_parc, PARC)
                norm_pe(pe, 6)
            if on(5):
                ssm_pe(pe)
                norm_pe(pe, 7)
            if on(6):
                ffn_pe(pe, 3, lambda q, half: out_pe(pe, q) if half else None)
                out_pe(pe, 4)

        @block.scalar
        def _(act):
            for m in range(KC):
                square(act, 0, m)
            late_loads(act)
            act.wait_ge(s_vbank, 1)
            act.activation(vcol[:, 0:4, :], ps[:, 5, :].rearrange("p (j d) -> p j d", j=4), ACT.Copy).then_inc(s_vcol, 1)
            act.activation(vcol[:, 4:6, :], ps[:, 6, 0:2 * P].rearrange("p (j d) -> p j d", j=2),
                           ACT.Copy).then_inc(s_vcol, 1)
            act.wait_ge(s_vcol, 2)
            act.activation(cond[:, :], vcol[:, 0, VROWS["c_2"]:VROWS["c_2"] + KC], ACT.Silu).then_inc(cond_done, 1)
            norm_act(act, 0)
            ffn_act(act, 0)
            for m in range(KC):
                square(act, 1, m)
            norm_act(act, 1)
            if on(1):
                act.wait_ge(s_late, 32)
                mix1_act(act)
                for m in range(KC):
                    square(act, 2, m)
                norm_act(act, 2)
            if on(2):
                tables_act(act)
                ffn_act(act, 1)
                for m in range(KC):
                    square(act, 3, m)
                    square_final(act, m)
            if on(3):
                norms_act(act)
                shift_act(act, 4, 0, lambda c: shift_of(0, 0, c))
                mix2_act(act)
                for m in range(KC):
                    square(act, 5, m)
                norm_act(act, 5)
                shift_act(act, 5, KC, lambda c: shift_of(0, 3, c))
            if on(4):
                conv_act(act, 2)
                ssm_prepare_act(act)
                for m in range(KC):
                    square(act, 6, m)
                    for step in {1: (0,), 3: (1, 2), 5: (3, 4)}.get(m, ()):
                        ssm_turned_act(act, step)
                    if m == 5:
                        ssm_begin_act(act)
                norm_act(act, 6)
                shift_act(act, 6, 2 * KC, lambda c: shift_of(1, 0, c), lambda c: stack(act, min(c, 1)) if c in (0, KC - 1) else None)
            if on(5):
                ssm_act(act)
                norm_act(act, 7)
                shift_act(act, 7, 3 * KC, lambda c: shift_of(1, 3, c))
            if on(6):
                conv_act(act, 3)
                out_act(act)

        @block.vector
        def _(dve):
            for m in range(KC):
                dve.wait_ge(x_turned, m + 1)
                dve.tensor_copy(xT[:, m, :], ps[:, m % 4, :]).then_inc(x_ready, 1)
                if m >= 1:
                    add_square(dve, 0, m - 1)
            add_square(dve, 0, KC - 1)
            dve.wait_ge(s_vcol, 2)
            norm_dve(dve, 0, lambda c: vec("ffn1_norm", c))
            ffn_dve(dve, 0)
            residual_dve(dve, 1, TILE0["ffn0"] + 2 * FC, lambda m: m % 4, lambda m: 0.5)
            norm_dve(dve, 1, lambda c: vec("mix_norm", c))
            ada_dve(dve)
            if on(1):
                dve.wait_ge(s_late, 32)
                mix1_dve(dve)
                norm_dve(dve, 2, lambda c: vec("ffn2_norm", c))
            if on(2):
                tables_dve(dve)
                ffn_dve(dve, 1)
                residual_dve(dve, 3, TILE0["ffn1"] + 2 * FC, lambda m: m % 4, lambda m: 0.5,
                             after={m: lambda m=m: add_square_final(dve, m - 1) for m in range(1, KC)})
            if on(3):
                norms_dve(dve)
                mix2_dve(dve)
                norm_dve(dve, 5, lambda c: modg[:, KC + c:KC + c + 1], shifted=True)
            if on(4):
                conv_dve(dve, 2)
                ssm_prepare_dve(dve)
                residual_dve(dve, 6, TILE0["ffn2"] + 2 * FC, lambda m: m % 4, lambda m: shift_of(0, 5, m),
                             after={1: lambda: ssm_matrices_dve(dve), 5: lambda: ssm_begin_dve(dve)})
                norm_dve(dve, 6, lambda c: modg[:, 2 * KC + c:2 * KC + c + 1], shifted=True, by_parity=True)
            if on(5):
                ssm_dve(dve)
                norm_dve(dve, 7, lambda c: modg[:, 3 * KC + c:3 * KC + c + 1], shifted=True)
            if on(6):
                conv_dve(dve, 3)
                residual_dve(dve, 8, TILE0["ffn3"] + 2 * FC, lambda m: m % 4, lambda m: shift_of(1, 5, m),
                             squares=False)

        @block.gpsimd
        def _(pool):
            for j in range(VTILES):
                pool.memset(v_rows[:, j, :], 0.0).then_inc(v_cleared, 1)
            ada_pool(pool)
            if on(1):
                pool.wait_ge(s_late, 32)
                mix1_pool(pool)
            if on(3):
                mix2_pool(pool)
            if on(4):
                ssm_prepare_pool(pool)
            if on(5):
                ssm_pool(pool)


VLOADS = 8 + 1 + 4 + 1 + 3 + 1


INPUTS = ["x", "ffn1_norm", "ffn1_w1", "ffn1_w3", "ffn1_w2", "mix_norm", "w_in", "w_branch_attn", "w_branch_pool",
          "pool_w", "pool_scale", "w_out", "ffn2_norm", "ffn2_w1", "ffn2_w3", "ffn2_w2", "final_norm", "c_2",
          "positions_2", "ada_w_2", "ada_b_2", "norm_mix_2", "norm_ffn_2", "attn_w_in_2", "attn_q_gain_2",
          "attn_k_gain_2", "attn_w_out_2", "ssm_a_re_2", "ssm_a_im_2", "ssm_log_dt_2", "ssm_b_re_2", "ssm_b_im_2",
          "ssm_c_re_2", "ssm_c_im_2", "ssm_d_2", "ssm_w_glu_2", "ffn_w_up_2", "ffn_conv_w_2", "ffn_conv_b_2",
          "ffn_w_down_2"]


def kernel(**inputs):
    import concourse.bacc as _bacc
    from concourse.bass_utils import run_bass_kernel_spmd as _run

    nc = _bacc.Bacc("TRN2", target_bir_lowering=False, num_devices=1)
    of_shapes = {"shape_constants": SHAPE_CONSTANTS, "steps": STEPS}
    arrays, args = {}, {}
    for name in INPUTS + list(of_shapes):
        x = of_shapes[name] if name in of_shapes else np.ascontiguousarray(inputs[name])
        arrays[f"in_{name}"] = x
        args[name] = nc.dram_tensor(f"in_{name}", x.shape, mybir.dt.from_np(x.dtype), kind="ExternalInput").ap()
    out = nc.dram_tensor("out", (1, T, D), F32, kind="ExternalOutput").ap()
    build(nc, args, out)
    result = _run(nc, [arrays], core_ids=[0])
    return result.results[0]["out"]
```
